# Optimizing a Trainium2 kernel written in Bass

```python
import math
import jax, jax.numpy as jnp
from jax import lax
import numpy as np

D_MODEL = 1024
BATCH = 1
SEQ = 2048
DEPTH = 2
DEC_BATCH = 8
DEC_SEQ = 4
PAST_LEN = 2048
PAGE_SIZE = 128

N_AB = (DEPTH + 1) // 2
N_C = DEPTH // 2
EPS = 1e-6
NEG_INF = -1e30
CHUNK = 64

A_HEADS = 8
A_KV_HEADS = 2
A_HEAD_DIM = 64
A_ROPE_DIM = A_HEAD_DIM // 4
ROPE_THETA = 500000.0
IDX_HEADS = 4
IDX_DIM = 64
IDX_ROPE_DIM = IDX_DIM // 4
TOPK_MAX = 256
Q_BLOCK = 128
A_WIDTH = A_HEADS * A_HEAD_DIM
A_KV_WIDTH = A_KV_HEADS * A_HEAD_DIM
IDX_Q_WIDTH = IDX_HEADS * IDX_DIM

B_HEADS = 4
B_QK_DIM = 64
B_V_DIM = 128
B_QK_WIDTH = B_HEADS * B_QK_DIM
B_WIDTH = B_HEADS * B_V_DIM
RET_THETA = 10000.0

C_QK_HEADS = 4
C_V_HEADS = 8
C_QK_DIM = 128
C_V_DIM = 128
C_QK_WIDTH = C_QK_HEADS * C_QK_DIM
C_WIDTH = C_V_HEADS * C_V_DIM
CONV_W = 4
C_CONV_DIM = 2 * C_QK_WIDTH + C_WIDTH

AB_SIZES = (A_WIDTH, A_KV_WIDTH, A_KV_WIDTH, IDX_Q_WIDTH, IDX_DIM, IDX_HEADS, A_WIDTH,
            B_QK_WIDTH, B_QK_WIDTH, B_WIDTH, B_WIDTH)
AB_IN = sum(AB_SIZES)
AB_OUT = A_WIDTH + B_WIDTH
C_SIZES = (C_CONV_DIM, C_WIDTH, C_V_HEADS, C_V_HEADS)
C_IN = sum(C_SIZES)

kernel_name = 'hybrid_dsa_retention_gdn_step'

F32 = jnp.float32

def _split(x, sizes):
    cuts = [int(c) for c in np.cumsum(sizes)[:-1]]
    return jnp.split(x, cuts, axis=-1)

def rmsnorm(x, g):
    xf = x.astype(F32)
    y = xf * lax.rsqrt(jnp.mean(xf * xf, axis=-1, keepdims=True) + EPS)
    return (y * g.astype(F32)).astype(x.dtype)

def l2norm(x):
    xf = x.astype(F32)
    return xf * lax.rsqrt(jnp.sum(xf * xf, axis=-1, keepdims=True) + EPS)

def rope(x, pos, rot_dim, theta):
    half = rot_dim // 2
    inv = 1.0 / (theta ** (jnp.arange(half, dtype=F32) / half))
    ang = pos.astype(F32)[:, None] * inv
    cos = jnp.cos(ang)[:, None, :]
    sin = jnp.sin(ang)[:, None, :]
    xr = x[..., :rot_dim].astype(F32)
    x1, x2 = xr[..., :half], xr[..., half:]
    rot = jnp.concatenate([x1 * cos - x2 * sin, x2 * cos + x1 * sin], axis=-1)
    return jnp.concatenate([rot.astype(x.dtype), x[..., rot_dim:]], axis=-1)

def gather_rows(x, idx):
    return jax.vmap(lambda xb, ib: xb[ib])(x, idx)

def index_scores(iq, ik, iw):
    s = jnp.einsum('bthd,bsd->bths', iq.astype(F32), ik.astype(F32)) * IDX_DIM ** -0.5
    return jnp.einsum('bths,bth->bts', jax.nn.relu(s), iw.astype(F32))

def sparse_attend(q, kg, vg, ok):
    Bn, T = q.shape[:2]
    qg = q.reshape(Bn, T, A_KV_HEADS, A_HEADS // A_KV_HEADS, A_HEAD_DIM).astype(F32)
    s = jnp.einsum('btgrd,btkgd->btgrk', qg, kg.astype(F32)) * A_HEAD_DIM ** -0.5
    s = jnp.where(ok[:, :, None, None, :], s, NEG_INF)
    p = jax.nn.softmax(s, axis=-1)
    o = jnp.einsum('btgrk,btkgd->btgrd', p, vg.astype(F32))
    return o.reshape(Bn, T, A_HEADS, A_HEAD_DIM).astype(q.dtype)

def dsa_prompt(q, k, v, iq, ik, iw, topk):
    Bn, S_ = q.shape[:2]
    nb = S_ // Q_BLOCK

    def to_blocks(t):
        return jnp.moveaxis(t.reshape((Bn, nb, Q_BLOCK) + t.shape[2:]), 1, 0)

    key_pos = jnp.arange(S_)

    def one_block(args):
        qb, iqb, iwb, t0 = args
        tpos = t0 + jnp.arange(Q_BLOCK)
        vis = key_pos[None, None, :] <= tpos[None, :, None]
        sc = jnp.where(vis, index_scores(iqb, ik, iwb), -jnp.inf)
        _, sel = lax.top_k(sc, topk)
        ok = sel <= tpos[None, :, None]
        return sparse_attend(qb, gather_rows(k, sel), gather_rows(v, sel), ok)

    out = lax.map(one_block, (to_blocks(q), to_blocks(iq), to_blocks(iw), jnp.arange(nb) * Q_BLOCK))
    return jnp.moveaxis(out, 0, 1).reshape(q.shape)

def dsa_sample(q, k_new, v_new, iq, ik_new, iw, cache_k, cache_v, cache_kidx, page_table, topk):
    DBn, T = q.shape[:2]
    past = page_table.shape[1] * PAGE_SIZE
    ik_past = cache_kidx[page_table].reshape(DBn, past, IDX_DIM)
    ik_all = jnp.concatenate([ik_past.astype(ik_new.dtype), ik_new], axis=1)
    tpos = past + jnp.arange(T)
    key_pos = jnp.arange(past + T)
    vis = key_pos[None, None, :] <= tpos[None, :, None]
    sc = jnp.where(vis, index_scores(iq, ik_all, iw), -jnp.inf)
    _, sel = lax.top_k(sc, topk)
    ok = sel <= tpos[None, :, None]
    in_past = sel < past
    lp = jnp.minimum(sel, past - 1)
    phys_page = jnp.take_along_axis(page_table, (lp // PAGE_SIZE).reshape(DBn, -1), axis=1).reshape(sel.shape)
    rows = phys_page * PAGE_SIZE + lp % PAGE_SIZE
    kp = cache_k.reshape((-1,) + cache_k.shape[2:])[rows]
    vp = cache_v.reshape((-1,) + cache_v.shape[2:])[rows]
    ln = jnp.clip(sel - past, 0, T - 1)
    kg = jnp.where(in_past[..., None, None], kp.astype(k_new.dtype), gather_rows(k_new, ln))
    vg = jnp.where(in_past[..., None, None], vp.astype(v_new.dtype), gather_rows(v_new, ln))
    return sparse_attend(q, kg, vg, ok)

def _to_chunks(t, nc, C):
    t = t.reshape((t.shape[0], nc, C) + t.shape[2:])
    return jnp.moveaxis(t, 2, 3)

def _from_chunks(o):
    Bn, nc, H, C, D = o.shape
    return jnp.moveaxis(o, 3, 2).reshape(Bn, nc * C, H, D)

def retention_chunked(q, k, v, state):
    Bn, S_, H = q.shape[:3]
    C = math.gcd(S_, CHUNK)
    nc = S_ // C
    log_g = jnp.log(1.0 - 2.0 ** (-5.0 - jnp.arange(H, dtype=F32)))
    q, k, v = (_to_chunks(t.astype(F32), nc, C) for t in (q, k, v))
    idx = jnp.arange(C, dtype=F32)
    diff = idx[:, None] - idx[None, :]
    dmask = jnp.where(diff >= 0, jnp.exp(diff[None] * log_g[:, None, None]), 0.0)
    q_dec = jnp.exp((idx + 1.0)[None, :] * log_g[:, None])
    k_dec = jnp.exp((C - 1.0 - idx)[None, :] * log_g[:, None])
    chunk_dec = jnp.exp(C * log_g)
    att = jnp.einsum('bnhid,bnhjd->bnhij', q, k) * dmask
    intra = jnp.einsum('bnhij,bnhje->bnhie', att, v)
    kv = jnp.einsum('bnhjd,hj,bnhje->bnhde', k, k_dec, v)

    def step(r, kv_n):
        return chunk_dec[None, :, None, None] * r + kv_n, r

    r_fin, r_prev = lax.scan(step, state.astype(F32), jnp.moveaxis(kv, 1, 0))
    r_prev = jnp.moveaxis(r_prev, 0, 1)
    cross = jnp.einsum('bnhid,hi,bnhde->bnhie', q, q_dec, r_prev)
    return _from_chunks(intra + cross), r_fin

def gated_delta_chunked(q, k, v, g, beta, state):
    Bn, S_, H, Dk = q.shape
    Dv = v.shape[-1]
    C = math.gcd(S_, CHUNK)
    nc = S_ // C
    q, k, v = (_to_chunks(t.astype(F32), nc, C) for t in (q, k, v))
    g = _to_chunks(g.astype(F32), nc, C)
    beta = _to_chunks(beta.astype(F32), nc, C)
    gc = jnp.cumsum(g, axis=-1)
    idx = jnp.arange(C)
    tri = idx[:, None] >= idx[None, :]
    strict = idx[:, None] > idx[None, :]
    decay = jnp.exp(jnp.where(tri, gc[..., :, None] - gc[..., None, :], -jnp.inf))
    kb = k * beta[..., None]
    m = jnp.where(strict, jnp.einsum('bnhid,bnhjd->bnhij', kb, k) * decay, 0.0)
    rhs = jnp.concatenate([v * beta[..., None], kb * jnp.exp(gc)[..., None]], axis=-1)
    sol = lax.linalg.triangular_solve(m + jnp.eye(C, dtype=F32), rhs, left_side=True,
                                      lower=True, unit_diagonal=True)
    u, w = sol[..., :Dv], sol[..., Dv:]
    qk = jnp.where(tri, jnp.einsum('bnhid,bnhjd->bnhij', q, k) * decay, 0.0)
    qd = q * jnp.exp(gc)[..., None]
    kt = k * jnp.exp(gc[..., -1:] - gc)[..., None]
    gl = jnp.exp(gc[..., -1])

    def step(s, xs):
        u_n, w_n, qk_n, qd_n, kt_n, gl_n = xs
        v_new = u_n - jnp.einsum('bhcd,bhde->bhce', w_n, s)
        o = jnp.einsum('bhcd,bhde->bhce', qd_n, s) + jnp.einsum('bhij,bhje->bhie', qk_n, v_new)
        s = s * gl_n[..., None, None] + jnp.einsum('bhcd,bhce->bhde', kt_n, v_new)
        return s, o

    xs = tuple(jnp.moveaxis(t, 1, 0) for t in (u, w, qk, qd, kt, gl))
    s_fin, o = lax.scan(step, state.astype(F32), xs)
    return _from_chunks(jnp.moveaxis(o, 0, 1)), s_fin

def causal_conv(x, prefix, w):
    T = x.shape[1]
    xp = jnp.concatenate([prefix.astype(x.dtype), x], axis=1)
    y = sum(xp[:, j:j + T] * w[j] for j in range(CONV_W))
    return jax.nn.silu(y), xp[:, T:]

def ab_project(h, pos, w_in):
    Bn, T, _ = h.shape
    qa, ka, va, iq, ik, iw, za, qb, kb, vb, zb = _split(h @ w_in, AB_SIZES)
    qa = rope(qa.reshape(Bn, T, A_HEADS, A_HEAD_DIM), pos, A_ROPE_DIM, ROPE_THETA)
    ka = rope(ka.reshape(Bn, T, A_KV_HEADS, A_HEAD_DIM), pos, A_ROPE_DIM, ROPE_THETA)
    va = va.reshape(Bn, T, A_KV_HEADS, A_HEAD_DIM)
    iq = rope(iq.reshape(Bn, T, IDX_HEADS, IDX_DIM), pos, IDX_ROPE_DIM, ROPE_THETA)
    ik = rope(ik.reshape(Bn, T, 1, IDX_DIM), pos, IDX_ROPE_DIM, ROPE_THETA)[:, :, 0]
    iw = iw * IDX_HEADS ** -0.5
    qb = rope(qb.reshape(Bn, T, B_HEADS, B_QK_DIM), pos, B_QK_DIM, RET_THETA)
    kb = rope(kb.reshape(Bn, T, B_HEADS, B_QK_DIM), pos, B_QK_DIM, RET_THETA) * B_QK_DIM ** -0.5
    vb = vb.reshape(Bn, T, B_HEADS, B_V_DIM)
    return qa, ka, va, iq, ik, iw, za, qb, kb, vb, zb

def ab_output(oa, za, ob, zb, gn_gain, w_out):
    Bn, T = oa.shape[:2]
    obf = ob.astype(F32)
    mu = jnp.mean(obf, axis=-1, keepdims=True)
    var = jnp.mean(jnp.square(obf - mu), axis=-1, keepdims=True)
    obn = (obf - mu) * lax.rsqrt(var + EPS) * gn_gain.astype(F32).reshape(B_HEADS, B_V_DIM)
    ya = oa.reshape(Bn, T, A_WIDTH) * jax.nn.silu(za)
    yb = (obn.reshape(Bn, T, B_WIDTH) * jax.nn.silu(zb.astype(F32))).astype(za.dtype)
    return jnp.concatenate([ya, yb], axis=-1) @ w_out

def c_mixer(h, w_in, conv_w, a_log, dt_bias, gdn_norm, w_out, conv_prefix, state):
    Bn, T, _ = h.shape
    qkv, z, a, b = _split(h @ w_in, C_SIZES)
    qkv, conv_new = causal_conv(qkv, conv_prefix, conv_w)
    q, k, v = _split(qkv, (C_QK_WIDTH, C_QK_WIDTH, C_WIDTH))
    rep = C_V_HEADS // C_QK_HEADS
    q = jnp.repeat(l2norm(q.reshape(Bn, T, C_QK_HEADS, C_QK_DIM)) * C_QK_DIM ** -0.5, rep, axis=2)
    k = jnp.repeat(l2norm(k.reshape(Bn, T, C_QK_HEADS, C_QK_DIM)), rep, axis=2)
    v = v.reshape(Bn, T, C_V_HEADS, C_V_DIM)
    g = -jnp.exp(a_log.astype(F32)) * jax.nn.softplus(a.astype(F32) + dt_bias.astype(F32))
    beta = jax.nn.sigmoid(b.astype(F32))
    o, s_new = gated_delta_chunked(q, k, v, g, beta, state)
    o = rmsnorm(o, gdn_norm) * jax.nn.silu(z.reshape(Bn, T, C_V_HEADS, C_V_DIM).astype(F32))
    y = o.reshape(Bn, T, C_WIDTH).astype(h.dtype) @ w_out
    return y, s_new, conv_new

def setup_inputs(seed: int = 0) -> dict:
    key = jax.random.key(seed)
    ks = iter(jax.random.split(key, 24))

    def nrm(shape, scale):
        return scale * jax.random.normal(next(ks), shape, F32)

    n_pages = PAST_LEN // PAGE_SIZE
    n_pool = (DEC_BATCH * n_pages * 5) // 4
    page_table = jax.random.permutation(next(ks), n_pool)[:DEC_BATCH * n_pages]
    page_table = page_table.reshape(DEC_BATCH, n_pages).astype(jnp.int32)
    a_log = jnp.log(jax.random.uniform(next(ks), (N_C, C_V_HEADS), F32, 1.0, 16.0))
    dt = jnp.exp(jax.random.uniform(next(ks), (N_C, C_V_HEADS), F32, math.log(1e-3), math.log(1e-1)))
    dt_bias = dt + jnp.log(-jnp.expm1(-dt))
    return {
        'x_prompt': nrm((BATCH, SEQ, D_MODEL), 1.0),
        'x_sample': nrm((DEC_BATCH, DEC_SEQ, D_MODEL), 1.0),
        'cache_k': nrm((N_AB, n_pool, PAGE_SIZE, A_KV_HEADS, A_HEAD_DIM), 1.0),
        'cache_v': nrm((N_AB, n_pool, PAGE_SIZE, A_KV_HEADS, A_HEAD_DIM), 1.0),
        'cache_kidx': nrm((N_AB, n_pool, PAGE_SIZE, IDX_DIM), 1.0),
        'state_ret': nrm((N_AB, DEC_BATCH, B_HEADS, B_QK_DIM, B_V_DIM), 0.3),
        'state_gdn': nrm((N_C, DEC_BATCH, C_V_HEADS, C_QK_DIM, C_V_DIM), 0.1),
        'state_conv': nrm((N_C, DEC_BATCH, CONV_W - 1, C_CONV_DIM), 1.0),
        'page_table': page_table,
        'norm_w': 1.0 + nrm((DEPTH, D_MODEL), 0.02),
        'w_in_ab': nrm((N_AB, D_MODEL, AB_IN), D_MODEL ** -0.5),
        'w_out_ab': nrm((N_AB, AB_OUT, D_MODEL), AB_OUT ** -0.5),
        'gn_ret': 1.0 + nrm((N_AB, B_WIDTH), 0.02),
        'w_in_c': nrm((N_C, D_MODEL, C_IN), D_MODEL ** -0.5),
        'conv_w': nrm((N_C, CONV_W, C_CONV_DIM), CONV_W ** -0.5),
        'a_log': a_log,
        'dt_bias': dt_bias,
        'gdn_norm': 1.0 + nrm((N_C, C_V_DIM), 0.02),
        'w_out_c': nrm((N_C, C_WIDTH, D_MODEL), C_WIDTH ** -0.5),
        'final_norm': 1.0 + nrm((D_MODEL,), 0.02),
    }

def reference(x_prompt, x_sample, cache_k, cache_v, cache_kidx, state_ret, state_gdn, state_conv,
              page_table, norm_w, w_in_ab, w_out_ab, gn_ret, w_in_c, conv_w, a_log, dt_bias,
              gdn_norm, w_out_c, final_norm):
    Bp, Tp = x_prompt.shape[:2]
    Ts = x_sample.shape[1]
    past = page_table.shape[1] * PAGE_SIZE
    pos_p = jnp.arange(Tp)
    pos_s = past + jnp.arange(Ts)
    topk_p = min(TOPK_MAX, Tp // 4)
    topk_s = min(TOPK_MAX, (past + Ts) // 4)
    yp, ys = x_prompt, x_sample
    kp_l, vp_l, ip_l, ks_l, vs_l, is_l = [], [], [], [], [], []
    rp_l, rs_l, gp_l, gs_l, cp_l, cs_l = [], [], [], [], [], []
    for layer in range(DEPTH):
        j = layer // 2
        if layer % 2 == 0:
            qa, ka, va, iq, ik, iw, za, qb, kb, vb, zb = ab_project(rmsnorm(yp, norm_w[layer]), pos_p, w_in_ab[j])
            oa = dsa_prompt(qa, ka, va, iq, ik, iw, topk_p)
            ob, r_new = retention_chunked(qb, kb, vb, jnp.zeros((Bp, B_HEADS, B_QK_DIM, B_V_DIM), F32))
            yp = yp + ab_output(oa, za, ob, zb, gn_ret[j], w_out_ab[j])
            kp_l.append(ka); vp_l.append(va); ip_l.append(ik); rp_l.append(r_new)
            qa, ka, va, iq, ik, iw, za, qb, kb, vb, zb = ab_project(rmsnorm(ys, norm_w[layer]), pos_s, w_in_ab[j])
            oa = dsa_sample(qa, ka, va, iq, ik, iw, cache_k[j], cache_v[j], cache_kidx[j], page_table, topk_s)
            ob, r_new = retention_chunked(qb, kb, vb, state_ret[j])
            ys = ys + ab_output(oa, za, ob, zb, gn_ret[j], w_out_ab[j])
            ks_l.append(ka); vs_l.append(va); is_l.append(ik); rs_l.append(r_new)
        else:
            zero_conv = jnp.zeros((Bp, CONV_W - 1, C_CONV_DIM), yp.dtype)
            zero_s = jnp.zeros((Bp, C_V_HEADS, C_QK_DIM, C_V_DIM), F32)
            dy, s_new, c_new = c_mixer(rmsnorm(yp, norm_w[layer]), w_in_c[j], conv_w[j], a_log[j], dt_bias[j],
                                       gdn_norm[j], w_out_c[j], zero_conv, zero_s)
            yp = yp + dy
            gp_l.append(s_new); cp_l.append(c_new)
            dy, s_new, c_new = c_mixer(rmsnorm(ys, norm_w[layer]), w_in_c[j], conv_w[j], a_log[j], dt_bias[j],
                                       gdn_norm[j], w_out_c[j], state_conv[j], state_gdn[j])
            ys = ys + dy
            gs_l.append(s_new); cs_l.append(c_new)
    y_prompt = rmsnorm(yp, final_norm)
    y_sample = rmsnorm(ys, final_norm)
    return (y_prompt, y_sample,
            jnp.stack(kp_l), jnp.stack(vp_l), jnp.stack(ip_l),
            jnp.stack(ks_l), jnp.stack(vs_l), jnp.stack(is_l),
            jnp.stack(rp_l), jnp.stack(rs_l),
            jnp.stack(gp_l), jnp.stack(gs_l),
            jnp.stack(cp_l), jnp.stack(cs_l))


_drawn_inputs = setup_inputs


def setup_inputs(seed=0):
    import zlib

    import numpy as np

    out = dict(_drawn_inputs(seed))
    spreads = {}
    factors = {'gn_ret': 5.357,
     'gdn_norm': 21.254,
     'final_norm': 8.0,
     'cache_k': 3.282,
     'cache_kidx': 2.733}
    for name, (base, spread) in spreads.items():
        noise = np.random.default_rng([zlib.crc32(name.encode()), seed]).standard_normal(out[name].shape)
        drawn = base * np.exp(spread * noise) if base else spread * noise
        out[name] = __import__('jax').numpy.asarray(drawn.astype(out[name].dtype))
    for name, factor in factors.items():
        out[name] = (out[name] * factor).astype(out[name].dtype)
    return out
```

```python
import concourse.bass as bass
from concourse import mybir
from contextlib import ExitStack
import numpy as np

FP = mybir.dt.float32
BF = mybir.dt.bfloat16
I32 = mybir.dt.int32
ALU = mybir.AluOpType
ACT = mybir.ActivationFunctionType
AX = mybir.AxisListType.X
ds = bass.ds

P = 128
D = 1024
KD = D // P
SEQ, DB, DT = 2048, 8, 4
NT = SEQ // P
ROWS = (NT + 1) * P
SR = DB * DT
PAST, PAGE = 2048, 128
NPG = PAST // PAGE
TOPK = 256
EPS = 1e-6
BIG = 1e30
AH, HD = 8, 64
RH, RV = 4, 128
ABW = 3140
C_QA, C_KA, C_VA, C_IQ, C_IK, C_IW, C_ZA = 0, 512, 640, 768, 1024, 1088, 1092
C_QB, C_KB, C_VB, C_ZB = 1604, 1860, 2116, 2628
AB_CUTS = [(0, 512), (512, 1024), (1024, 1092), (1092, 1604), (1604, 2116), (2116, 2628), (2628, 3140)]
A_UNITS = 2 + len(AB_CUTS)
NHEADS17 = 17
GROUPS = 4
GT = NT // GROUPS
CH = 512
STEPS = 24
CC, CIN = 2048, 3088


def units_before(g):
    return sum(GT * (k + 1) for k in range(g))


def constants():
    f = np.float32
    out = {}
    out["ident"] = np.eye(P, dtype=f)
    pos = np.concatenate([np.arange(SEQ), np.tile(PAST + np.arange(DT), DB), np.zeros(ROWS - SEQ - SR)]).astype(f)
    half = HD // 4 // 2
    inv = (1.0 / (f(500000.0) ** (np.arange(half, dtype=f) / half))).astype(f)
    ang = (pos[:, None] * inv).astype(f)
    c, s = np.cos(ang).astype(f), np.sin(ang).astype(f)
    cc = np.tile(np.concatenate([c, c], 1)[:, None], (1, NHEADS17, 1))
    ss = np.tile(np.concatenate([-s, s], 1)[:, None], (1, NHEADS17, 1))
    cc[:, 10:12] = 1.0
    ss[:, 10:12] = 0.0
    out["ropea"] = np.stack([cc, ss], 1).reshape(ROWS, -1).astype(f)
    half = 32
    inv = (1.0 / (f(10000.0) ** (np.arange(half, dtype=f) / half))).astype(f)
    ang = (pos[:, None] * inv).astype(f)
    c, s = np.cos(ang).astype(f), np.sin(ang).astype(f)
    out["ropeb"] = np.concatenate([c, c, -s, s], 1).astype(f)
    p = np.arange(P)
    caus = np.where(np.arange(CH)[None, None] <= np.arange(GT)[None, :, None] * P + p[:, None, None], 0.0, -BIG)
    out["caus"] = caus.reshape(P, GT * CH).astype(f)
    lg = np.log(1.0 - 2.0 ** (-5.0 - np.arange(RH)))
    dif = p[None, :] - p[:, None]
    rm = np.where(dif[:, None, :] >= 0, np.exp(dif[:, None, :] * lg[None, :, None]), 0.0) * HD ** -0.5
    rm = rm[:, [0, 2, 1, 3]]
    out["rmask"] = rm.reshape(P, RH * P).astype(f)
    head = 2 * np.arange(2)[None] + (p[:, None] >= 64)
    out["qdec"] = np.exp((p[None, None] + 1.0) * lg[head][:, :, None]).reshape(P, 2 * P).astype(f)
    out["kdec"] = (np.exp((P - 1.0 - p)[:, None] * lg[None]) * HD ** -0.5).astype(f)
    out["cdec"] = np.tile(np.exp(P * lg), (P, 1)).astype(f)
    out["pow2"] = np.tile(2.0 ** -(1.0 + np.arange(STEPS + 1)), (P, 1)).astype(f)
    return out


START = 1


def after(n):
    return n + START


def link_in(eng, sem):
    n = [0]

    def link(ins=None):
        n[0] += 1
        if ins is None:
            eng.sem_inc(sem, 1)
        else:
            ins.then_inc(sem, 1)
        eng.wait_ge(sem, n[0])

    def fresh():
        eng.sem_clear(sem)
        n[0] = 0

    fresh()
    return link, fresh


def turn_half(pe, out, src, ident, half):
    if half:
        return pe.matmul(out, src, ident, start=True, stop=True)
    return pe.transpose(out, src, ident)


def layer0_mixers(nc, io, S):
    ctx = ExitStack()
    with ctx:
        def sb(name, shape, dt=FP):
            return ctx.enter_context(nc.sbuf_tensor(name, shape, dt))

        w_in = sb("w_in", [P, KD, ABW])
        xa = sb("xa", [P, D])
        hT = sb("hT", [P, KD, P])
        pr = sb("pr", [P, ABW])
        kT = sb("kT", [P, SEQ])
        ikT = sb("ikT", [P, SEQ])
        vst = sb("vst", [P, NT, P])
        isc = sb("isc", [P, SEQ])
        sm = sb("sm", [P, 2, SEQ])
        mb = sb("mb", [P, SEQ], BF)
        ident = sb("ident", [P, P])
        caus = sb("caus_t", [P, CH])
        rmask = sb("rmask_t", [P, 2, 2 * P])
        qdec = sb("qdec_t", [P, 2, P])
        kdec = sb("kdec_t", [P, RH])
        cdec = sb("cdec_t", [P, RH])
        pow2 = sb("pow2_t", [P, STEPS + 1])
        ropea = sb("ropea_t", [P, 2, NHEADS17, 16])
        ropeb = sb("ropeb_t", [P, 2, HD])
        ptT = sb("ptT", [P, 2, CH])
        qT = sb("qT", [P, AH, P])
        iqT = sb("iqT", [P, 4, P])
        qkbT = sb("qkbT", [P, 4, P])
        qbd = sb("qbd", [P, 2, P])
        attm = ptT[:, :, 0:2 * P]
        tg = sb("tg", [P, D])
        yab = tg
        relu = sb("relu", [P, 2, CH])
        rst = sb("rst", [P, RH, RV])
        kd = sb("kd", [P, RH, P])
        nw0 = sb("nw0", [P, KD])
        gng = sb("gng", [P, RH * RV])
        small = sb("small", [P, 64])
        nhalf = sb("nhalf", [P, RH])
        ssum, rstd = small[:, 0:1], small[:, 1:2]
        lo_b, hi_b, rng_, mid, cnt, ph, hi_c, lo_c, cgt, need = [small[:, 2 + i:3 + i] for i in range(10)]
        mxc, negm, rsum = small[:, 12:16], small[:, 16:24], small[:, 24:32]
        gsum, gsq, grs = small[:, 32:36], small[:, 36:40], small[:, 40:44]
        iwc = small[:, 44:48]
        rinv = small[:, 48:56]
        vtmp = small[:, 56:57]
        halves = sb("halves", [P, STEPS + 1])
        rt_a = sm[:, 0, 0:512]
        rt_b = sm[:, 1, 0:512]
        gn_c = relu[:, 0, :]
        gn_q = relu[:, 1, :]

        def ps(name):
            return ctx.enter_context(nc.psum_tensor(name, [P, 512], FP))

        PA = [ps("PA0"), ps("PA1")]
        PS = [ps("PS0"), ps("PS1")]
        PT = [ps("PT0"), ps("PT1")]
        PO, PR = ps("PO"), ps("PR")

        block = ctx.enter_context(nc.Block())

        @block.scalar
        def _(act):
            link, fresh = link_in(act, S["act_link"])

            def stage_a(ai, t_done):
                fresh()
                act.wait_ge(S["x_loaded"], after(16 * (ai + 1)))
                act.wait_ge(S["a_evac"], after(A_UNITS * ai))
                act.activation(hT[:, :, :].rearrange("p c t -> p (c t)"), xa[:, :], ACT.Square,
                               accum_out=ssum).then_inc(S["ss_ready"], 1)
                act.wait_ge(S["rstd_ready"], after(ai + 1))
                act.wait_ge(S["ss_ready"], after(ai + 1))
                act.activation(xa[:, :], xa[:, :], ACT.Copy, scale=rstd).then_inc(S["hn_ready"], 1)
                for u in range(2):
                    act.wait_ge(S["a_psum"], after(A_UNITS * ai + u + 1))
                    for k in range(4):
                        c = 4 * u + k
                        ins = act.activation(hT[:, c, :], PA[u][:, k * P:(k + 1) * P], ACT.Copy,
                                             scale=nw0[:, c:c + 1])
                    ins.then_inc(S["a_evac"], 1)
                if t_done is not None:
                    act.wait_ge(S["kv_stored"], after(48 * t_done))
                    act.wait_ge(S["v_stored"], after(t_done))
                    act.wait_ge(S["ro_ps"], after(t_done))
                    act.wait_ge(S["rs_ps"], after(t_done))
                    act.wait_ge(S["gates_done"], after(t_done))
                    act.wait_ge(S["iw_ready"], after(t_done))
                for n, (a, b) in enumerate(AB_CUTS):
                    act.wait_ge(S["a_psum"], after(A_UNITS * ai + n + 3))
                    act.copy(pr[:, a:b], PA[n % 2][:, 0:b - a]).then_inc(S["a_evac"], 1)

            def tile_in(g, j):
                t, U, NK = j + GT * g, j * (g + 1) + units_before(g), g + 1
                fresh()
                act.wait_ge(S["tr_ps"], after(3 * t + 1))
                for a in range(2):
                    ins = act.copy(qT[a * HD:(a + 1) * HD, 4 * a:4 * a + 4, :].rearrange("p r t -> p (r t)"),
                                   PT[0][a * HD:(a + 1) * HD, :])
                ins.then_inc(S["tr_sb"], 1)
                act.wait_ge(S["tr_ps"], after(3 * t + 2))
                act.copy(kT[:, ds(t * P, P)], PT[1][:, 0:P])
                for a in range(2):
                    act.copy(iqT[:, :, :].rearrange("p (c a) t -> p c a t", a=2)[a * HD:(a + 1) * HD, :, a],
                             PT[1][a * HD:(a + 1) * HD, P:3 * P].rearrange("p (c t) -> p c t", c=2))
                act.copy(ikT[:, ds(t * P, P)], PT[1][:, 3 * P:4 * P]).then_inc(S["tr_sb"], 1)
                act.wait_ge(S["tr_ps"], after(3 * t + 3))
                act.copy(qkbT[:, :, :].rearrange("p r t -> p (r t)"), PT[0][:, :]).then_inc(S["tr_sb"], 1)
                act.wait_ge(S["a_evac"], after(A_UNITS * (t + 1)))
                act.wait_ge(S["yab_stored"], after(16 * t))
                act.activation(tg[:, 0:512], pr[:, C_ZA:C_ZA + 512], ACT.Tanh, scale=0.5)
                act.activation(tg[:, 512:1024], pr[:, C_ZB:C_ZB + 512], ACT.Tanh, scale=0.5).then_inc(S["g_tanh"], 1)
                for u in range(4 * NK):
                    act.wait_ge(S["idx_ps"], after(4 * U + u + 1))
                    if u >= 2:
                        act.wait_ge(S["idx_acc"], after(4 * U + u - 1))
                    else:
                        act.wait_ge(S["gn_done"], after(t))
                        act.wait_ge(S["idx_acc"], after(4 * U))
                    act.activation(relu[:, u % 2, :], PS[u % 2][:, :], ACT.Relu, scale=1.0 / 16)\
                       .then_inc(S["idx_rd"], 1)

            def tile_attend(g, j):
                t, U, NK = j + GT * g, j * (g + 1) + units_before(g), g + 1
                fresh()
                W = NK * CH
                for h in range(AH + 1):
                    if h < AH:
                        act.wait_ge(S["nm_ready"], after(8 * t + h + 1))
                        act.activation(sm[:, h % 2, 0:W], sm[:, h % 2, 0:W], ACT.Exp, bias=negm[:, h:h + 1],
                                       scale=HD ** -0.5, accum_out=rsum[:, h:h + 1]).then_inc(S["exp_done"], 1)
                    if h:
                        for c in range(NK):
                            v = (h - 1) * NK + c
                            act.wait_ge(S["pt_ps"], after(8 * U + v + 1))
                            act.wait_ge(S["pv_done"], after(8 * U + max(v - 1, 0)))
                            act.copy(ptT[:, v % 2, :], PT[v % 2][:, :]).then_inc(S["pt_sb"], 1)

            act.wait_ge(S["const_ready"], after(2))
            act.wait_ge(S["c_loaded"], after(16 * 8))
            act.wait_ge(S["zeroed"], after(7))
            stage_a(0, None)
            for g in range(GROUPS):
                with act.Fori(0, GT) as j:
                    tile_in(g, j)
                    stage_a(j + GT * g + 1, j + GT * g + 1)
                    tile_attend(g, j)

        @block.tensor
        def _(pe):
            def stage_a(ai):
                pe.wait_ge(S["hn_ready"], after(ai + 1))
                pe.wait_ge(S["a_evac"], after(A_UNITS * ai))
                for u in range(2):
                    for k in range(4):
                        c = 4 * u + k
                        ins = pe.transpose(PA[u][:, k * P:(k + 1) * P], xa[:, c * P:(c + 1) * P], ident[:, :])
                    ins.then_inc(S["a_psum"], 1)
                for n, (a, b) in enumerate(AB_CUTS):
                    pe.wait_ge(S["a_evac"], after(A_UNITS * ai + max(2, n + 1)))
                    for c in range(KD):
                        ins = pe.matmul(PA[n % 2][:, 0:b - a], hT[:, c, :], w_in[:, c, a:b],
                                        start=(c == 0), stop=(c == KD - 1))
                    ins.then_inc(S["a_psum"], 1)

            def tile_in(g, j):
                t, U, NK = j + GT * g, j * (g + 1) + units_before(g), g + 1
                pe.wait_ge(S["rope_done"], after(t + 1))
                pe.wait_ge(S["pt_sb"], after(8 * U))
                pe.transpose(PT[1][:, 0:P], pr[:, C_KA:C_KA + P], ident[:, :])
                for h in range(AH):
                    lo, r = HD * (h // 4), h % 4
                    ins = turn_half(pe, PT[0][lo:lo + HD, r * P:(r + 1) * P], pr[:, h * HD:(h + 1) * HD],
                                    ident[:, :], h // 4)
                ins.then_inc(S["tr_ps"], 1)
                pe.transpose(PT[1][:, P:2 * P], pr[:, C_IQ:C_IQ + P], ident[:, :])
                pe.transpose(PT[1][:, 2 * P:3 * P], pr[:, C_IQ + P:C_IQ + 2 * P], ident[:, :])
                for a in range(2):
                    ins = turn_half(pe, PT[1][a * HD:(a + 1) * HD, 3 * P:4 * P], pr[:, C_IK:C_IK + HD],
                                    ident[:, :], a)
                ins.then_inc(S["tr_ps"], 1)
                pe.wait_ge(S["tr_sb"], after(3 * t + 1))
                for r in range(4):
                    ins = pe.transpose(PT[0][:, r * P:(r + 1) * P], pr[:, C_QB + r * P:C_QB + (r + 1) * P],
                                       ident[:, :])
                ins.then_inc(S["tr_ps"], 1)
                pe.wait_ge(S["tr_sb"], after(3 * t + 2))
                pe.wait_ge(S["sm_done"], after(8 * U))
                for u in range(4 * NK):
                    c, h = divmod(u, 4)
                    if u >= 2:
                        pe.wait_ge(S["idx_rd"], after(4 * U + u - 1))
                    pe.matmul(PS[u % 2][:, :], iqT[:, h, :], ikT[:, c * CH:(c + 1) * CH],
                              start=True, stop=True).then_inc(S["idx_ps"], 1)
                pe.wait_ge(S["tr_sb"], after(3 * t + 3))
                pe.wait_ge(S["idx_rd"], after(4 * U + 4 * NK))
                for h in range(RH):
                    lo = HD * (h % 2)
                    ins = pe.matmul(PS[h % 2][:, (h // 2) * P:(h // 2 + 1) * P], qkbT[lo:lo + HD, 2 + h // 2, :],
                                    qkbT[lo:lo + HD, h // 2, :], start=True, stop=True)
                ins.then_inc(S["ra_ps"], 1)
                pe.wait_ge(S["kd_ready"], after(t + 1))
                for h in range(RH):
                    ins = pe.matmul(PT[1][:, h * RV:(h + 1) * RV], kd[:, h, :],
                                    pr[:, C_VB + h * RV:C_VB + (h + 1) * RV], start=True, stop=True)
                ins.then_inc(S["rs_ps"], 1)
                pe.wait_ge(S["ra_sb"], after(t + 1))
                pe.wait_ge(S["qd_ready"], after(t + 1))
                pe.wait_ge(S["r_upd"], after(t))
                pe.wait_ge(S["gn_done"], after(t))
                for h in range(RH):
                    o = PR[:, h * RV:(h + 1) * RV]
                    pe.matmul(o, attm[:, h % 2, (h // 2) * P:(h // 2 + 1) * P], pr[:, C_VB + h * RV:C_VB + (h + 1) * RV], start=True, stop=False)
                    ins = pe.matmul(o, qbd[:, h // 2, :], rst[:, h, :], start=False,
                                    stop=True)
                ins.then_inc(S["ro_ps"], 1)

            def tile_attend(g, j):
                t, U, NK = j + GT * g, j * (g + 1) + units_before(g), g + 1
                pe.wait_ge(S["r_upd"], after(t + 1))
                pe.wait_ge(S["ra_sb"], after(t + 1))
                pe.wait_ge(S["mask_ready"], after(t + 1))
                for h in range(AH + 1):
                    if h < AH:
                        for c in range(NK):
                            u = h * NK + c
                            if u >= 2:
                                pe.wait_ge(S["sm_done"], after(8 * U + u - 1))
                            pe.matmul(PS[u % 2][:, :], qT[:, h, :], kT[:, c * CH:(c + 1) * CH],
                                      start=True, stop=True).then_inc(S["s_ps"], 1)
                    if not h:
                        continue
                    pe.wait_ge(S["exp_done"], after(8 * t + h))
                    for c in range(NK + 1):
                        v = (h - 1) * NK + c
                        if c < NK:
                            if v >= 2:
                                pe.wait_ge(S["pt_sb"], after(8 * U + v - 1))
                            for k in range(4):
                                ins = pe.transpose(PT[v % 2][:, k * P:(k + 1) * P],
                                                   sm[:, (h - 1) % 2, c * CH + k * P:c * CH + (k + 1) * P],
                                                   ident[:, :])
                            ins.then_inc(S["pt_ps"], 1)
                        if c:
                            if v == 1:
                                pe.wait_ge(S["yab_ready"], after(t))
                            pe.wait_ge(S["pt_sb"], after(8 * U + v))
                            gv = (h - 1) // 4
                            for k in range(4):
                                ins = pe.matmul(PO[:, (h - 1) * HD:h * HD], ptT[:, (v - 1) % 2, k * P:(k + 1) * P],
                                                vst[:, 4 * (c - 1) + k, gv * HD:(gv + 1) * HD],
                                                start=(c == 1 and k == 0), stop=(c == NK and k == 3))
                            ins.then_inc(S["pv_done"], 1)

            pe.wait_ge(S["w_loaded"], after(16 * KD))
            pe.wait_ge(S["c_loaded"], after(16 * 8))
            pe.wait_ge(S["zeroed"], after(7))
            stage_a(0)
            for g in range(GROUPS):
                with pe.Fori(0, GT) as j:
                    tile_in(g, j)
                    stage_a(j + GT * g + 1)
                    tile_attend(g, j)

        @block.vector
        def _(dve):
            link, fresh = link_in(dve, S["dve_link"])

            def tile_in(g, j):
                t, U, NK = j + GT * g, j * (g + 1) + units_before(g), g + 1
                W = NK * CH
                fresh()
                dve.wait_ge(S["a_evac"], after(A_UNITS * (t + 1)))
                dve.wait_ge(S["tab_loaded"], after(32 * (t + 1)))
                dve.wait_ge(S["pt_ps"], after(8 * U))
                x17 = pr[:, 0:17 * HD].rearrange("p (h d) -> p h d", d=HD)
                ta = rt_a[:, 0:272].rearrange("p (h d) -> p h d", d=16)
                tb = rt_b[:, 0:272].rearrange("p (h d) -> p h d", d=16)
                dve.tensor_tensor(ta, x17[:, :, 0:16], ropea[:, 0], ALU.mult)
                dve.tensor_tensor(tb[:, :, 0:8], x17[:, :, 8:16], ropea[:, 1, :, 0:8], ALU.mult)
                link(dve.tensor_tensor(tb[:, :, 8:16], x17[:, :, 0:8], ropea[:, 1, :, 8:16], ALU.mult))
                link(dve.tensor_tensor(x17[:, :, 0:16], ta, tb, ALU.add))
                x8 = pr[:, C_QB:C_QB + 512].rearrange("p (h d) -> p h d", d=HD)
                ta = rt_a.rearrange("p (h d) -> p h d", d=HD)
                tb = rt_b.rearrange("p (h d) -> p h d", d=HD)

                def row(k, a, b):
                    return ropeb[:, k:k + 1, a:b].to_broadcast([P, 8, b - a])

                dve.tensor_tensor(ta, x8, row(0, 0, HD), ALU.mult)
                dve.tensor_tensor(tb[:, :, 0:32], x8[:, :, 32:64], row(1, 0, 32), ALU.mult)
                link(dve.tensor_tensor(tb[:, :, 32:64], x8[:, :, 0:32], row(1, 32, 64), ALU.mult))
                dve.tensor_copy(iwc, pr[:, C_IW:C_IW + 4]).then_inc(S["iw_ready"], 1)
                dve.wait_ge(S["ra_ps"], after(t))
                dve.tensor_tensor(x8, ta, tb, ALU.add).then_inc(S["rope_done"], 1)
                dve.wait_ge(S["rope_done"], after(t + 1))
                dve.wait_ge(S["rs_ps"], after(t))
                for a in range(2):
                    kv = kd[:, :, :].rearrange("p (c a) d -> p a c d", a=2)[:, a, :, a * HD:(a + 1) * HD]
                    src = pr[:, C_KB:C_KB + 256].rearrange("p (c a d) -> p a c d", a=2, d=HD)[:, a]
                    dec = kdec[:, :].rearrange("p (c a) -> p a c", a=2)[:, a].unsqueeze(2).to_broadcast([P, 2, HD])
                    ins = dve.tensor_tensor(kv, src, dec, ALU.mult)
                ins.then_inc(S["kd_ready"], 1)
                dve.wait_ge(S["g_tanh"], after(t + 1))
                dve.scalar_tensor_tensor(tg[:, 0:512], tg[:, 0:512], 1.0, pr[:, C_ZA:C_ZA + 512], ALU.add, ALU.mult)
                dve.scalar_tensor_tensor(tg[:, 512:1024], tg[:, 512:1024], 1.0, pr[:, C_ZB:C_ZB + 512], ALU.add,
                                         ALU.mult).then_inc(S["gates_done"], 1)
                dve.wait_ge(S["tr_sb"], after(3 * t + 3))
                dve.wait_ge(S["ro_ps"], after(t))
                dve.tensor_tensor(qbd[:, :, :], qkbT[:, 0:2, :], qdec[:, :, :], ALU.mult)\
                   .then_inc(S["qd_ready"], 1)
                dve.wait_ge(S["iw_ready"], after(t + 1))
                for u in range(4 * NK):
                    c, h = divmod(u, 4)
                    dve.wait_ge(S["idx_rd"], after(4 * U + u + 1))
                    dst = isc[:, c * CH:(c + 1) * CH]
                    if h == 0:
                        dve.tensor_scalar(dst, relu[:, u % 2, :], iwc[:, 0:1], None, ALU.mult)\
                           .then_inc(S["idx_acc"], 1)
                    else:
                        dve.wait_ge(S["idx_acc"], after(4 * U + u))
                        dve.scalar_tensor_tensor(dst, relu[:, u % 2, :], iwc[:, h:h + 1], dst, ALU.mult, ALU.add)\
                           .then_inc(S["idx_acc"], 1)
                dve.wait_ge(S["ra_ps"], after(t + 1))
                for a in range(2):
                    ins = dve.tensor_tensor(attm[:, a, :], PS[a][:, 0:2 * P], rmask[:, a, :], ALU.mult)
                ins.then_inc(S["ra_sb"], 1)
                dve.wait_ge(S["ro_ps"], after(t + 1))
                for h in range(RH):
                    ins = dve.scalar_tensor_tensor(rst[:, h, :], rst[:, h, :], cdec[:, h:h + 1],
                                                   PT[1][:, h * RV:(h + 1) * RV], ALU.mult, ALU.add)
                ins.then_inc(S["r_upd"], 1)
                pv = PR[:, :].rearrange("p (h d) -> p h d", d=RV)
                cv = gn_c.rearrange("p (h d) -> p h d", d=RV)
                qv = gn_q.rearrange("p (h d) -> p h d", d=RV)
                dve.wait_ge(S["idx_acc"], after(4 * U + 4 * NK))
                link(dve.tensor_reduce(gsum, pv, AX, ALU.add))
                link(dve.tensor_scalar(gsum, gsum, -1.0 / RV, None, ALU.mult))
                link(dve.tensor_tensor(cv, pv, gsum.unsqueeze(2).to_broadcast([P, RH, RV]), ALU.add))
                link(dve.tensor_tensor(qv, cv, cv, ALU.mult))
                dve.tensor_reduce(gsq, qv, AX, ALU.add).then_inc(S["gn_sum"], 1)
                link(dve.tensor_reduce(lo_b, isc[:, 0:W], AX, ALU.min))
                link(dve.tensor_reduce(hi_b, isc[:, 0:W], AX, ALU.max))
                dve.wait_ge(S["caus_loaded"], after(16 * (t + 1)))
                tail = isc[:, W - CH:W]
                link(dve.tensor_tensor(tail, tail, caus[:, :], ALU.add))
                link(dve.tensor_scalar(lo_b, lo_b, 0.0, None, ALU.min))
                link(dve.tensor_scalar(hi_b, hi_b, 0.0, 1e-20, ALU.max, ALU.add))
                link(dve.tensor_tensor(rng_, hi_b, lo_b, ALU.subtract))
                link(dve.tensor_scalar(halves[:, :], pow2[:, :], rng_, None, ALU.mult))
                link(dve.tensor_tensor(mid, lo_b, halves[:, 0:1], ALU.add))
                for n in range(STEPS):
                    link(dve.tensor_scalar(mb[:, 0:W], isc[:, 0:W], mid, 0.0, ALU.is_gt, ALU.add, accum_out=cnt))
                    link(dve.tensor_scalar(ph, cnt, TOPK - 0.5, halves[:, n:n + 1], ALU.is_ge, ALU.mult))
                    link(dve.scalar_tensor_tensor(mid, ph, halves[:, n + 1:n + 2], mid, ALU.subtract, ALU.add))
                w = halves[:, STEPS - 3:STEPS - 2]
                link(dve.tensor_tensor(hi_c, mid, w, ALU.add))
                link(dve.tensor_tensor(lo_c, mid, w, ALU.subtract))
                above, band, order = sm[:, 0, 0:W], sm[:, 1, 0:W], isc[:, 0:W]
                link(dve.tensor_scalar(above, isc[:, 0:W], hi_c, 0.0, ALU.is_gt, ALU.add, accum_out=cgt))
                link(dve.tensor_scalar(need, cgt, -1.0, float(TOPK), ALU.mult, ALU.add))
                link(dve.scalar_tensor_tensor(band, isc[:, 0:W], lo_c, above, ALU.is_gt, ALU.subtract))
                link(dve.tensor_tensor_scan(order, band, band, 0.0, ALU.add, ALU.bypass))
                link(dve.scalar_tensor_tensor(band, order, need, band, ALU.is_le, ALU.mult))
                link(dve.tensor_tensor(band, band, above, ALU.add))
                link(dve.tensor_scalar(mb[:, 0:W], band, BIG, -BIG, ALU.mult, ALU.add))
                dve.wait_ge(S["gn_rs"], after(t + 1))
                link(dve.tensor_tensor(cv, cv, grs.unsqueeze(2).to_broadcast([P, RH, RV]), ALU.mult))
                link(dve.tensor_tensor(gn_c, gn_c, gng[:, :], ALU.mult))
                dve.tensor_tensor(yab[:, 512:1024], gn_c, tg[:, 512:1024], ALU.mult).then_inc(S["gn_done"], 1)
                dve.sem_inc(S["mask_ready"], 1)

            def tile_attend(g, j):
                t, U, NK = j + GT * g, j * (g + 1) + units_before(g), g + 1
                fresh()
                for h in range(AH):
                    for c in range(NK):
                        u = h * NK + c
                        dve.wait_ge(S["s_ps"], after(8 * U + u + 1))
                        link()
                        if c == 0 and h >= 2:
                            dve.wait_ge(S["pt_ps"], after(8 * U + (h - 1) * NK))
                        dve.tensor_tensor_reduce(sm[:, h % 2, c * CH:(c + 1) * CH], PS[u % 2][:, :],
                                                 mb[:, c * CH:(c + 1) * CH], 1.0, -3e38, ALU.add, ALU.max,
                                                 mxc[:, c:c + 1]).then_inc(S["sm_done"], 1)
                    dve.wait_ge(S["sm_done"], after(8 * U + h * NK + NK))
                    link(dve.tensor_reduce(vtmp, mxc[:, 0:NK], AX, ALU.max))
                    dve.tensor_scalar(negm[:, h:h + 1], vtmp, -HD ** -0.5, None, ALU.mult).then_inc(S["nm_ready"], 1)
                dve.wait_ge(S["exp_done"], after(8 * t + 8))
                link(dve.reciprocal(rinv, rsum))
                link(dve.tensor_scalar(rinv, rinv, 0.5, None, ALU.mult))
                dve.wait_ge(S["pv_done"], after(8 * U + 8 * NK))
                for h in range(AH):
                    hs = slice(h * HD, (h + 1) * HD)
                    ins = dve.scalar_tensor_tensor(yab[:, hs], PO[:, hs], rinv[:, h:h + 1], tg[:, hs], ALU.mult,
                                                   ALU.mult)
                ins.then_inc(S["yab_ready"], 1)

            dve.wait_ge(S["c_loaded"], after(16 * 8))
            dve.tensor_scalar(gng[:, :], gng[:, :], 0.5, None, ALU.mult).then_inc(S["const_ready"], 1)
            dve.memset(nhalf[:, :], -0.5).then_inc(S["const_ready"], 1)
            dve.wait_ge(S["const_ready"], after(2))
            dve.wait_ge(S["zeroed"], after(7))
            for g in range(GROUPS):
                with dve.Fori(0, GT) as j:
                    tile_in(g, j)
                    tile_attend(g, j)

        @block.gpsimd
        def _(pool):
            link, fresh = link_in(pool, S["pool_link"])
            for z in (qT[:, :, :], iqT[:, :, :], kT[:, :], ikT[:, :], vst[:, :, :], rst[:, :, :], kd[:, :, :]):
                pool.memset(z, 0.0).then_inc(S["zeroed"], 1)
            pool.wait_ge(S["const_ready"], after(2))

            def stage_a(ai):
                fresh()
                pool.wait_ge(S["ss_ready"], after(ai + 1))
                link()
                link(pool.tensor_scalar(rstd, ssum, 1.0 / D, EPS, ALU.mult, ALU.add))
                pool.tensor_tensor(rstd, rstd, nhalf[:, 0:1], ALU.pow).then_inc(S["rstd_ready"], 1)

            def tile(t):
                pool.wait_ge(S["rope_done"], after(t + 1))
                pool.wait_ge(S["a_evac"], after(A_UNITS * (t + 1)))
                pool.wait_ge(S["zeroed"], after(7))
                pool.tensor_copy(vst[:, ds(t, 1), :], pr[:, C_VA:C_VA + P].unsqueeze(1)).then_inc(S["v_stored"], 1)
                stage_a(t + 1)
                pool.wait_ge(S["gn_sum"], after(t + 1))
                link()
                link(pool.tensor_scalar(grs, gsq, 1.0 / RV, EPS, ALU.mult, ALU.add))
                pool.tensor_tensor(grs, grs, nhalf[:, :], ALU.pow).then_inc(S["gn_rs"], 1)

            stage_a(0)
            for g in range(GROUPS):
                with pool.Fori(0, GT) as j:
                    tile(j + GT * g)

        @block.sync
        def _(sp):
            for c in range(KD):
                sp.dma_start(w_in[:, c, :], io["w_in_ab"][c * P:(c + 1) * P, :]).then_inc(S["w_loaded"], 16)
            for dst, src in ((ident, io["ident"]), (rmask, io["rmask"].rearrange("p (h t) -> p h t", h=2)),
                             (qdec, io["qdec"].rearrange("p (h t) -> p h t", h=2)), (kdec, io["kdec"]),
                             (cdec, io["cdec"]), (pow2, io["pow2"]),
                             (nw0, io["norm_w"][0:1, :].rearrange("a (c p) -> p (a c)", p=P)),
                             (gng, io["gn_ret"].partition_broadcast(P))):
                sp.dma_start(dst[tuple(slice(None) for _ in dst.shape)], src,
                             allow_slow_non_contiguous=True).then_inc(S["c_loaded"], 16)

            def load_x(ai):
                sp.dma_start(xa[:, :], io["x_all"][ds(ai * P, P), :]).then_inc(S["x_loaded"], 16)

            def load_tables(t):
                sp.dma_start(ropea[:, :, :, :].rearrange("p a h d -> p (a h d)"), io["ropea"][ds(t * P, P), :])\
                  .then_inc(S["tab_loaded"], 16)
                sp.dma_start(ropeb[:, :, :].rearrange("p a d -> p (a d)"), io["ropeb"][ds(t * P, P), :])\
                  .then_inc(S["tab_loaded"], 16)

            load_x(0)
            load_tables(0)
            for g in range(GROUPS):
                with sp.Fori(0, GT) as j:
                    t = j + GT * g
                    sp.wait_ge(S["a_evac"], after(A_UNITS * (t + 1)))
                    load_x(t + 1)
                    sp.wait_ge(S["mask_ready"], after(t))
                    sp.dma_start(caus[:, :], io["caus"][:, ds(j * CH, CH)]).then_inc(S["caus_loaded"], 16)
                    sp.wait_ge(S["rope_done"], after(t + 1))
                    sp.dma_start(io["k_all"][ds(t * P, P), :], pr[:, C_KA:C_KA + P]).then_inc(S["kv_stored"], 16)
                    sp.dma_start(io["v_all"][ds(t * P, P), :], pr[:, C_VA:C_VA + P]).then_inc(S["kv_stored"], 16)
                    sp.dma_start(io["ik_all"][ds(t * P, P), :], pr[:, C_IK:C_IK + HD]).then_inc(S["kv_stored"], 16)
                    load_tables(t + 1)
                    sp.wait_ge(S["yab_ready"], after(t + 1))
                    sp.wait_ge(S["gn_done"], after(t + 1))
                    sp.dma_start(io["yab_all"][ds(t * P, P), :], yab[:, :]).then_inc(S["yab_stored"], 16)
            sp.wait_ge(S["kv_stored"], after(48 * NT))
            sp.wait_ge(S["yab_stored"], after(16 * NT))
            sp.wait_ge(S["r_upd"], after(NT))
            for h in range(RH):
                lo = HD * (h % 2)
                sp.dma_start(io["ret_prompt"][h], rst[lo:lo + HD, h, :]).then_inc(S["ret_stored"], 16)
            sp.wait_ge(S["a_evac"], after(A_UNITS * (NT + 1)))
            sp.dma_start(io["pr_s"], pr[:, :]).then_inc(S["ret_stored"], 16)
            sp.wait_ge(S["ret_stored"], after(80))




NBLK = CC // P
CONV = 4
LAYER0_SIGNALS = """
    a_evac a_psum c_loaded caus_loaded const_ready exp_done g_tanh gates_done gn_done gn_rs gn_sum hn_ready
    idx_acc idx_ps idx_rd iw_ready kd_ready kv_stored mask_ready nm_ready pt_ps pt_sb pv_done qd_ready r_upd
    ra_ps ra_sb ret_stored ro_ps rope_done rs_ps rstd_ready s_ps sm_done ss_ready tab_loaded tr_ps tr_sb
    v_stored w_loaded x_loaded yab_ready yab_stored zeroed"""
SAMPLES_SIGNALS = """
    c4_loaded const4 exp4 gr4 gs4 iS_ps iS_sb isc4 iw_ps kd4 kt_ps kt_sb0 kt_sb1 mb4 new_out nm4 oall4 og4
    pt4_ps pt4_sb pv4 q4_ps qbm4 qkb4 qm4 ra4_ps ra4_sb ret4_done ro4_ps rope4 rs4_upd rs_loaded rs_stored
    s4_mx s4_ps s4_sb stage0 stage1 su4_ps tails4 tanh4 v4_0 vm4 vt4 w4 wsel4 ya4 yab4 zeroed4 zeroed5"""
CONV_SIGNALS = """
    blk_ps c2_loaded c_stored0 c_stored1 const2_ready crow_ps crow_ready cs_ps cs_ready cv_ready cv_stored
    cvh_ready cvt_ready hT2_ps hT2_sb hn2_ready pre_kept pre_loaded pre_ps pre_ready raw_ready rstd2_ready
    ss2_ready tail_kept w2c_loaded w2o_loaded x2_loaded y1_ps y1_ready y1_stored yT_ps yT_sb yab2_loaded
    z_free z_ps zg_ready zg_stored zt_ready"""
DELTA_SIGNALS = """
    ML_ready MT_ready QKD_ready R_ready bb_ps bv_ready c3_loaded cin_loaded const3_ready cur_ready dec_ready
    dif_ready egl_ps egl_read eglm_ready fr_ready fs_ready g_ready gc_ps gcb_ps kk_ps ks_ps ks_read kt_ready
    oT_ps oT_ready o_ps o_ready o_sq og_ready or_ready os_ready p1_ps p1_ready pre_a pre_d qkT_ps qkT_ready
    qk_ps qk_rs qk_sq qk_ss qkm_ready qkm_zero qkn_ready qs_ps qs_read sg_loaded sg_upd sgu_ps st_stored
    st_upd su_ps vn_ps vn_ready vnm_ready w3_loaded x_ps x_ready y13_loaded y2_ps y2_ready yo_ready
    yo_stored zg3_loaded"""
LINKS = "act_link dve_link pool_link late_values"
OUTS = {"y_all": (ROWS, D), "k_all": (ROWS, 128), "v_all": (ROWS, 128), "ik_all": (ROWS, 64),
        "ret_prompt": (RH, HD, RV), "ret_sample": (DB, RH, HD, RV),
        "gdn_prompt": (8, P, P), "gdn_sample": (DB, 8, P, P), "conv_prompt": (3, CC), "conv_sample": (DB * 3, CC),
        "yab_all": (ROWS, D), "y1_all": (ROWS, D), "zg_all": (ROWS, D), "c_all": (ROWS, CC), "pr_s": (P, ABW)}


SKEYS = PAST + DT
N_CONST4 = 17
STAGE_FREE = (12, 16, 24, 32)
HB = DB // 2


def layer0_samples(nc, io, S):
    ctx = ExitStack()
    with ctx:
        def sb(name, shape, dt=FP):
            return ctx.enter_context(nc.sbuf_tensor(name, shape, dt))

        def ps(name):
            return ctx.enter_context(nc.psum_tensor(name, [P, 512], FP))

        pr = sb("prs", [P, ABW])
        K_T = [sb("kT0", [P, HB, SKEYS]), sb("kT1", [P, HB, SKEYS])]
        rows_a = sb("rows_a", [P, HB * SKEYS])
        rows_b = sb("rows_b", [P, 8 * DB * P])
        ikT = rows_a[:, :].rearrange("p (b s) -> p b s", b=HB)
        V_A = rows_a[:, 0:8 * DB * P].rearrange("p (g b d) -> p g b d", g=8, b=DB)
        V_B = rows_b[:, :].rearrange("p (g b d) -> p g b d", g=8, b=DB)
        stage = rows_b[:, :].rearrange("p (s g d) -> p s g d", s=2, g=NPG)
        sc = [sb("sc0", [P, SKEYS]), sb("sc1", [P, SKEYS])]
        isc = sb("isc_s", [SR, SKEYS])
        mb128 = sb("mb_s", [P, SKEYS])
        mb = mb128[0:SR, :]
        ptT = sb("ptT_s", [P, 2, 512])
        ptz = sb("ptt_s", [P, 2, P])
        vtz = sb("vtail", [P, DB, P])
        ptd = sb("ptd", [P, 512])
        qm = sb("qm", [P, 3, HB, P])
        hm = sb("hm_t", [P, HB, SR])
        rep = sb("rep_t", [P, SR])
        rep4 = sb("rep4_t", [P, P])
        tmask = sb("tmask_t", [SR, DT])
        dsel = sb("dsel_t", [P, DB])
        wcol = sb("wcol", [P, 1])
        wsel = sb("wsel", [P, SR])
        ident = sb("ident4", [P, P])
        pow2 = sb("pow2_s", [P, STEPS + 1])
        ptab = sb("ptab", [1, DB * NPG], I32)
        tg = sb("tg_s", [P, D])
        oall = sb("oall", [SR, 512])
        og = sb("og_s", [P, 2, HD])
        small = sb("small_s", [P, 64])
        halves = sb("halves_s", [P, STEPS + 1])
        nhalf = sb("nhalf_s", [P, RH])
        r0 = K_T[0][:, :, :].rearrange("p b s -> p (b s)")
        rs = r0[:, 0:DB * RH * P].rearrange("p (b h d) -> p b h d", b=DB, h=RH)
        vm = r0[:, 4096:4096 + 2048].rearrange("p (a b d) -> p a b d", a=2, b=DB)
        qbm = r0[:, 6144:6144 + 512].rearrange("p (c b t) -> p c b t", c=2, b=DB)
        kd = r0[:, 6656:7168].rearrange("p (h d) -> p h d", h=RH)
        qkbT = r0[:, 7168:7680].rearrange("p (h d) -> p h d", h=4)
        attm = r0[:, 7680:8192].rearrange("p (a d) -> p a d", a=2)
        r1 = K_T[1][:, :, :].rearrange("p b s -> p (b s)")
        rmask = r1[:, 0:512].rearrange("p (a d) -> p a d", a=2)
        qdec = r1[:, 512:1024].rearrange("p (c b t) -> p c b t", c=2, b=DB)
        gng = r1[:, 1024:1536]
        kdec = r1[:, 1536:1540]
        cdec = r1[:, 1540:1544]
        bsel = r1[:, 1544:1552]
        gn_c, gn_q = r1[:, 2048:2560], r1[:, 2560:3072]
        rt_a, rt_b = r1[:, 3072:3584], r1[:, 3584:4096]
        ropea = r1[:, 4096:4096 + 544].rearrange("p (a h d) -> p a h d", a=2, h=NHEADS17)
        ropeb = r1[:, 4640:4640 + 128].rearrange("p (a d) -> p a d", a=2)
        lo_b, hi_b, rng_, mid, cnt, ph, hi_c, lo_c, cgt, need = [small[0:SR, i:i + 1] for i in range(10)]
        gsum, gsq, grs = small[:, 12:16], small[:, 16:20], small[:, 20:24]
        mx8, mx1, negm, rsum, rinv = small[:, 24:34], small[:, 34:36], small[:, 36:38], small[:, 38:40], small[:, 40:42]
        PA = [ps("SA0"), ps("SA1")]
        PS = [ps("SS0"), ps("SS1")]
        PT = [ps("ST0"), ps("ST1")]
        PO = [ps("SO0"), ps("SO1")]
        block = ctx.enter_context(nc.Block())
        CHUNKS = [(c * CH, CH) for c in range(PAST // CH)] + [(PAST, DT)]
        NCH = len(CHUNKS)
        npool = io["cache_k"].shape[0]

        def fetch(eng, cache, b, first, count, dst_of, signal):
            with eng.Fori(0, count // 4) as g4:
                for k in range(4):
                    g = 4 * g4 + k
                    page = eng.value_load(ptab[0:1, ds(g + (b * NPG + first), 1)], min_val=0, max_val=npool - 1)
                    eng.dma_start(dst_of(g), cache(page)).then_inc(S[signal], 16)

        def index_pages(eng, i, a):
            fetch(eng, lambda page: io["cache_kidx"][ds(page, 1)].rearrange("a k d -> k (a d)"), i + HB * a, 0, NPG,
                  lambda g: stage[:, i % 2, ds(g, 1), a * HD:(a + 1) * HD].rearrange("p a d -> p (a d)"),
                  "stage%d" % (i % 2))

        def key_pages(eng, i, a):
            fetch(eng, lambda page: io["cache_k"][ds(page, 1)].rearrange("a k (g d) -> k (a g) d", g=2), i + HB * a,
                  0, NPG, lambda g: stage[:, i % 2, ds(g, 1), :]
                  .rearrange("p x (g a d) -> p (x g) a d", g=2, a=2)[:, :, a], "stage%d" % (i % 2))

        def value_pages(eng, part, b):
            dst = (V_A, V_B)[part]
            fetch(eng, lambda page: io["cache_v"][ds(page, 1)].rearrange("a k d -> k (a d)"), b, 8 * part, NPG // 2,
                  lambda g: dst[:, ds(g, 1), b, :].rearrange("p x d -> p (x d)"), ("v4_0", "late_values")[part])

        @block.sync
        def _(sp):
            consts = ((ident[:, :], io["ident"]), (hm[:, :, :].rearrange("p b t -> p (b t)"), io["hm"]),
                      (rep[:, :], io["rep"]), (rep4[:, :], io["rep4"]), (tmask[:, :], io["tmask"]),
                      (dsel[:, :], io["dsel"]), (pow2[:, :], io["pow2"]), (ptab[:, :], io["page_table"]),
                      (rmask.rearrange("p a d -> p (a d)"), io["rmask_s"]),
                      (qdec.rearrange("p c b t -> p (c b t)"), io["qdec_s"]), (kdec, io["kdec_s"]),
                      (cdec, io["cdec_s"]), (bsel, io["bsel"][:, 0:DB]), (gng, io["gn_ret"].partition_broadcast(P)),
                      (ropea.rearrange("p a h d -> p (a h d)"), io["ropea"][SEQ:ROWS, :]),
                      (ropeb.rearrange("p a d -> p (a d)"), io["ropeb"][SEQ:ROWS, :]),
                      (pr[:, :], io["pr_s"]))
            for dst, src in consts:
                sp.dma_start(dst, src, allow_slow_non_contiguous=True).then_inc(S["c4_loaded"], 16)
            assert len(consts) == N_CONST4
            sp.wait_ge(S["zeroed4"], after(2))
            for h in range(RH):
                lo = HD * (h % 2)
                sp.dma_start(rs[lo:lo + HD, :, h, :], io["state_ret"][:, h].rearrange("b d e -> d b e"))\
                  .then_inc(S["rs_loaded"], 16)

            sp.wait_ge(S["c4_loaded"], after(16 * N_CONST4))

            for i in range(2):
                index_pages(sp, i, 0)
            sp.wait_ge(S["rope4"], after(1))
            sp.dma_start(io["k_all"][SEQ:ROWS, :], pr[:, C_KA:C_KA + P]).then_inc(S["new_out"], 16)
            sp.dma_start(io["v_all"][SEQ:ROWS, :], pr[:, C_VA:C_VA + P]).then_inc(S["new_out"], 16)
            sp.dma_start(io["ik_all"][SEQ:ROWS, :], pr[:, C_IK:C_IK + HD]).then_inc(S["new_out"], 16)
            for h in range(4):
                sp.dma_start(wcol[h * SR:(h + 1) * SR, :], pr[0:SR, C_IW + h:C_IW + h + 1]).then_inc(S["w4"], 16)
            sp.wait_ge(S["zeroed5"], after(3))
            for b in range(DB):
                sp.dma_start(vtz[0:DT, b, :], pr[b * DT:(b + 1) * DT, C_VA:C_VA + P]).then_inc(S["vt4"], 16)
            for i in range(2, HB):
                sp.wait_ge(S["kt_ps"], after(4 * (i - 1)))
                index_pages(sp, i, 0)
            sp.wait_ge(S["rs4_upd"], after(2 * RH))
            for h in range(RH):
                lo = HD * (h % 2)
                sp.dma_start(io["ret_sample"][:, h].rearrange("b d e -> d b e"), rs[lo:lo + HD, :, h, :])\
                  .then_inc(S["rs_stored"], 16)
            for i in range(HB):
                sp.wait_ge(S["kt_ps"], after(STAGE_FREE[i]))
                key_pages(sp, i, 0)
            sp.wait_ge(S["iS_ps"], after(NCH))
            for b in range(DB):
                value_pages(sp, 0, b)
            sp.wait_ge(S["og4"], after(2))
            for g in range(2):
                for r in range(4):
                    h = 4 * g + r
                    sp.dma_start(oall[:, h * HD:(h + 1) * HD], og[r * SR:(r + 1) * SR, g, :]).then_inc(S["oall4"], 16)
            sp.dma_start(io["yab_all"][SEQ + SR:ROWS, :], io["x_all"][SEQ + SR:ROWS, :]).then_inc(S["yab4"], 16)
            sp.wait_ge(S["ya4"], after(2))
            sp.dma_start(io["yab_all"][SEQ:SEQ + SR, :], tg[0:SR, :]).then_inc(S["yab4"], 16)
            sp.wait_ge(S["yab4"], after(32))
            sp.wait_ge(S["rs_stored"], after(64))
            sp.wait_ge(S["new_out"], after(48))

        @block.tensor
        def _(pe):
            pe.wait_ge(S["c4_loaded"], after(16 * N_CONST4))
            pe.wait_ge(S["rope4"], after(1))
            for n, base in enumerate((C_QA, C_QA + 256, C_IQ)):
                for r in range(4):
                    for a in range(2):
                        c0 = n * P + r * SR
                        ins = turn_half(pe, PO[0][a * HD:(a + 1) * HD, c0:c0 + SR],
                                        pr[0:SR, base + r * HD:base + (r + 1) * HD], ident[0:SR, 0:SR], a)
            ins.then_inc(S["q4_ps"], 1)
            for n, base in enumerate((C_KA, C_KA + HD, C_IK)):
                for a in range(2):
                    ins = turn_half(pe, PO[1][a * HD:(a + 1) * HD, n * SR:(n + 1) * SR],
                                    pr[0:SR, base:base + HD], ident[0:SR, 0:SR], a)
            ins.then_inc(S["q4_ps"], 1)
            for r in range(4):
                ins = pe.transpose(PA[0][:, r * P:(r + 1) * P], pr[:, C_QB + r * P:C_QB + (r + 1) * P], ident[:, :])
            ins.then_inc(S["q4_ps"], 1)
            pe.wait_ge(S["qkb4"], after(1))
            for h in range(RH):
                lo = HD * (h % 2)
                ins = pe.matmul(PS[h % 2][:, (h // 2) * P:(h // 2 + 1) * P], qkbT[lo:lo + HD, 2 + h // 2, :],
                                qkbT[lo:lo + HD, h // 2, :], start=True, stop=True)
            ins.then_inc(S["ra4_ps"], 1)
            pe.wait_ge(S["ra4_sb"], after(1))
            pe.wait_ge(S["qbm4"], after(1))
            pe.wait_ge(S["rs_loaded"], after(64))
            for h in range(RH):
                o = PA[1][0:SR, h * RV:(h + 1) * RV]
                pe.matmul(o, attm[:, h % 2, (h // 2) * P:(h // 2) * P + SR], pr[:, C_VB + h * RV:C_VB + (h + 1) * RV],
                          start=True, stop=False)
                for b in range(DB):
                    ins = pe.matmul(o, qbm[:, h // 2, b, :], rs[:, b, h, :], start=False, stop=(b == DB - 1))
            ins.then_inc(S["ro4_ps"], 1)
            pe.wait_ge(S["kd4"], after(1))
            for h in range(RH):
                pe.wait_ge(S["vm4"], after(h + 1))
                pe.wait_ge(S["rs4_upd"], after(2 * h))
                for g in range(2):
                    pe.matmul(PT[g][:, :], kd[:, h, :],
                              vm[:, h % 2, 4 * g:4 * g + 4, :].rearrange("p b d -> p (b d)"), start=True, stop=True)\
                      .then_inc(S["su4_ps"], 1)
            pe.wait_ge(S["rs4_upd"], after(2 * RH))

            def turn(units):
                for n, (slot, page, off) in enumerate(units):
                    u = turned[0] + n
                    if u >= 2:
                        pe.wait_ge(S["kt_sb%d" % (u % 2)], after(u // 2))
                    for k in range(4):
                        ins = pe.transpose(PT[u % 2][:, k * P:(k + 1) * P],
                                           stage[:, slot, page + k, off:off + P], ident[:, :])
                    ins.then_inc(S["kt_ps"], 1)
                turned[0] += len(units)

            turned = [0]
            for i in range(HB):
                pe.wait_ge(S["stage%d" % (i % 2)], after(512 * (i // 2 + 1)))
                turn([(i % 2, 4 * q, 0) for q in range(4)])
            pe.wait_ge(S["kt_sb0"], after(8))
            pe.wait_ge(S["kt_sb1"], after(8))
            pe.wait_ge(S["tails4"], after(1))
            pe.wait_ge(S["qm4"], after(3))
            for n, (c0, w) in enumerate(CHUNKS):
                if n >= 2:
                    pe.wait_ge(S["iS_sb"], after(n - 1))
                for i in range(HB):
                    ins = pe.matmul(PS[n % 2][:, 0:w], qm[:, 2, i, :], ikT[:, i, c0:c0 + w], start=(i == 0),
                                    stop=(i == HB - 1))
                ins.then_inc(S["iS_ps"], 1)
            pe.wait_ge(S["wsel4"], after(1))
            for n, (c0, w) in enumerate(CHUNKS):
                pe.wait_ge(S["iS_sb"], after(n + 1))
                if n >= 2:
                    pe.wait_ge(S["isc4"], after(n - 1))
                pe.matmul(PA[n % 2][0:SR, 0:w], wsel[:, :], sc[0][:, c0:c0 + w], start=True, stop=True)\
                  .then_inc(S["iw_ps"], 1)
            for i in range(HB):
                pe.wait_ge(S["stage%d" % (i % 2)], after(1024 + 512 * (i // 2 + 1)))
                turn([(i % 2, 4 * q, P * g) for g in range(2) for q in range(4)])
            pe.wait_ge(S["kt_sb0"], after(24))
            pe.wait_ge(S["kt_sb1"], after(24))
            pe.wait_ge(S["tails4"], after(3))
            pe.wait_ge(S["mb4"], after(1))
            pe.wait_ge(S["zeroed5"], after(3))
            for g in range(2):
                for n, (c0, w) in enumerate(CHUNKS):
                    u = g * NCH + n
                    if u >= 2:
                        pe.wait_ge(S["s4_sb"], after(u - 1))
                        pe.wait_ge(S["s4_mx"], after(u - 1))
                    for i in range(HB):
                        pe.matmul(PS[u % 2][:, 0:w], qm[:, g, i, :], K_T[g][:, i, c0:c0 + w], start=(i == 0),
                                  stop=False)
                    pe.matmul(PS[u % 2][:, 0:w], rep4[:, :], mb128[:, c0:c0 + w], start=False, stop=True)\
                      .then_inc(S["s4_ps"], 1)
            for g in range(2):
                pe.wait_ge(S["exp4"], after(g + 1))
                pe.wait_ge(S["vt4"], after(16 * DB))
                for q in range(5):
                    u = 5 * g + q
                    if u >= 2:
                        pe.wait_ge(S["pt4_sb"], after(u - 1))
                    if q < 4:
                        for k in range(4):
                            c0 = (4 * q + k) * P
                            ins = pe.transpose(PT[u % 2][:, k * P:(k + 1) * P], sc[g][:, c0:c0 + P], ident[:, :])
                    else:
                        ins = pe.transpose(PT[u % 2][0:DT, 0:P], sc[g][:, PAST:SKEYS], ident[:, :])
                    ins.then_inc(S["pt4_ps"], 1)
                    if q == 0:
                        pe.wait_ge(S["v4_0"], after(16 * 8 * DB))
                    if q == 2:
                        pe.wait_ge(S["late_values"], 16 * 8 * DB)
                    pe.wait_ge(S["pt4_sb"], after(u + 1))
                    if q < 4:
                        for k in range(4):
                            pg = 4 * q + k
                            V = (V_A, V_B)[pg // 8]
                            ins = pe.matmul(PO[g][:, :], ptT[:, u % 2, k * P:(k + 1) * P],
                                            V[:, pg % 8, :, g * HD:(g + 1) * HD], start=(pg == 0), stop=False)
                    else:
                        ins = pe.matmul(PO[g][:, :], ptz[:, g, :], vtz[:, :, g * HD:(g + 1) * HD], start=False,
                                        stop=True)
                    ins.then_inc(S["pv4"], 1)

        @block.scalar
        def _(act):
            act.wait_ge(S["c4_loaded"], after(16 * N_CONST4))
            for i in range(2):
                index_pages(act, i, 1)
            act.activation(tg[:, 0:512], pr[:, C_ZA:C_ZA + 512], ACT.Tanh, scale=0.5)
            act.activation(tg[:, 512:1024], pr[:, C_ZB:C_ZB + 512], ACT.Tanh, scale=0.5).then_inc(S["tanh4"], 1)
            act.wait_ge(S["q4_ps"], after(3))
            act.wait_ge(S["zeroed4"], after(2))
            act.copy(qkbT.rearrange("p h d -> p (h d)"), PA[0][:, :]).then_inc(S["qkb4"], 1)

            def evac(u, dst):
                act.wait_ge(S["kt_ps"], after(u + 1))
                act.copy(dst, PT[0][:, :]).then_inc(S["kt_sb0"], 1)

            for i in range(HB):
                for q in (0, 2):
                    evac(4 * i + q, ikT[:, i, q * 512:(q + 1) * 512])
                act.wait_ge(S["kt_ps"], after(4 * (i + 1)))
                if i + 2 < HB:
                    index_pages(act, i + 2, 1)
                else:
                    key_pages(act, i + 2 - HB, 1)
            for n, (c0, w) in enumerate(CHUNKS):
                act.wait_ge(S["iS_ps"], after(n + 1))
                act.activation(sc[0][:, c0:c0 + w], PS[n % 2][:, 0:w], ACT.Relu, scale=1.0 / 16)\
                   .then_inc(S["iS_sb"], 1)
            act.wait_ge(S["ret4_done"], after(1))
            act.wait_ge(S["rs_stored"], after(64))
            for i in range(HB):
                for g in range(2):
                    for q in (0, 2):
                        evac(16 + 8 * i + 4 * g + q, K_T[g][:, i, q * 512:(q + 1) * 512])
                if i + 2 < HB:
                    act.wait_ge(S["kt_ps"], after(STAGE_FREE[i + 2]))
                    key_pages(act, i + 2, 1)
            act.wait_ge(S["mb4"], after(1))
            for g in range(2):
                for n, (c0, w) in enumerate(CHUNKS):
                    u = g * NCH + n
                    act.wait_ge(S["s4_mx"], after(u + 1))
                    act.copy(sc[g][:, c0:c0 + w], PS[u % 2][:, 0:w]).then_inc(S["s4_sb"], 1)
            for g in range(2):
                act.wait_ge(S["nm4"], after(g + 1))
                act.wait_ge(S["s4_sb"], after(NCH * (g + 1)))
                act.activation(sc[g][:, :], sc[g][:, :], ACT.Exp, bias=negm[:, g:g + 1], scale=HD ** -0.5,
                               accum_out=rsum[:, g:g + 1]).then_inc(S["exp4"], 1)
            for u in range(10):
                g, q = divmod(u, 5)
                act.wait_ge(S["pt4_ps"], after(u + 1))
                act.wait_ge(S["zeroed5"], after(3))
                if u >= 2:
                    act.wait_ge(S["pv4"], after(u - 1))
                if q < 4:
                    act.copy(ptT[:, u % 2, :], PT[u % 2][:, :]).then_inc(S["pt4_sb"], 1)
                else:
                    act.copy(ptz[0:DT, g, :], PT[u % 2][0:DT, 0:P]).then_inc(S["pt4_sb"], 1)

        @block.vector
        def _(dve):
            link, fresh = link_in(dve, S["dve_link"])
            dve.memset(nhalf[:, :], -0.5).then_inc(S["const4"], 1)
            dve.wait_ge(S["c4_loaded"], after(16 * N_CONST4))
            link(dve.tensor_scalar(gng, gng, 0.5, None, ALU.mult))
            x17 = pr[:, 0:17 * HD].rearrange("p (h d) -> p h d", d=HD)
            ta = rt_a[:, 0:272].rearrange("p (h d) -> p h d", d=16)
            tb = rt_b[:, 0:272].rearrange("p (h d) -> p h d", d=16)
            dve.tensor_tensor(ta, x17[:, :, 0:16], ropea[:, 0], ALU.mult)
            dve.tensor_tensor(tb[:, :, 0:8], x17[:, :, 8:16], ropea[:, 1, :, 0:8], ALU.mult)
            link(dve.tensor_tensor(tb[:, :, 8:16], x17[:, :, 0:8], ropea[:, 1, :, 8:16], ALU.mult))
            link(dve.tensor_tensor(x17[:, :, 0:16], ta, tb, ALU.add))
            x8 = pr[:, C_QB:C_QB + 512].rearrange("p (h d) -> p h d", d=HD)
            ta = rt_a.rearrange("p (h d) -> p h d", d=HD)
            tb = rt_b.rearrange("p (h d) -> p h d", d=HD)

            def row(k, a, b):
                return ropeb[:, k:k + 1, a:b].to_broadcast([P, 8, b - a])

            dve.tensor_tensor(ta, x8, row(0, 0, HD), ALU.mult)
            dve.tensor_tensor(tb[:, :, 0:32], x8[:, :, 32:64], row(1, 0, 32), ALU.mult)
            link(dve.tensor_tensor(tb[:, :, 32:64], x8[:, :, 0:32], row(1, 32, 64), ALU.mult))
            link(dve.tensor_tensor(x8, ta, tb, ALU.add))
            dve.sem_inc(S["rope4"], 1)
            dve.wait_ge(S["zeroed4"], after(2))
            for a in range(2):
                kv = kd.rearrange("p (c a) d -> p a c d", a=2)[:, a, :, a * HD:(a + 1) * HD]
                src = pr[:, C_KB:C_KB + 256].rearrange("p (c a d) -> p a c d", a=2, d=HD)[:, a]
                dec = kdec.rearrange("p (c a) -> p a c", a=2)[:, a].unsqueeze(2).to_broadcast([P, 2, HD])
                ins = dve.tensor_tensor(kv, src, dec, ALU.mult)
            ins.then_inc(S["kd4"], 1)
            dve.wait_ge(S["tanh4"], after(1))
            dve.scalar_tensor_tensor(tg[:, 0:512], tg[:, 0:512], 1.0, pr[:, C_ZA:C_ZA + 512], ALU.add, ALU.mult)
            link(dve.scalar_tensor_tensor(tg[:, 512:1024], tg[:, 512:1024], 1.0, pr[:, C_ZB:C_ZB + 512], ALU.add,
                                          ALU.mult))
            dve.wait_ge(S["q4_ps"], after(2))
            for n in range(3):
                src = PO[0][:, n * P:(n + 1) * P].rearrange("p (r t) -> p r t", t=SR).unsqueeze(1)\
                    .to_broadcast([P, HB, 4, SR])
                dve.tensor_tensor(qm[:, n].rearrange("p b (r t) -> p b r t", t=SR), src,
                                  hm[:, :, :].unsqueeze(2).to_broadcast([P, HB, 4, SR]), ALU.mult)\
                   .then_inc(S["qm4"], 1)
            dve.wait_ge(S["w4"], after(64))
            dve.tensor_scalar(wsel[:, :], rep[:, :], wcol[:, 0:1], None, ALU.mult).then_inc(S["wsel4"], 1)
            dve.wait_ge(S["qkb4"], after(1))
            dve.tensor_tensor(qbm, qkbT[:, 0:2, 0:SR].unsqueeze(2).to_broadcast([P, 2, DB, SR]), qdec, ALU.mult)\
               .then_inc(S["qbm4"], 1)
            dve.wait_ge(S["ra4_ps"], after(1))
            for a in range(2):
                ins = dve.tensor_tensor(attm[:, a, :], PS[a][:, 0:2 * P], rmask[:, a, :], ALU.mult)
            ins.then_inc(S["ra4_sb"], 1)
            for h in range(RH):
                if h >= 2:
                    dve.wait_ge(S["su4_ps"], after(2 * (h - 1)))
                vb = pr[:, C_VB + h * RV:C_VB + (h + 1) * RV].unsqueeze(1).to_broadcast([P, DB, RV])
                dve.tensor_tensor(vm[:, h % 2], vb, bsel.unsqueeze(2).to_broadcast([P, DB, RV]), ALU.mult)\
                   .then_inc(S["vm4"], 1)
                if h == 0:
                    dve.wait_ge(S["ro4_ps"], after(1))
                for g in range(2):
                    dve.wait_ge(S["su4_ps"], after(2 * h + g + 1))
                    dve.scalar_tensor_tensor(rs[:, 4 * g:4 * g + 4, h, :], rs[:, 4 * g:4 * g + 4, h, :], cdec[:, h:h + 1],
                                             PT[g][:, :].rearrange("p (b d) -> p b d", b=4), ALU.mult, ALU.add)\
                       .then_inc(S["rs4_upd"], 1)
            R32 = slice(0, SR)
            pv = PA[1][R32, :].rearrange("p (h d) -> p h d", d=RV)
            cv = gn_c[R32].rearrange("p (h d) -> p h d", d=RV)
            qv = gn_q[R32].rearrange("p (h d) -> p h d", d=RV)
            link(dve.tensor_reduce(gsum[R32], pv, AX, ALU.add))
            link(dve.tensor_scalar(gsum[R32], gsum[R32], -1.0 / RV, None, ALU.mult))
            link(dve.tensor_tensor(cv, pv, gsum[R32].unsqueeze(2).to_broadcast([SR, RH, RV]), ALU.add))
            link(dve.tensor_tensor(qv, cv, cv, ALU.mult))
            dve.tensor_reduce(gsq[R32], qv, AX, ALU.add).then_inc(S["gs4"], 1)
            dve.wait_ge(S["gr4"], after(1))
            link(dve.tensor_tensor(cv, cv, grs[R32].unsqueeze(2).to_broadcast([SR, RH, RV]), ALU.mult))
            link(dve.tensor_tensor(gn_c[R32], gn_c[R32], gng[R32], ALU.mult))
            link(dve.tensor_tensor(tg[R32, 512:1024], gn_c[R32], tg[R32, 512:1024], ALU.mult))
            dve.sem_inc(S["ret4_done"], 1)
            dve.sem_inc(S["ya4"], 1)

            def evac(u, dst):
                dve.wait_ge(S["kt_ps"], after(u + 1))
                dve.tensor_copy(dst, PT[1][:, :]).then_inc(S["kt_sb1"], 1)

            def tails(n, dst):
                for a in range(2):
                    lo = a * HD
                    src = PO[1][lo:lo + HD, n * SR + a * (SR // 2):n * SR + (a + 1) * (SR // 2)]
                    ins = dve.tensor_copy(dst[lo:lo + HD, :, PAST:SKEYS], src.rearrange("p (b t) -> p b t", t=DT))
                ins.then_inc(S["tails4"], 1)

            tails(2, ikT)
            for i in range(HB):
                for q in (1, 3):
                    evac(4 * i + q, ikT[:, i, q * 512:(q + 1) * 512])
            for n, (c0, w) in enumerate(CHUNKS):
                dve.wait_ge(S["iw_ps"], after(n + 1))
                dve.tensor_copy(isc[:, c0:c0 + w], PA[n % 2][0:SR, 0:w]).then_inc(S["isc4"], 1)
            dve.wait_ge(S["rs_stored"], after(64))
            tails(0, K_T[0])
            tails(1, K_T[1])
            for i in range(HB):
                for g in range(2):
                    for q in (1, 3):
                        evac(16 + 8 * i + 4 * g + q, K_T[g][:, i, q * 512:(q + 1) * 512])
            dve.wait_ge(S["isc4"], after(NCH))
            pw = pow2[R32]
            hv = halves[R32]
            link(dve.tensor_reduce(lo_b, isc[:, :], AX, ALU.min))
            link(dve.tensor_reduce(hi_b, isc[:, :], AX, ALU.max))
            tail = isc[:, PAST:SKEYS]
            link(dve.tensor_tensor(tail, tail, tmask[:, :], ALU.add))
            link(dve.tensor_scalar(lo_b, lo_b, 0.0, None, ALU.min))
            link(dve.tensor_scalar(hi_b, hi_b, 0.0, 1e-20, ALU.max, ALU.add))
            link(dve.tensor_tensor(rng_, hi_b, lo_b, ALU.subtract))
            link(dve.tensor_scalar(hv, pw, rng_, None, ALU.mult))
            link(dve.tensor_tensor(mid, lo_b, hv[:, 0:1], ALU.add))
            dve.wait_ge(S["zeroed5"], after(3))
            for n in range(STEPS):
                link(dve.tensor_scalar(mb[:, :], isc[:, :], mid, 0.0, ALU.is_gt, ALU.add, accum_out=cnt))
                link(dve.tensor_scalar(ph, cnt, TOPK - 0.5, hv[:, n:n + 1], ALU.is_ge, ALU.mult))
                link(dve.scalar_tensor_tensor(mid, ph, hv[:, n + 1:n + 2], mid, ALU.subtract, ALU.add))
            w = hv[:, STEPS - 3:STEPS - 2]
            link(dve.tensor_tensor(hi_c, mid, w, ALU.add))
            link(dve.tensor_tensor(lo_c, mid, w, ALU.subtract))
            above, band, order = sc[0][R32, :], sc[1][R32, :], isc[:, :]
            dve.wait_ge(S["iw_ps"], after(NCH))
            link(dve.tensor_scalar(above, isc[:, :], hi_c, 0.0, ALU.is_gt, ALU.add, accum_out=cgt))
            link(dve.tensor_scalar(need, cgt, -1.0, float(TOPK), ALU.mult, ALU.add))
            link(dve.scalar_tensor_tensor(band, isc[:, :], lo_c, above, ALU.is_gt, ALU.subtract))
            link(dve.tensor_tensor_scan(order, band, band, 0.0, ALU.add, ALU.bypass))
            link(dve.scalar_tensor_tensor(band, order, need, band, ALU.is_le, ALU.mult))
            link(dve.tensor_tensor(band, band, above, ALU.add))
            dve.tensor_scalar(mb[:, :], band, BIG, -BIG, ALU.mult, ALU.add).then_inc(S["mb4"], 1)
            for g in range(2):
                for n, (c0, w) in enumerate(CHUNKS):
                    u = g * NCH + n
                    dve.wait_ge(S["s4_ps"], after(u + 1))
                    dve.tensor_reduce(mx8[:, u:u + 1], PS[u % 2][:, 0:w], AX, ALU.max).then_inc(S["s4_mx"], 1)
                dve.wait_ge(S["s4_mx"], after(NCH * (g + 1)))
                link(dve.tensor_reduce(mx1[:, g:g + 1], mx8[:, g * NCH:(g + 1) * NCH], AX, ALU.max))
                dve.tensor_scalar(negm[:, g:g + 1], mx1[:, g:g + 1], -HD ** -0.5, None, ALU.mult).then_inc(S["nm4"], 1)
            dve.wait_ge(S["exp4"], after(2))
            link(dve.reciprocal(rinv, rsum))
            od = ptd[:, :].rearrange("p (b d) -> p b d", b=DB)
            for g in range(2):
                dve.wait_ge(S["pv4"], after(5 * (g + 1)))
                link(dve.tensor_tensor(od, PO[g][:, :].rearrange("p (b d) -> p b d", b=DB),
                                       dsel[:, :].unsqueeze(2).to_broadcast([P, DB, HD]), ALU.mult))
                link(dve.tensor_reduce(og[:, g, :], ptd[:, :].rearrange("p (b d) -> p d b", b=DB), AX, ALU.add))
                dve.tensor_scalar(og[:, g, :], og[:, g, :], rinv[:, g:g + 1], None, ALU.mult).then_inc(S["og4"], 1)
            dve.wait_ge(S["oall4"], after(16 * AH))
            dve.scalar_tensor_tensor(tg[R32, 0:512], oall[:, :], 0.5, tg[R32, 0:512], ALU.mult, ALU.mult)\
               .then_inc(S["ya4"], 1)

        @block.gpsimd
        def _(pool):
            link, fresh = link_in(pool, S["pool_link"])
            pool.memset(rs, 0.0).then_inc(S["zeroed4"], 1)
            for z in (mb128[:, :], ptz[:, :, :], vtz[:, :, :]):
                pool.memset(z, 0.0).then_inc(S["zeroed5"], 1)
            pool.memset(kd, 0.0).then_inc(S["zeroed4"], 1)
            pool.wait_ge(S["gs4"], after(1))
            pool.wait_ge(S["const4"], after(1))
            link(pool.tensor_scalar(grs[0:SR], gsq[0:SR], 1.0 / RV, EPS, ALU.mult, ALU.add))
            pool.tensor_tensor(grs[0:SR], grs[0:SR], nhalf[0:SR, :], ALU.pow).then_inc(S["gr4"], 1)
            pool.wait_ge(S["c4_loaded"], after(16 * N_CONST4))
            pool.wait_ge(S["kt_ps"], after(48))
            for b in range(DB):
                value_pages(pool, 1, b)


def layer0_out_and_conv(nc, io, S, ab_all):
    ctx = ExitStack()
    with ctx:
        def sb(name, shape, dt=FP):
            return ctx.enter_context(nc.sbuf_tensor(name, shape, dt))

        def ps(name):
            return ctx.enter_context(nc.psum_tensor(name, [P, 512], FP))

        w_c = sb("w_c", [P, KD, CIN])
        w_o = sb("w_o", [P, KD, D])
        hT = sb("hT2", [P, KD, GT * P])
        yab = sb("yab2", [P, D])
        hn = sb("hn", [P, D])
        xin = sb("xin", [P, D])
        y1 = sb("y1", [P, D])
        sx = sb("sx", [P, DB * (DT + 3)])
        yT = sb("yT", [P, KD, P])
        raw = sb("raw", [P, 2, 3 + GT * P])
        cva = sb("cva", [P, 2, GT * P])
        cvt = sb("cvt", [P, GT * P])
        crow = sb("crow", [P, 2, GT * P])
        tails = sb("tails", [P, NBLK, 3])
        cw = sb("cw", [P, CONV, NBLK])
        ident = sb("ident2", [P, P])
        nw1 = sb("nw1", [P, KD])
        gn = sb("gn_t", [P, P])
        zg = sb("zg", [P, 512])
        pre = sb("pre", [P, NBLK, DB * 3])
        nhalf = sb("nhalf2", [P, 1])
        stat = sb("stat2", [P, 2])
        ssum, rstd = stat[:, 0:1], stat[:, 1:2]
        crw = sb("crw", [DB * 3, CC])
        PA = [ps("QA0"), ps("QA1")]
        PS = [ps("QS0"), ps("QS1")]
        PT = [ps("QT0"), ps("QT1")]
        PB = [ps("QB0"), ps("QB1")]
        block = ctx.enter_context(nc.Block())
        NSUB = NT + 1
        NB_ALL = NBLK * (GROUPS + 1)

        Z_CUTS = [(CC, CC + 512), (CC + 512, CC + 1024), (CC + 1024, CIN)]

        @block.sync
        def _(sp):
            for c in range(KD):
                sp.dma_start(w_o[:, c, :], io["w_out_ab"][c * P:(c + 1) * P, :]).then_inc(S["w2o_loaded"], 16)
            for c in range(KD):
                sp.dma_start(w_c[:, c, :], io["w_in_c"][c * P:(c + 1) * P, :]).then_inc(S["w2c_loaded"], 16)
            for dst, src in ((ident, io["ident"]),
                             (nw1, io["norm_w"][1:2, :].rearrange("a (c p) -> p (a c)", p=P)),
                             (gn, io["gdn_norm"].partition_broadcast(P))):
                sp.dma_start(dst[:, :], src, allow_slow_non_contiguous=True).then_inc(S["c2_loaded"], 16)
            for k in range(CONV):
                sp.dma_start(cw[:, k, :], io["conv_w"][k:k + 1, :].rearrange("a (c p) -> p (a c)", p=P),
                             allow_slow_non_contiguous=True).then_inc(S["c2_loaded"], 16)

            def sub_in(T):
                sp.wait_ge(S["yT_ps"], after(2 * T))
                sp.dma_start(yab[:, :], io["yab_all"][ds(T * P, P), :]).then_inc(S["yab2_loaded"], 16)
                sp.wait_ge(S["y1_ready"], after(2 * T))
                sp.dma_start(xin[:, :], io["x_all"][ds(T * P, P), :]).then_inc(S["x2_loaded"], 16)

            def sub_out(T):
                sp.wait_ge(S["y1_ready"], after(2 * T + 2))
                sp.dma_start(io["y1_all"][ds(T * P, P), :], y1[:, :]).then_inc(S["y1_stored"], 16)

            def z_out(T):
                for k in range(2):
                    sp.wait_ge(S["zg_ready"], after(2 * T + k + 1))
                    sp.dma_start(io["zg_all"][ds(T * P, P), k * 512:(k + 1) * 512], zg[:, :])\
                      .then_inc(S["zg_stored"], 16)

            def blocks(G, n):
                for b in range(NBLK):
                    u = NBLK * G + b
                    sp.wait_ge(S["crow_ready"], after(u + 1))
                    for s in range(n):
                        sp.dma_start(io["c_all"][ds((G * GT + s) * P, P), b * P:(b + 1) * P],
                                     crow[:, b % 2, s * P:(s + 1) * P]).then_inc(S["c_stored%d" % (b % 2)], 16)

            def group(G, n):
                for s in range(n + 1):
                    if s < n:
                        sub_in(G * GT + s)
                        sub_out(G * GT + s)
                    if s:
                        z_out(G * GT + s - 1)
                blocks(G, n)

            with sp.Fori(0, GROUPS) as G:
                group(G, GT)
            sp.wait_ge(S["cs_ready"], after(4))
            sp.dma_start(io["conv_prompt"], crw[0:3, :]).then_inc(S["cv_stored"], 16)
            sp.wait_ge(S["cv_stored"], after(16))
            sp.dma_start(crw[:, :], io["state_conv"]).then_inc(S["pre_loaded"], 16)
            group(GROUPS, 1)
            sp.wait_ge(S["cs_ready"], after(8))
            sp.dma_start(io["conv_sample"], crw[:, :]).then_inc(S["cv_stored"], 16)
            sp.wait_ge(S["cv_stored"], after(32))
            sp.wait_ge(S["y1_stored"], after(16 * NSUB))
            sp.wait_ge(S["zg_stored"], after(32 * NSUB))
            for k in range(2):
                sp.wait_ge(S["c_stored%d" % k], after(16 * NBLK // 2 * (NT + 1)))

        @block.tensor
        def _(pe):
            def out_proj(T):
                pe.wait_ge(S["yab2_loaded"], after(16 * (T + 1)))
                pe.wait_ge(S["hT2_sb"], after(2 * T))
                for u in range(2):
                    for k in range(4):
                        c = 4 * u + k
                        ins = pe.transpose(PT[u][:, k * P:(k + 1) * P], yab[:, c * P:(c + 1) * P], ident[:, :])
                    ins.then_inc(S["yT_ps"], 1)
                pe.wait_ge(S["yT_sb"], after(2 * T + 2))
                pe.wait_ge(S["y1_ready"], after(2 * T))
                for n in range(2):
                    for c in range(KD):
                        ins = pe.matmul(PS[n][:, :], yT[:, c, :], w_o[:, c, n * 512:(n + 1) * 512],
                                        start=(c == 0), stop=(c == KD - 1))
                    ins.then_inc(S["y1_ps"], 1)

            def turn_h(T, s):
                pe.wait_ge(S["hn2_ready"], after(T + 1))
                pe.wait_ge(S["yT_sb"], after(2 * T + 2))
                for u in range(2):
                    for k in range(4):
                        c = 4 * u + k
                        ins = pe.transpose(PT[u][:, k * P:(k + 1) * P], hn[:, c * P:(c + 1) * P], ident[:, :])
                    ins.then_inc(S["hT2_ps"], 1)

            def z_proj(T, s):
                pe.wait_ge(S["hT2_sb"], after(2 * T + 2))
                pe.wait_ge(S["w2c_loaded"], after(16 * KD))
                for n, (a, b) in enumerate(Z_CUTS):
                    if n < 2:
                        pe.wait_ge(S["z_free"], after(3 * T))
                    else:
                        pe.wait_ge(S["z_free"], after(3 * T + 1))
                    for c in range(KD):
                        ins = pe.matmul(PA[n % 2][:, 0:b - a], hT[:, c, s * P:(s + 1) * P], w_c[:, c, a:b],
                                        start=(c == 0), stop=(c == KD - 1))
                    ins.then_inc(S["z_ps"], 1)

            def blocks(G, n):
                N = n * P
                for b in range(NBLK + 2):
                    u = G * NBLK + b
                    if b < NBLK:
                        pe.wait_ge(S["raw_ready"], after(u - 1) if b >= 2 else after(G * NBLK))
                        for c in range(KD):
                            ins = pe.matmul(PB[b % 2][:, 0:N], w_c[:, c, b * P:(b + 1) * P], hT[:, c, 0:N],
                                            start=(c == 0), stop=(c == KD - 1))
                        ins.then_inc(S["blk_ps"], 1)
                    if b >= 2:
                        v = u - 2
                        pe.wait_ge(S["cv_ready"], after(v + 1))
                        if b >= 4:
                            pe.wait_ge(S["crow_ready"], after(v - 1))
                        elif b == 2:
                            pe.wait_ge(S["z_free"], after(3 * (G * GT + n)))
                        for s in range(n):
                            ins = pe.transpose(PA[b % 2][:, s * P:(s + 1) * P], cva[:, b % 2, s * P:(s + 1) * P],
                                               ident[:, :])
                        ins.then_inc(S["crow_ps"], 1)

            def group(G, n):
                for s in range(n + 1):
                    T = G * GT + s
                    if s < n:
                        out_proj(T)
                    if s:
                        z_proj(T - 1, s - 1)
                    if s < n:
                        if s == 0:
                            pe.wait_ge(S["crow_ready"], after(G * NBLK))
                        turn_h(T, s)
                blocks(G, n)

            def conv_state(src, width, k):
                for q in range(4):
                    pe.wait_ge(S["cs_ready"], after(4 * k + q))
                    for i in range(4):
                        ins = pe.transpose(PT[0][0:width, i * P:(i + 1) * P], src(4 * q + i), ident[:, :])
                    ins.then_inc(S["cs_ps"], 1)

            pe.wait_ge(S["w2o_loaded"], after(16 * KD))
            pe.wait_ge(S["c2_loaded"], after(16 * 7))
            with pe.Fori(0, GROUPS) as G:
                group(G, GT)
            pe.wait_ge(S["tail_kept"], after(NBLK * GROUPS))
            pe.wait_ge(S["hT2_sb"], after(2 * NT))
            conv_state(lambda b: tails[:, b, :], 3, 0)
            pe.wait_ge(S["pre_loaded"], after(16))
            pe.wait_ge(S["cs_ready"], after(4))
            for b in range(NBLK):
                ins = pe.transpose(PT[1][:, b * 24:(b + 1) * 24], crw[:, b * P:(b + 1) * P], ident[0:24, 0:24])
            ins.then_inc(S["pre_ps"], 1)
            pe.wait_ge(S["pre_ready"], after(1))
            group(GROUPS, 1)
            pe.wait_ge(S["pre_kept"], after(NBLK))
            pe.wait_ge(S["hT2_sb"], after(2 * NT + 2))
            conv_state(lambda b: pre[:, b, :], DB * 3, 1)

        @block.scalar
        def _(act):
            def z_gate(T, G):
                for n in range(2):
                    act.wait_ge(S["z_ps"], after(3 * T + n + 1))
                    act.wait_ge(S["cv_ready"], after(G * NBLK))
                    act.wait_ge(S["z_free"], after(3 * T + n))
                    act.activation(cvt[:, 0:512], PA[n][:, :], ACT.Tanh, scale=0.5).then_inc(S["zt_ready"], 1)

            def blocks(G, n):
                N = n * P
                act.wait_ge(S["z_free"], after(3 * (G * GT + n)))
                for b in range(NBLK):
                    u = G * NBLK + b
                    act.wait_ge(S["blk_ps"], after(u + 1))
                    act.wait_ge(S["tail_kept"], after(u - 1) if b >= 2 else after(G * NBLK))
                    act.wait_ge(S["cvh_ready"], after(u - 1) if b >= 2 else after(G * NBLK))
                    act.copy(raw[:, b % 2, 3:3 + N], PB[b % 2][:, 0:N]).then_inc(S["raw_ready"], 1)
                    if b:
                        tanh_and_rows(u - 1, b - 1, N)
                tanh_and_rows(G * NBLK + NBLK - 1, NBLK - 1, N)

            def tanh_and_rows(u, b, N):
                act.wait_ge(S["cvh_ready"], after(u + 1))
                act.wait_ge(S["cv_ready"], after(u))
                act.activation(cvt[:, 0:N], cva[:, b % 2, 0:N], ACT.Tanh).then_inc(S["cvt_ready"], 1)

            def group(G, n):
                for s in range(n + 1):
                    T = G * GT + s
                    if s < n:
                        sub_front(T)
                    if s:
                        z_gate(T - 1, G)
                    if s < n:
                        sub_back(T, s)
                blocks(G, n)

            def sub_front(T):
                for u in range(2):
                    act.wait_ge(S["yT_ps"], after(2 * T + u + 1))
                    act.copy(yT[:, 4 * u:4 * u + 4, :].rearrange("p c t -> p (c t)"), PT[u][:, :])\
                       .then_inc(S["yT_sb"], 1)
                act.wait_ge(S["y1_ready"], after(2 * T + 2))
                act.wait_ge(S["hT2_ps"], after(2 * T))
                act.activation(hn[:, :], y1[:, :], ACT.Square, accum_out=ssum).then_inc(S["ss2_ready"], 1)
                act.wait_ge(S["ss2_ready"], after(T + 1))
                act.wait_ge(S["rstd2_ready"], after(T + 1))
                act.activation(hn[:, :], y1[:, :], ACT.Copy, scale=rstd).then_inc(S["hn2_ready"], 1)

            def sub_back(T, s):
                for u in range(2):
                    act.wait_ge(S["hT2_ps"], after(2 * T + u + 1))
                    for k in range(4):
                        c = 4 * u + k
                        ins = act.activation(hT[:, c, s * P:(s + 1) * P], PT[u][:, k * P:(k + 1) * P], ACT.Copy,
                                             scale=nw1[:, c:c + 1])
                    ins.then_inc(S["hT2_sb"], 1)

            act.wait_ge(S["c2_loaded"], after(16 * 7))
            with act.Fori(0, GROUPS) as G:
                group(G, GT)
            for q in range(4):
                act.wait_ge(S["cs_ps"], after(q + 1))
                act.copy(crw[0:3, q * 512:(q + 1) * 512], PT[0][0:3, :]).then_inc(S["cs_ready"], 1)
            group(GROUPS, 1)
            for q in range(4):
                act.wait_ge(S["cs_ps"], after(4 + q + 1))
                act.copy(crw[:, q * 512:(q + 1) * 512], PT[0][0:DB * 3, :]).then_inc(S["cs_ready"], 1)

        @block.vector
        def _(dve):
            link, fresh = link_in(dve, S["dve_link"])

            def residual(T):
                dve.wait_ge(S["x2_loaded"], after(16 * (T + 1)))
                for n in range(2):
                    dve.wait_ge(S["y1_ps"], after(2 * T + n + 1))
                    dve.wait_ge(S["y1_stored"], after(16 * T))
                    dve.wait_ge(S["hn2_ready"], after(T))
                    dve.tensor_tensor(y1[:, n * 512:(n + 1) * 512], xin[:, n * 512:(n + 1) * 512], PS[n][:, :],
                                      ALU.add).then_inc(S["y1_ready"], 1)

            def z_gate(T):
                for n in range(2):
                    dve.wait_ge(S["zt_ready"], after(2 * T + n + 1))
                    dve.wait_ge(S["zg_stored"], after(16 * (2 * T + n)))
                    dve.scalar_tensor_tensor(zg[:, :], cvt[:, 0:512], 1.0, PA[n][:, :], ALU.add, ALU.mult)\
                       .then_inc(S["z_free"], 1)
                    dve.wait_ge(S["z_free"], after(3 * T + n + 1))
                    dve.tensor_tensor(zg[:, :].rearrange("p (h d) -> p h d", d=P),
                                      zg[:, :].rearrange("p (h d) -> p h d", d=P),
                                      gn[:, :].unsqueeze(1).to_broadcast([P, 4, P]), ALU.mult)\
                       .then_inc(S["zg_ready"], 1)
                dve.wait_ge(S["z_ps"], after(3 * T + 3))
                dve.tensor_copy(ab_all[:, ds(T, 1), :], PA[0][:, 0:16].unsqueeze(1)).then_inc(S["z_free"], 1)

            def blocks(G, n, sample=False):
                N = n * P
                fresh()
                for b in range(NBLK):
                    u = G * NBLK + b
                    dve.wait_ge(S["raw_ready"], after(u + 1))
                    if b >= 2:
                        dve.wait_ge(S["crow_ps"], after(u - 1))
                    r = raw[:, b % 2, :]
                    a = cva[:, b % 2, 0:N]
                    if sample:
                        rv = r[:, 3:3 + SR].rearrange("p (b t) -> p b t", t=DT)
                        xv = sx[:, :].rearrange("p (b t) -> p b t", t=DT + 3)
                        dve.tensor_copy(xv[:, :, 0:3], pre[:, b, :].rearrange("p (b t) -> p b t", t=3))
                        link(dve.tensor_copy(xv[:, :, 3:7], rv))
                        av = cva[:, b % 2, 0:SR].rearrange("p (b t) -> p b t", t=DT)
                        link(dve.tensor_scalar(av, xv[:, :, 0:DT], cw[:, 0, b:b + 1], None, ALU.mult))
                        for k in range(1, CONV):
                            ins = dve.scalar_tensor_tensor(av, xv[:, :, k:k + DT], cw[:, k, b:b + 1], av, ALU.mult,
                                                           ALU.add)
                            if k < CONV - 1:
                                link(ins)
                        ins.then_inc(S["cvh_ready"], 1)
                        dve.tensor_copy(pre[:, b, :].rearrange("p (b t) -> p b t", t=3), xv[:, :, 4:7])\
                           .then_inc(S["pre_kept"], 1)
                        dve.wait_ge(S["pre_kept"], after(b + 1))
                        dve.sem_inc(S["tail_kept"], 1)
                    else:
                        link(dve.tensor_copy(r[:, 0:3], tails[:, b, :]))
                        link(dve.tensor_scalar(a, r[:, 0:N], cw[:, 0, b:b + 1], None, ALU.mult))
                        for k in range(1, CONV):
                            ins = dve.scalar_tensor_tensor(a, r[:, k:k + N], cw[:, k, b:b + 1], a, ALU.mult, ALU.add)
                            if k < CONV - 1:
                                link(ins)
                        ins.then_inc(S["cvh_ready"], 1)
                        dve.tensor_copy(tails[:, b, :], r[:, N:N + 3]).then_inc(S["tail_kept"], 1)
                    if b:
                        silu(u - 1, b - 1, N)
                    if b >= 3:
                        rows(G, u - 3, b - 3, N)
                silu(G * NBLK + NBLK - 1, NBLK - 1, N)
                for b in range(NBLK - 3, NBLK):
                    rows(G, G * NBLK + b, b, N)

            def silu(u, b, N):
                dve.wait_ge(S["cvt_ready"], after(u + 1))
                dve.scalar_tensor_tensor(cva[:, b % 2, 0:N], cvt[:, 0:N], 1.0, cva[:, b % 2, 0:N], ALU.add, ALU.mult)\
                   .then_inc(S["cv_ready"], 1)

            def rows(G, u, b, N):
                dve.wait_ge(S["crow_ps"], after(u + 1))
                before = (16 * GT * (GROUPS * NBLK // 2) + 16 * (b // 2)) if N == P else 16 * GT * (G * (NBLK // 2) + b // 2)
                dve.wait_ge(S["c_stored%d" % (b % 2)], after(before))
                dve.tensor_copy(crow[:, b % 2, 0:N], PA[b % 2][:, 0:N]).then_inc(S["crow_ready"], 1)

            def group(G, n, sample=False):
                for s in range(n + 1):
                    if s < n:
                        residual(G * GT + s)
                    if s:
                        z_gate(G * GT + s - 1)
                blocks(G, n, sample)

            dve.memset(nhalf[:, :], -0.5).then_inc(S["const2_ready"], 1)
            dve.memset(tails[:, :, :], 0.0).then_inc(S["const2_ready"], 1)
            dve.wait_ge(S["c2_loaded"], after(16 * 7))
            dve.tensor_scalar(cw[:, :, :], cw[:, :, :], 0.5, None, ALU.mult).then_inc(S["const2_ready"], 1)
            dve.tensor_scalar(gn[:, :], gn[:, :], 0.5, None, ALU.mult).then_inc(S["const2_ready"], 1)
            dve.memset(cva[:, :, :], 0.0).then_inc(S["const2_ready"], 1)
            dve.wait_ge(S["const2_ready"], after(5))
            with dve.Fori(0, GROUPS) as G:
                group(G, GT)
            dve.wait_ge(S["pre_ps"], after(1))
            dve.tensor_copy(pre[:, :, :].rearrange("p b t -> p (b t)"), PT[1][:, 0:NBLK * 24])\
               .then_inc(S["pre_ready"], 1)
            dve.wait_ge(S["pre_ready"], after(1))
            group(GROUPS, 1, True)

        @block.gpsimd
        def _(pool):
            link, fresh = link_in(pool, S["pool_link"])
            pool.wait_ge(S["const2_ready"], after(5))
            with pool.Fori(0, NSUB) as T:
                fresh()
                pool.wait_ge(S["ss2_ready"], after(T + 1))
                link()
                link(pool.tensor_scalar(rstd, ssum, 1.0 / D, EPS, ALU.mult, ALU.add))
                pool.tensor_tensor(rstd, rstd, nhalf[:, 0:1], ALU.pow).then_inc(S["rstd2_ready"], 1)


GH = 8
LEVELS = 7
SAMPLE_LEVELS = 2
QT_G, QT_BETA, QT_GC, QT_EGC, QT_EKT, QT_EGL = range(6)


def tri_constants(size):
    f = np.float32
    j, i = np.arange(P)[:, None], np.arange(P)[None]
    same = j // size == i // size
    tri = (same & (j <= i)).astype(f)
    strict = (same & (j < i)).astype(f)
    levels = [((i >> n) % 2 == 1) & ((j >> n) == (i >> n) - 1) & same for n in range(LEVELS)]
    return np.concatenate([tri, strict, same.astype(f)] + [m.astype(f) for m in levels], 1)


def layer1_delta(nc, io, S, ab_all):
    ctx = ExitStack()
    with ctx:
        def sb(name, shape, dt=FP):
            return ctx.enter_context(nc.sbuf_tensor(name, shape, dt))

        def ps(name):
            return ctx.enter_context(nc.psum_tensor(name, [P, 512], FP))

        def heads(name):
            return sb(name, [P, GH, P])

        w_co = sb("w_co", [P, KD, D])
        state = heads("state")
        tc = sb("tri_t", [P, 3 + LEVELS, P])
        tcs = sb("tris_t", [P, 3 + LEVELS, P])
        ident = sb("ident3", [P, P])
        fng = sb("fng", [P, D])
        alog = sb("alog", [P, GH])
        dtb = sb("dtb", [P, GH])
        q_all = sb("q_all", [P, NT + 1, 6, GH])
        cur = sb("cur", [P, 6, GH])
        begc = sb("begc", [P, GH])
        spa = sb("spa", [P, NT + 1, GH])
        spb = sb("spb", [P, NT + 1, GH])
        spc = sb("spc", [P, NT + 1, GH])
        nhalf = sb("nhalf3", [P, GH])
        qks = sb("qks", [P, GH])
        st = sb("stat3", [P, 4 * GH])
        ss8, rs8, os8, or8 = [st[:, k * GH:(k + 1) * GH] for k in range(4)]
        fst = sb("fst", [P, 2])
        cin = sb("cin", [P, CC])
        zgt = sb("zgt", [P, D])
        y1t = sb("y1t", [P, D])
        y2 = sb("y2", [P, D])
        yo = sb("yo", [P, D])
        sq = sb("sq3", [P, D])
        qkn, qkT, dec, dst, MT, QKD = [heads(n) for n in ("qkn", "qkT", "dec", "dst", "MT", "QKD")]
        ML = sb("ML", [P, 2, GH, P])
        X, XT, P1, bv, kt, R, vn, qs, o, oT = [heads(n) for n in
                                               ("X", "XT", "P1", "bv", "kt", "R", "vn", "qsd", "o", "oT")]
        PA = [ps("RA0"), ps("RA1")]
        PS = [ps("RS0"), ps("RS1")]
        PT = [ps("RT0"), ps("RT1")]
        PB = [ps("RB0"), ps("RB1")]
        sg = sb("sg", [P, DB, GH, P])
        qkm = sb("qkm", [P, DB, GH, SR])
        vnm = sb("vnm", [SR, 2, DB, P])
        bsel = sb("bsel_t", [P, 2 * DB])
        eglm = sb("eglm", [P, DB, GH])
        eglb = sb("eglb", [P, DB, GH])
        block = ctx.enter_context(nc.Block())

        def flat(x):
            return x[:, :, :].rearrange("p h d -> p (h d)")

        def half(x, g):
            return x[:, 4 * g:4 * g + 4, :].rearrange("p h d -> p (h d)")

        def quad(x, g):
            return x[:, 4 * g:4 * g + 4, :]

        def bank(x):
            return x[:, :].rearrange("p (h d) -> p h d", d=P)

        def col(v, n=P):
            return v.unsqueeze(2).to_broadcast([P, v.shape[1], n])

        def over(m, n):
            return m.unsqueeze(1).to_broadcast([P, n, P])

        @block.sync
        def _(sp):
            for c in range(KD):
                sp.dma_start(w_co[:, c, :], io["w_out_c"][c * P:(c + 1) * P, :]).then_inc(S["w3_loaded"], 16)
            for dst_, src in ((ident[:, :], io["ident"]), (tc[:, :, :].rearrange("p a b -> p (a b)"), io["tri"]),
                              (tcs[:, :, :].rearrange("p a b -> p (a b)"), io["tri_s"]),
                              (fng[:, :], io["final_norm"].partition_broadcast(P)),
                              (alog[:, :], io["a_log"].partition_broadcast(P)),
                              (dtb[:, :], io["dt_bias"].partition_broadcast(P)),
                              (qks[:, :], io["qk_scale"]), (bsel[:, :], io["bsel"])):
                sp.dma_start(dst_, src, allow_slow_non_contiguous=True).then_inc(S["c3_loaded"], 16)

            for b in range(DB):
                sp.dma_start(sg[:, b], io["state_gdn"][b].rearrange("h d e -> d h e")).then_inc(S["sg_loaded"], 16)

            def tile(t):
                sp.wait_ge(S["bv_ready"], after(t))
                sp.wait_ge(S["qkn_ready"], after(t))
                sp.wait_ge(S["qk_sq"], after(t))
                sp.dma_start(cin[:, :], io["c_all"][ds(t * P, P), :]).then_inc(S["cin_loaded"], 16)
                sp.wait_ge(S["og_ready"], after(t))
                sp.dma_start(zgt[:, :], io["zg_all"][ds(t * P, P), :]).then_inc(S["zg3_loaded"], 16)
                sp.wait_ge(S["y2_ready"], after(2 * t))
                sp.dma_start(y1t[:, :], io["y1_all"][ds(t * P, P), :]).then_inc(S["y13_loaded"], 16)

            def store(t):
                sp.wait_ge(S["yo_ready"], after(t + 1))
                sp.dma_start(io["y_all"][ds(t * P, P), :], yo[:, :]).then_inc(S["yo_stored"], 16)

            tile(0)
            with sp.Fori(0, NT) as t:
                tile(t + 1)
                store(t)
            sp.wait_ge(S["st_upd"], after(NT))
            sp.dma_start(io["gdn_prompt"].rearrange("h d e -> d h e"), state[:, :, :]).then_inc(S["st_stored"], 16)
            store(NT)
            for b in range(DB):
                sp.wait_ge(S["sg_upd"], after(16))
                sp.dma_start(io["gdn_sample"][b].rearrange("h d e -> d h e"), sg[:, b])\
                  .then_inc(S["st_stored"], 16)
            sp.wait_ge(S["yo_stored"], after(16 * (NT + 1)))
            sp.wait_ge(S["st_stored"], after(16 * (DB + 1)))

        def tile_masks(sample):
            return tcs if sample else tc

        @block.tensor
        def _(pe):
            def front(t, sample):
                m = tile_masks(sample)
                pe.wait_ge(S["cur_ready"], after(t + 1))
                pe.wait_ge(S["o_ready"], after(2 * t))
                for g in range(2):
                    for k in range(4):
                        ins = pe.matmul(PS[g][:, k * P:(k + 1) * P],
                                        cur[:, QT_G, 4 * g + k:4 * g + k + 1].to_broadcast([P, P]), m[:, 0, :],
                                        start=True, stop=True)
                    ins.then_inc(S["gcb_ps"], 1)
                pe.wait_ge(S["st_upd"], after(t))
                for g in range(2):
                    for k in range(4):
                        ins = pe.matmul(PT[g][:, k * P:(k + 1) * P],
                                        cur[:, QT_BETA, 4 * g + k:4 * g + k + 1].to_broadcast([P, P]), ident[:, :],
                                        start=True, stop=True)
                    ins.then_inc(S["bb_ps"], 1)
                pe.wait_ge(S["qkn_ready"], after(t + 1))
                pe.wait_ge(S["y2_ready"], after(2 * t))
                for g in range(2):
                    for k in range(4):
                        h = 4 * g + k
                        ins = pe.transpose(PA[g][:, k * P:(k + 1) * P], qkn[:, h, :], ident[:, :])
                    ins.then_inc(S["qkT_ps"], 1)
                pe.wait_ge(S["qkT_ready"], after(2 * t + 2))
                pe.wait_ge(S["oT_ready"], after(2 * t))
                for k in range(4):
                    ins = pe.matmul(PB[0][:, k * P:(k + 1) * P], qkT[:, 4 + k, :], qkT[:, 4 + k, :], start=True,
                                    stop=True)
                ins.then_inc(S["kk_ps"], 1)
                for k in range(4):
                    ins = pe.matmul(PB[1][:, k * P:(k + 1) * P], qkT[:, 4 + k, :], qkT[:, k, :], start=True,
                                    stop=True)
                ins.then_inc(S["qk_ps"], 1)

            def state_reads(t):
                pe.wait_ge(S["st_upd"], after(t))
                pe.wait_ge(S["MT_ready"], after(t + 1))
                pe.wait_ge(S["QKD_ready"], after(t + 1))
                for k in range(4):
                    ins = pe.matmul(PB[k // 2][:, (k % 2) * 256:(k % 2 + 1) * 256], qkT[:, 4 + k, :],
                                    state[:, 2 * k:2 * k + 2, :].rearrange("p h d -> p (h d)"), start=True,
                                    stop=True)
                ins.then_inc(S["ks_ps"], 1)

            def query_reads(t):
                pe.wait_ge(S["ks_read"], after(t + 1))
                for k in range(4):
                    ins = pe.matmul(PB[k // 2][:, (k % 2) * 256:(k % 2 + 1) * 256], qkT[:, k, :],
                                    state[:, 2 * k:2 * k + 2, :].rearrange("p h d -> p (h d)"), start=True,
                                    stop=True)
                ins.then_inc(S["qs_ps"], 1)

            def inverse(t, levels, after_level):
                pe.wait_ge(S["ML_ready"], after(LEVELS * t + 1))
                pe.wait_ge(S["qkT_ready"], after(2 * t + 2))
                for g in range(2):
                    for k in range(4):
                        ins = pe.transpose(PA[g][:, k * P:(k + 1) * P], ML[:, 0, 4 * g + k, :], ident[:, :])
                    ins.then_inc(S["x_ps"], 1)
                for n in range(1, levels):
                    pe.wait_ge(S["ML_ready"], after(LEVELS * t + n + 1))
                    for g in range(2):
                        pe.wait_ge(S["x_ready"], after(14 * t + 2 * n - 1 + g))
                        pe.wait_ge(S["p1_ready"], after(12 * t + max(2 * (n - 1) - 1 + g, 0)))
                        for k in range(4):
                            ins = pe.matmul(PA[g][:, k * P:(k + 1) * P], ML[:, n % 2, 4 * g + k, :],
                                            X[:, 4 * g + k, :], start=True, stop=True)
                        ins.then_inc(S["p1_ps"], 1)
                    after_level(n)
                    for g in range(2):
                        pe.wait_ge(S["p1_ready"], after(12 * t + 2 * (n - 1) + 1 + g))
                        for k in range(4):
                            h = 4 * g + k
                            pe.matmul(PT[g][:, k * P:(k + 1) * P], P1[:, h, :], XT[:, h, :], start=True, stop=True)
                            ins = pe.matmul(PS[g][:, k * P:(k + 1) * P], XT[:, h, :], P1[:, h, :], start=True,
                                            stop=True)
                        ins.then_inc(S["x_ps"], 1)

            def back(t, levels):
                pe.wait_ge(S["R_ready"], after(2 * t + 2))
                pe.wait_ge(S["x_ready"], after(14 * t + 2 * levels))
                for g in range(2):
                    for k in range(4):
                        h = 4 * g + k
                        ins = pe.matmul(PA[g][:, k * P:(k + 1) * P], XT[:, h, :], R[:, h, :], start=True, stop=True)
                    ins.then_inc(S["vn_ps"], 1)
                for g in range(2):
                    pe.wait_ge(S["vn_ready"], after(2 * t + g + 1))
                    for k in range(4):
                        h = 4 * g + k
                        ins = pe.matmul(PS[g][:, k * P:(k + 1) * P], QKD[:, h, :], vn[:, h, :], start=True,
                                        stop=True)
                    ins.then_inc(S["o_ps"], 1)

            def state_update(t):
                for g in range(2):
                    pe.wait_ge(S["kt_ready"], after(t + 1))
                    for k in range(4):
                        h = 4 * g + k
                        ins = pe.matmul(PT[g][:, k * P:(k + 1) * P], kt[:, h, :], vn[:, h, :], start=True, stop=True)
                    ins.then_inc(S["su_ps"], 1)

            def out(t):
                pe.wait_ge(S["og_ready"], after(t + 1))
                pe.wait_ge(S["qs_read"], after(t + 1))
                for g in range(2):
                    for k in range(4):
                        ins = pe.transpose(PB[g][:, k * P:(k + 1) * P], o[:, 4 * g + k, :], ident[:, :])
                    ins.then_inc(S["oT_ps"], 1)
                pe.wait_ge(S["oT_ready"], after(2 * t + 2))
                pe.wait_ge(S["vn_ready"], after(2 * t + 2))
                for n in range(2):
                    for c in range(KD):
                        ins = pe.matmul(PA[n][:, :], oT[:, c, :], w_co[:, c, n * 512:(n + 1) * 512], start=(c == 0),
                                        stop=(c == KD - 1))
                    ins.then_inc(S["y2_ps"], 1)

            pe.wait_ge(S["c3_loaded"], after(16 * 8))
            pe.wait_ge(S["const3_ready"], after(2))
            pe.wait_ge(S["g_ready"], after(1))
            for r, which in enumerate((0, 2)):
                pe.matmul(PA[r][:, 0:NT * GH], tc[:, which, :], spa[:, 0:NT, :].rearrange("p t h -> p (t h)"),
                          start=True, stop=True)
                pe.matmul(PA[r][:, NT * GH:(NT + 1) * GH], tcs[:, which, :], spa[:, NT, :], start=True, stop=True)\
                  .then_inc(S["gc_ps"], 1)
            pe.wait_ge(S["w3_loaded"], after(16 * KD))
            with pe.Fori(0, NT) as t:
                front(t, False)

                def between(n):
                    if n == 1:
                        state_reads(t)
                    if n == 2:
                        query_reads(t)

                inverse(t, LEVELS, between)
                back(t, LEVELS)
                state_update(t)
                out(t)
            front(NT, True)
            t = NT
            pe.wait_ge(S["sg_loaded"], after(16 * DB))
            pe.wait_ge(S["qkm_ready"], after(1))
            pe.wait_ge(S["MT_ready"], after(t + 1))
            pe.wait_ge(S["QKD_ready"], after(t + 1))

            def sample_reads(first):
                for k in range(4):
                    for b in range(DB):
                        ins = pe.matmul(PB[k // 2][0:SR, (k % 2) * 256:(k % 2 + 1) * 256], qkm[:, b, first + k, :],
                                        sg[:, b, 2 * k:2 * k + 2, :].rearrange("p h d -> p (h d)"), start=(b == 0),
                                        stop=(b == DB - 1))
                return ins

            sample_reads(4).then_inc(S["ks_ps"], 1)
            pe.wait_ge(S["ks_read"], after(t + 1))
            sample_reads(0).then_inc(S["qs_ps"], 1)
            inverse(t, SAMPLE_LEVELS, lambda n: None)
            back(t, SAMPLE_LEVELS)
            pe.wait_ge(S["eglm_ready"], after(1))
            pe.matmul(PT[0][:, 0:DB * GH], tc[:, 2, :], eglm[:, :, :].rearrange("p b h -> p (b h)"), start=True,
                      stop=True).then_inc(S["egl_ps"], 1)
            pe.wait_ge(S["egl_read"], after(1))
            pe.wait_ge(S["kt_ready"], after(t + 1))
            for h in range(GH):
                pe.wait_ge(S["vnm_ready"], after(h + 1))
                if h:
                    pe.wait_ge(S["sg_upd"], after(2 * h))
                for g in range(2):
                    pe.matmul(PT[g][:, :], kt[0:SR, h, :], vnm[:, h % 2, 4 * g:4 * g + 4, :]
                              .rearrange("p b d -> p (b d)"), start=True, stop=True).then_inc(S["sgu_ps"], 1)
            out(t)

        @block.scalar
        def _(act):
            def front(t):
                act.wait_ge(S["cin_loaded"], after(16 * (t + 1)))
                act.wait_ge(S["fs_ready"], after(t))
                act.activation(sq[:, :], cin[:, 0:D], ACT.Square).then_inc(S["qk_sq"], 1)
                for g in range(2):
                    act.wait_ge(S["qkT_ps"], after(2 * t + g + 1))
                    act.copy(half(qkT, g), PA[g][:, :]).then_inc(S["qkT_ready"], 1)
                act.wait_ge(S["dif_ready"], after(t + 1))
                act.activation(flat(dec), flat(dec), ACT.Exp).then_inc(S["dec_ready"], 1)

            def inverse(t, levels):
                for n in range(1, levels):
                    for g in range(2):
                        act.wait_ge(S["p1_ps"], after(12 * t + 2 * (n - 1) + g + 1))
                        act.copy(half(P1, g), PA[g][:, :]).then_inc(S["p1_ready"], 1)

            def back(t):
                for g in range(2):
                    act.wait_ge(S["vn_ps"], after(2 * t + g + 1))
                    act.copy(half(vn, g), PA[g][:, :]).then_inc(S["vn_ready"], 1)
                act.wait_ge(S["o_ready"], after(2 * t + 2))
                act.activation(sq[:, :], flat(o), ACT.Square).then_inc(S["o_sq"], 1)
                for g in range(2):
                    act.wait_ge(S["oT_ps"], after(2 * t + g + 1))
                    act.copy(half(oT, g), PB[g][:, :]).then_inc(S["oT_ready"], 1)
                act.wait_ge(S["y2_ready"], after(2 * t + 2))
                act.wait_ge(S["os_ready"], after(t + 1))
                act.activation(sq[:, :], y2[:, :], ACT.Square, accum_out=fst[:, 0:1]).then_inc(S["fs_ready"], 1)

            act.wait_ge(S["c3_loaded"], after(16 * 8))
            act.activation(alog[:, :], alog[:, :], ACT.Exp).then_inc(S["pre_a"], 1)
            act.wait_ge(S["pre_d"], after(2))
            act.activation(spb[:, :, :], spb[:, :, :], ACT.Exp, scale=-1.0).then_inc(S["pre_a"], 1)
            act.activation(q_all[:, :, QT_BETA, :], ab_all[:, :, GH:2 * GH], ACT.Tanh, scale=0.5)\
               .then_inc(S["pre_a"], 1)
            act.wait_ge(S["pre_a"], after(3))
            act.activation(spb[:, :, :], spb[:, :, :], ACT.Ln, bias=1.0).then_inc(S["pre_a"], 1)
            act.wait_ge(S["pre_d"], after(3))
            for r, k in enumerate((QT_EGC, QT_EKT, QT_EGL)):
                ins = act.activation(q_all[:, :, k, :], (spa, spb, spc)[r][:, :, :], ACT.Exp)
            ins.then_inc(S["pre_a"], 1)
            with act.Fori(0, NT) as t:
                front(t)
                inverse(t, LEVELS)
                back(t)
            front(NT)
            inverse(NT, SAMPLE_LEVELS)
            back(NT)

        @block.vector
        def _(dve):
            link, fresh = link_in(dve, S["dve_link"])

            def front(t, sample):
                m = tile_masks(sample)
                dve.wait_ge(S["R_ready"], after(2 * t))
                dve.tensor_copy(cur[:, :, :].unsqueeze(1), q_all[:, ds(t, 1), :, :]).then_inc(S["cur_ready"], 1)
                dve.wait_ge(S["cur_ready"], after(t + 1))
                link(dve.tensor_tensor(begc[:, :], cur[:, QT_BETA, :], cur[:, QT_EGC, :], ALU.mult))
                dve.wait_ge(S["qk_sq"], after(t + 1))
                dve.tensor_reduce(ss8, sq[:, :].rearrange("p (h d) -> p h d", d=P), AX, ALU.add)\
                   .then_inc(S["qk_ss"], 1)
                for g in range(2):
                    dve.wait_ge(S["gcb_ps"], after(2 * t + g + 1))
                    for k in range(4):
                        h = 4 * g + k
                        ins = dve.tensor_scalar(dec[:, h, :], PS[g][:, k * P:(k + 1) * P],
                                                cur[:, QT_GC, h:h + 1], 0.0, ALU.subtract, ALU.min)
                ins.then_inc(S["dif_ready"], 1)
                dve.wait_ge(S["qk_rs"], after(t + 1))
                dve.tensor_tensor(qkn[:, :, :], cin[:, 0:D].rearrange("p (h d) -> p h d", d=P), col(rs8),
                                  ALU.mult).then_inc(S["qkn_ready"], 1)
                dve.wait_ge(S["dec_ready"], after(t + 1))
                link(dve.tensor_tensor(dst[:, :, :], dec[:, :, :], over(m[:, 1, :], GH), ALU.mult))
                link(dve.tensor_tensor(dec[:, :, :], dec[:, :, :], over(m[:, 0, :], GH), ALU.mult))
                dve.wait_ge(S["kk_ps"], after(t + 1))
                kk = PB[0][:, :].rearrange("p (q d) -> p q d", d=P).unsqueeze(2).to_broadcast([P, 4, 2, P])
                link(dve.tensor_tensor(MT[:, :, :].rearrange("p (q r) d -> p q r d", r=2), kk,
                                       dst[:, :, :].rearrange("p (q r) d -> p q r d", r=2), ALU.mult))
                dve.wait_ge(S["bb_ps"], after(2 * t + 2))
                for g in range(2):
                    ins = dve.tensor_tensor(half(MT, g), half(MT, g), PT[g][:, :], ALU.mult)
                ins.then_inc(S["MT_ready"], 1)
                dve.wait_ge(S["qk_ps"], after(t + 1))
                qk = PB[1][:, :].rearrange("p (q d) -> p q d", d=P).unsqueeze(2).to_broadcast([P, 4, 2, P])
                dve.tensor_tensor(QKD[:, :, :].rearrange("p (q r) d -> p q r d", r=2), qk,
                                  dec[:, :, :].rearrange("p (q r) d -> p q r d", r=2), ALU.mult)\
                   .then_inc(S["QKD_ready"], 1)

            def level_0(t):
                dve.wait_ge(S["ML_ready"], after(LEVELS * t + 1))
                link(dve.tensor_tensor(XT[:, :, :], over(ident[:, :], GH), ML[:, 0], ALU.subtract))
                for g in range(2):
                    dve.wait_ge(S["x_ps"], after(14 * t + g + 1))
                    dve.tensor_tensor(quad(X, g), over(ident[:, :], 4), bank(PA[g]), ALU.subtract)\
                       .then_inc(S["x_ready"], 1)

            def level(t, n):
                for g in range(2):
                    dve.wait_ge(S["x_ps"], after(14 * t + 2 * n + g + 1))
                    dve.wait_ge(S["x_ready"], after(14 * t + 2 * (n - 1) + g + 1))
                    dve.tensor_tensor(half(XT, g), half(XT, g), PT[g][:, :], ALU.subtract)
                    dve.tensor_tensor(half(X, g), half(X, g), PS[g][:, :], ALU.subtract).then_inc(S["x_ready"], 1)

            def key_reads(t):
                dve.wait_ge(S["ks_ps"], after(t + 1))
                for g in range(2):
                    ins = dve.tensor_tensor(quad(R, g), bank(PB[g]), col(begc[:, 4 * g:4 * g + 4]), ALU.mult)
                ins.then_inc(S["ks_read"], 1)
                dve.wait_ge(S["ks_read"], after(t + 1))
                dve.wait_ge(S["bv_ready"], after(t + 1))
                for g in range(2):
                    dve.tensor_tensor(half(R, g), half(bv, g), half(R, g), ALU.subtract).then_inc(S["R_ready"], 1)

            def query_reads(t):
                dve.wait_ge(S["qs_ps"], after(t + 1))
                for g in range(2):
                    ins = dve.tensor_tensor(quad(qs, g), bank(PB[g]), col(cur[:, QT_EGC, 4 * g:4 * g + 4]), ALU.mult)
                ins.then_inc(S["qs_read"], 1)

            def back(t):
                dve.wait_ge(S["qs_read"], after(t + 1))
                for g in range(2):
                    dve.wait_ge(S["o_ps"], after(2 * t + g + 1))
                    dve.tensor_tensor(half(o, g), half(qs, g), PS[g][:, :], ALU.add).then_inc(S["o_ready"], 1)

            def state_update(t):
                for g in range(2):
                    dve.wait_ge(S["su_ps"], after(2 * t + g + 1))
                    for k in range(4):
                        h = 4 * g + k
                        ins = dve.scalar_tensor_tensor(state[:, h, :], state[:, h, :], cur[:, QT_EGL, h:h + 1],
                                                       PT[g][:, k * P:(k + 1) * P], ALU.mult, ALU.add)
                ins.then_inc(S["st_upd"], 1)

            def out(t):
                dve.wait_ge(S["o_sq"], after(t + 1))
                dve.tensor_reduce(os8, sq[:, :].rearrange("p (h d) -> p h d", d=P), AX, ALU.add)\
                   .then_inc(S["os_ready"], 1)
                dve.wait_ge(S["or_ready"], after(t + 1))
                link(dve.tensor_tensor(o[:, :, :], o[:, :, :], col(or8), ALU.mult))
                dve.wait_ge(S["zg3_loaded"], after(16 * (t + 1)))
                dve.tensor_tensor(flat(o), flat(o), zgt[:, :], ALU.mult).then_inc(S["og_ready"], 1)
                dve.wait_ge(S["y13_loaded"], after(16 * (t + 1)))
                for n in range(2):
                    dve.wait_ge(S["y2_ps"], after(2 * t + n + 1))
                    dve.tensor_tensor(y2[:, n * 512:(n + 1) * 512], y1t[:, n * 512:(n + 1) * 512], PA[n][:, :],
                                      ALU.add).then_inc(S["y2_ready"], 1)
                dve.wait_ge(S["fr_ready"], after(t + 1))
                dve.wait_ge(S["yo_stored"], after(16 * t))
                dve.scalar_tensor_tensor(yo[:, :], y2[:, :], fst[:, 1:2], fng[:, :], ALU.mult, ALU.mult)\
                   .then_inc(S["yo_ready"], 1)

            dve.memset(nhalf[:, :], -0.5).then_inc(S["const3_ready"], 1)
            dve.memset(state[:, :, :], 0.0).then_inc(S["const3_ready"], 1)
            dve.wait_ge(S["const3_ready"], after(2))
            dve.wait_ge(S["c3_loaded"], after(16 * 8))
            dt_b = dtb[:, :].unsqueeze(1).to_broadcast([P, NT + 1, GH])
            dve.tensor_tensor(spa[:, :, :], ab_all[:, :, 0:GH], dt_b, ALU.add).then_inc(S["pre_d"], 1)
            dve.wait_ge(S["pre_d"], after(1))
            dve.scalar_tensor_tensor(spb[:, :, :], spa[:, :, :], -1.0, spa[:, :, :], ALU.mult, ALU.max).then_inc(S["pre_d"], 1)
            dve.wait_ge(S["pre_a"], after(4))
            link(dve.scalar_tensor_tensor(spa[:, :, :], spa[:, :, :], 0.0, spb[:, :, :], ALU.max, ALU.add))
            link(dve.tensor_scalar(alog[:, :], alog[:, :], -1.0, None, ALU.mult))
            dve.tensor_tensor(spa[:, :, :], spa[:, :, :], alog[:, :].unsqueeze(1).to_broadcast([P, NT + 1, GH]),
                              ALU.mult).then_inc(S["g_ready"], 1)
            dve.wait_ge(S["g_ready"], after(1))
            dve.tensor_copy(q_all[:, :, QT_G, :], spa[:, :, :])
            link(dve.tensor_scalar(q_all[:, :, QT_BETA, :], q_all[:, :, QT_BETA, :], 0.5, 0.5, ALU.mult, ALU.add))
            dve.wait_ge(S["gc_ps"], after(2))
            gc = PA[0][:, 0:(NT + 1) * GH].rearrange("p (t h) -> p t h", h=GH)
            gl = PA[1][:, 0:(NT + 1) * GH].rearrange("p (t h) -> p t h", h=GH)
            dve.tensor_copy(q_all[:, :, QT_GC, :], gc)
            link(dve.tensor_copy(spa[:, :, :], gc))
            link(dve.tensor_tensor(spb[:, :, :], gl, spa[:, :, :], ALU.subtract))
            dve.tensor_copy(spc[:, :, :], gl).then_inc(S["pre_d"], 1)
            dve.wait_ge(S["pre_a"], after(5))
            with dve.Fori(0, NT) as t:
                fresh()
                front(t, False)
                level_0(t)
                for n in range(1, LEVELS):
                    if n == 2:
                        key_reads(t)
                    if n == 3:
                        query_reads(t)
                    level(t, n)
                back(t)
                state_update(t)
                out(t)
            t = NT
            fresh()
            front(t, True)
            dve.wait_ge(S["qkT_ready"], after(2 * t + 2))
            dve.wait_ge(S["qkm_zero"], after(1))
            for b in range(DB):
                ins = dve.tensor_copy(qkm[:, b, :, b * DT:(b + 1) * DT], qkT[:, :, b * DT:(b + 1) * DT])
            ins.then_inc(S["qkm_ready"], 1)
            dve.tensor_tensor(eglm[:, :, :], cur[:, QT_EGL:QT_EGL + 1, :].to_broadcast([P, DB, GH]),
                              bsel[:, DB:2 * DB].unsqueeze(2).to_broadcast([P, DB, GH]), ALU.mult)\
               .then_inc(S["eglm_ready"], 1)
            key_reads(t)
            query_reads(t)
            level_0(t)
            level(t, 1)
            back(t)
            dve.wait_ge(S["egl_ps"], after(1))
            dve.tensor_copy(eglb[:, :, :].rearrange("p b h -> p (b h)"), PT[0][:, 0:DB * GH])\
               .then_inc(S["egl_read"], 1)
            dve.wait_ge(S["egl_read"], after(1))
            dve.wait_ge(S["qs_ps"], after(t + 1))
            sgf = sg[:, :, :, :].rearrange("p b h d -> p (b h) d")
            link(dve.tensor_tensor(sgf, sgf, eglb[:, :, :].rearrange("p b h -> p (b h)").unsqueeze(2)
                                   .to_broadcast([P, DB * GH, P]), ALU.mult))
            for h in range(GH):
                if h >= 2:
                    dve.wait_ge(S["sgu_ps"], after(2 * (h - 1)))
                dve.tensor_tensor(vnm[:, h % 2], vn[0:SR, h:h + 1, :].to_broadcast([SR, DB, P]),
                                  bsel[0:SR, 0:DB].unsqueeze(2).to_broadcast([SR, DB, P]), ALU.mult)\
                   .then_inc(S["vnm_ready"], 1)
                for g in range(2):
                    dve.wait_ge(S["sgu_ps"], after(2 * h + g + 1))
                    dve.tensor_tensor(sg[:, 4 * g:4 * g + 4, h, :], sg[:, 4 * g:4 * g + 4, h, :], bank(PT[g]), ALU.add)\
                       .then_inc(S["sg_upd"], 1)
            out(t)

        @block.gpsimd
        def _(pool):
            link, fresh = link_in(pool, S["pool_link"])

            def tile(t, sample):
                m = tile_masks(sample)
                fresh()
                if sample:
                    pool.memset(qkm[:, :, :, :], 0.0).then_inc(S["qkm_zero"], 1)
                pool.wait_ge(S["qk_ss"], after(t + 1))
                link()
                link(pool.tensor_scalar(rs8, ss8, EPS, None, ALU.add))
                link(pool.tensor_tensor(rs8, rs8, nhalf[:, :], ALU.pow))
                pool.tensor_tensor(rs8, rs8, qks[:, :], ALU.mult).then_inc(S["qk_rs"], 1)
                pool.wait_ge(S["cur_ready"], after(t + 1))
                pool.tensor_tensor(bv[:, :, :], cin[:, D:2 * D].rearrange("p (h d) -> p h d", d=P),
                                   col(cur[:, QT_BETA, :]), ALU.mult).then_inc(S["bv_ready"], 1)
                for n in range(SAMPLE_LEVELS if sample else LEVELS):
                    if n == 0:
                        pool.wait_ge(S["MT_ready"], after(t + 1))
                        pool.wait_ge(S["x_ready"], after(14 * t))
                    elif n >= 2:
                        pool.wait_ge(S["x_ready"], after(14 * t + 2 * (n - 1)))
                    pool.tensor_tensor(ML[:, n % 2], MT[:, :, :], over(m[:, 3 + n, :], GH), ALU.mult)\
                        .then_inc(S["ML_ready"], 1)
                    if n == 0:
                        pool.wait_ge(S["qkn_ready"], after(t + 1))
                        pool.wait_ge(S["su_ps"], after(2 * t))
                        for g in range(2):
                            ins = pool.tensor_tensor(
                                quad(kt, g).rearrange("p (q r) d -> p q r d", r=2),
                                qkn[:, 4 + 2 * g:6 + 2 * g, :].unsqueeze(2).to_broadcast([P, 2, 2, P]),
                                cur[:, QT_EKT, 4 * g:4 * g + 4].rearrange("p (q r) -> p q r", r=2).unsqueeze(3)
                                .to_broadcast([P, 2, 2, P]), ALU.mult)
                        ins.then_inc(S["kt_ready"], 1)
                pool.wait_ge(S["os_ready"], after(t + 1))
                link()
                link(pool.tensor_scalar(or8, os8, 1.0 / P, EPS, ALU.mult, ALU.add))
                pool.tensor_tensor(or8, or8, nhalf[:, :], ALU.pow).then_inc(S["or_ready"], 1)
                pool.wait_ge(S["fs_ready"], after(t + 1))
                link()
                link(pool.tensor_scalar(fst[:, 1:2], fst[:, 0:1], 1.0 / D, EPS, ALU.mult, ALU.add))
                pool.tensor_tensor(fst[:, 1:2], fst[:, 1:2], nhalf[:, 0:1], ALU.pow).then_inc(S["fr_ready"], 1)

            pool.wait_ge(S["const3_ready"], after(1))
            pool.wait_ge(S["c3_loaded"], after(16 * 8))
            with pool.Fori(0, NT) as t:
                tile(t, False)
            tile(NT, True)


def hybrid_step(nc, io):
    ctx = ExitStack()
    with ctx:
        most = max(len(n.split()) for n in (LAYER0_SIGNALS, SAMPLES_SIGNALS, CONV_SIGNALS, DELTA_SIGNALS))
        pool = [ctx.enter_context(nc.semaphore(f"signal{k}")) for k in range(most)]
        links = {n: ctx.enter_context(nc.semaphore(n)) for n in LINKS.split()}
        ab_all = ctx.enter_context(nc.sbuf_tensor("ab_all", [P, NT + 1, 16], FP))

        def signals(names):
            given = dict(zip(names.split(), pool))
            with nc.Block() as block:
                @block.sync
                def _(sp):
                    for s in given.values():
                        sp.sem_clear(s)
                        sp.sem_inc(s, START)
            return given | links

        layer0_mixers(nc, io, signals(LAYER0_SIGNALS))
        layer0_samples(nc, io, signals(SAMPLES_SIGNALS))
        layer0_out_and_conv(nc, io, signals(CONV_SIGNALS), ab_all)
        layer1_delta(nc, io, signals(DELTA_SIGNALS), ab_all)


def kernel(**inputs):
    import concourse.bacc as _bacc
    from concourse.bass_utils import run_bass_kernel_spmd as _run

    nc = _bacc.Bacc("TRN2", target_bir_lowering=False, num_devices=1)
    inp = {k: np.ascontiguousarray(v) for k, v in inputs.items()}
    f = np.float32
    pad = np.zeros((ROWS - SEQ - SR, D), f)
    arrays = {
        "x_all": np.concatenate([inp["x_prompt"][0], inp["x_sample"].reshape(SR, D), pad]),
        "w_in_ab": inp["w_in_ab"][0], "norm_w": inp["norm_w"], "gn_ret": inp["gn_ret"],
        "w_out_ab": inp["w_out_ab"][0], "w_in_c": inp["w_in_c"][0], "w_out_c": inp["w_out_c"][0],
        "conv_w": inp["conv_w"][0], "gdn_norm": inp["gdn_norm"], "final_norm": inp["final_norm"][None],
        "state_conv": inp["state_conv"][0].reshape(DB * 3, CC),
        "a_log": inp["a_log"], "dt_bias": inp["dt_bias"],
        "state_ret": inp["state_ret"][0], "state_gdn": inp["state_gdn"][0],
        "cache_k": inp["cache_k"][0].reshape(-1, PAGE, 128), "cache_v": inp["cache_v"][0].reshape(-1, PAGE, 128),
        "cache_kidx": inp["cache_kidx"][0], "page_table": inp["page_table"].reshape(1, -1).astype(np.int32),
    }
    arrays.update(constants())
    p = np.arange(P)
    arrays["tri"], arrays["tri_s"] = tri_constants(P), tri_constants(DT)
    arrays["qk_scale"] = np.tile(np.where(np.arange(GH) < 4, P ** -0.5, 1.0), (P, 1)).astype(f)
    batch = p[:, None] // DT == np.arange(DB)[None]
    arrays["bsel"] = np.concatenate([batch, batch & (p[:, None] % DT == 0)], 1).astype(f)
    lg = np.log(1.0 - 2.0 ** (-5.0 - np.arange(RH)))
    same = p[:, None] // DT == p[None] // DT
    dif = p[None, :] - p[:, None]
    rm = np.where((same & (dif >= 0))[:, None, :], np.exp(dif[:, None, :] * lg[None, :, None]), 0.0) * HD ** -0.5
    arrays["rmask_s"] = rm[:, [0, 2, 1, 3]].reshape(P, RH * P).astype(f)
    head = 2 * np.arange(2)[None] + (p[:, None] >= HD)
    tok = np.arange(SR)
    own = tok[None] // DT == np.arange(DB)[:, None]
    qd = np.exp((tok % DT + 1.0)[None, None] * lg[head][:, :, None])
    arrays["qdec_s"] = (qd[:, :, None] * own[None, None]).reshape(P, -1).astype(f)
    arrays["kdec_s"] = (np.exp((DT - 1.0 - p % DT)[:, None] * lg[None]) * HD ** -0.5).astype(f)
    arrays["cdec_s"] = np.tile(np.exp(DT * lg), (P, 1)).astype(f)
    pair = np.arange(HB)[None, :, None] + HB * (p[:, None, None] >= HD)
    arrays["hm"] = (tok[None, None] // DT == pair).reshape(P, -1).astype(f)
    arrays["rep"] = (p[:, None] % SR == tok[None]).astype(f)
    arrays["rep4"] = ((p[:, None] == p[None] % SR)).astype(f)
    arrays["tmask"] = np.where(np.arange(DT)[None] <= tok[:, None] % DT, 0.0, -BIG).astype(f)
    arrays["dsel"] = ((p[:, None] % SR) // DT == np.arange(DB)[None]).astype(f)
    io = {}
    for name, a in arrays.items():
        io[name] = nc.dram_tensor(f"in_{name}", a.shape, mybir.dt.from_np(a.dtype), kind="ExternalInput").ap()
    for name, shape in OUTS.items():
        io[name] = nc.dram_tensor(f"out_{name}", shape, FP, kind="ExternalOutput").ap()
    hybrid_step(nc, io)
    r = _run(nc, [{f"in_{k}": v for k, v in arrays.items()}], core_ids=[0])
    o = {n: r.results[0][f"out_{n}"] for n in OUTS}
    k, v, ik = o["k_all"], o["v_all"], o["ik_all"]
    return (o["y_all"][None, :SEQ], o["y_all"][SEQ:SEQ + SR].reshape(DB, DT, D),
            k[:SEQ].reshape(1, 1, SEQ, 2, HD), v[:SEQ].reshape(1, 1, SEQ, 2, HD), ik[:SEQ].reshape(1, 1, SEQ, HD),
            k[SEQ:SEQ + SR].reshape(1, DB, DT, 2, HD), v[SEQ:SEQ + SR].reshape(1, DB, DT, 2, HD),
            ik[SEQ:SEQ + SR].reshape(1, DB, DT, HD),
            o["ret_prompt"][None, None], o["ret_sample"][None], o["gdn_prompt"][None, None], o["gdn_sample"][None],
            o["conv_prompt"][None, None], o["conv_sample"].reshape(1, DB, 3, CC))
```

```python
import concourse.bass as bass
from concourse import mybir
from contextlib import ExitStack
import numpy as np

FP = mybir.dt.float32
BF = mybir.dt.bfloat16
I32 = mybir.dt.int32
ALU = mybir.AluOpType
ACT = mybir.ActivationFunctionType
AX = mybir.AxisListType.X
ds = bass.ds

P = 128
D = 1024
KD = D // P
SEQ, DB, DT = 2048, 8, 4
NT = SEQ // P
ROWS = (NT + 1) * P
SR = DB * DT
PAST, PAGE = 2048, 128
NPG = PAST // PAGE
TOPK = 256
EPS = 1e-6
BIG = 1e30
AH, HD = 8, 64
RH, RV = 4, 128
ABW = 3140
C_QA, C_KA, C_VA, C_IQ, C_IK, C_IW, C_ZA = 0, 512, 640, 768, 1024, 1088, 1092
C_QB, C_KB, C_VB, C_ZB = 1604, 1860, 2116, 2628
A_CUTS = [(0, 512), (512, 1024), (1024, 1092)]
B_CUTS = [(1092, 1604), (1604, 2116), (2116, 2628), (2628, 3140)]
AW, NB = 1092, len(B_CUTS)
NHEADS17 = 17
GROUPS = 4
GT = NT // GROUPS
CH = 512
STEPS = 24
CC, CIN = 2048, 3088


def units_before(g):
    return sum(GT * (k + 1) for k in range(g))


def constants():
    f = np.float32
    out = {}
    out["ident"] = np.eye(P, dtype=f)
    pos = np.concatenate([np.arange(SEQ), np.tile(PAST + np.arange(DT), DB), np.zeros(ROWS - SEQ - SR)]).astype(f)
    half = HD // 4 // 2
    inv = (1.0 / (f(500000.0) ** (np.arange(half, dtype=f) / half))).astype(f)
    ang = (pos[:, None] * inv).astype(f)
    c, s = np.cos(ang).astype(f), np.sin(ang).astype(f)
    cc = np.tile(np.concatenate([c, c], 1)[:, None], (1, NHEADS17, 1))
    ss = np.tile(np.concatenate([-s, s], 1)[:, None], (1, NHEADS17, 1))
    cc[:, 10:12] = 1.0
    ss[:, 10:12] = 0.0
    out["ropea"] = np.stack([cc, ss], 1).reshape(ROWS, -1).astype(f)
    half = 32
    inv = (1.0 / (f(10000.0) ** (np.arange(half, dtype=f) / half))).astype(f)
    ang = (pos[:, None] * inv).astype(f)
    c, s = np.cos(ang).astype(f), np.sin(ang).astype(f)
    out["ropeb"] = np.concatenate([c, c, -s, s], 1).astype(f)
    p = np.arange(P)
    caus = np.where(np.arange(CH)[None, None] <= np.arange(GT)[None, :, None] * P + p[:, None, None], 0.0, -BIG)
    out["caus"] = caus.reshape(P, GT * CH).astype(f)
    lg = np.log(1.0 - 2.0 ** (-5.0 - np.arange(RH)))
    dif = p[None, :] - p[:, None]
    rm = np.where(dif[:, None, :] >= 0, np.exp(dif[:, None, :] * lg[None, :, None]), 0.0) * HD ** -0.5
    rm = rm[:, [0, 2, 1, 3]]
    out["rmask"] = rm.reshape(P, RH * P).astype(f)
    head = 2 * np.arange(2)[None] + (p[:, None] >= 64)
    out["qdec"] = np.exp((p[None, None] + 1.0) * lg[head][:, :, None]).reshape(P, 2 * P).astype(f)
    out["kdec"] = (np.exp((P - 1.0 - p)[:, None] * lg[None]) * HD ** -0.5).astype(f)
    out["cdec"] = np.tile(np.exp(P * lg), (P, 1)).astype(f)
    out["pow2"] = np.tile(2.0 ** -(1.0 + np.arange(STEPS + 1)), (P, 1)).astype(f)
    return out


START = 1


def after(n):
    return n + START


def link_in(eng, sem):
    n = [0]

    def link(ins=None):
        n[0] += 1
        if ins is None:
            eng.sem_inc(sem, 1)
        else:
            ins.then_inc(sem, 1)
        eng.wait_ge(sem, n[0])

    def fresh():
        eng.sem_clear(sem)
        n[0] = 0

    fresh()
    return link, fresh


def turn_half(pe, out, src, ident, half):
    if half:
        return pe.matmul(out, src, ident, start=True, stop=True)
    return pe.transpose(out, src, ident)


def layer0_project(nc, io, S, w_b):
    ctx = ExitStack()
    with ctx:
        def sb(name, shape, dt=FP):
            return ctx.enter_context(nc.sbuf_tensor(name, shape, dt))

        w_a = sb("w_a", [P, KD, AW])
        x = sb("x_rows", [P, 2, D])
        hT = sb("hT", [P, 2, KD, P])
        junk = sb("squares", [P, D])
        pr = sb("pr_out", [P, 2, AW])
        ident = sb("ident0", [P, P])
        nw0 = sb("nw0", [P, KD])
        ssum, rstd, nhalf = sb("ssum0", [P, 2]), sb("rstd0", [P, 2]), sb("nhalf0", [P, 1])
        PT = [ctx.enter_context(nc.psum_tensor("P0T%d" % k, [P, 512], FP)) for k in range(2)]
        PA = [ctx.enter_context(nc.psum_tensor("P0A%d" % k, [P, 512], FP)) for k in range(4)]
        block = ctx.enter_context(nc.Block())
        NU, PAIRS = len(A_CUTS), NT // 2 - 1

        @block.sync
        def _(sp):
            sp.dma_start(x[:, 0, :], io["x_all"][0:P, :]).then_inc(S["x0_loaded0"], 16)
            sp.dma_start(x[:, 1, :], io["x_all"][P:2 * P, :]).then_inc(S["x0_loaded1"], 16)
            sp.dma_start(ident[:, :], io["ident"]).then_inc(S["c0_loaded"], 16)
            sp.dma_start(nw0[:, :], io["norm_w"][0:1, :].rearrange("a (c p) -> p (a c)", p=P),
                         allow_slow_non_contiguous=True).then_inc(S["c0_loaded"], 16)
            for n, (a, b) in enumerate(A_CUTS):
                for c in range(KD):
                    sp.dma_start(w_a[:, c, a:b], io["w_in_ab"][c * P:(c + 1) * P, a:b]).then_inc(S["w0_loaded%d" % n], 16)
            for c in range(KD):
                sp.dma_start(w_b[:, c, :], io["w_in_ab"][c * P:(c + 1) * P, AW:ABW]).then_inc(S["wb_loaded"], 16)

            def tile(t, s, ahead):
                if ahead:
                    sp.wait_ge(S["xT_ps"], after(2 * (t + 1)))
                    sp.dma_start(x[:, s, :], io["x_all"][ds((t + 2) * P, P), :]).then_inc(S["x0_loaded%d" % s], 16)
                sp.wait_ge(S["hT_sb"], after(2 * t + 2))
                sp.dma_start(io["hT_all"][ds(t * P, P), :], hT[:, s].rearrange("p c t -> p (c t)"))\
                  .then_inc(S["hT_stored%d" % s], 16)
                sp.wait_ge(S["m_evac"], after(NU * (t + 1)))
                sp.dma_start(io["pr_all"][ds(t * P, P), 0:AW], pr[:, s, :]).then_inc(S["pr_stored%d" % s], 16)

            with sp.Fori(0, PAIRS) as q:
                for s in range(2):
                    tile(2 * q + s, s, True)
            for t in range(2 * PAIRS, NT + 1):
                tile(t, t % 2, t + 2 <= NT)
            sp.wait_ge(S["pr_stored0"], after(16 * (NT // 2 + 1)))
            sp.wait_ge(S["pr_stored1"], after(16 * (NT // 2)))
            sp.wait_ge(S["hT_stored0"], after(16 * (NT // 2 + 1)))
            sp.wait_ge(S["hT_stored1"], after(16 * (NT // 2)))
            sp.wait_ge(S["wb_loaded"], after(16 * KD))

        @block.scalar
        def _(act):
            def norm(t, s, q):
                act.wait_ge(S["x0_loaded%d" % s], after(16 * (q + 1)))
                act.wait_ge(S["rstd0_ready"], after(t))
                act.wait_ge(S["x0_scaled"], after(t))
                act.activation(junk[:, :], x[:, s, :], ACT.Square, accum_out=ssum[:, s:s + 1]).then_inc(S["ss0_ready"], 1)
                act.wait_ge(S["rstd0_ready"], after(t + 1))
                act.wait_ge(S["ss0_ready"], after(t + 1))
                act.activation(x[:, s, :], x[:, s, :], ACT.Copy, scale=rstd[:, s:s + 1]).then_inc(S["x0_scaled"], 1)

            def turned(t, s, q):
                act.wait_ge(S["hT_stored%d" % s], after(16 * q))
                act.wait_ge(S["m_ps"], after(NU * (t - 1)) if not isinstance(t, int) or t > 1 else after(0))
                for u in range(2):
                    act.wait_ge(S["xT_ps"], after(2 * t + u + 1))
                    for k in range(4):
                        c = 4 * u + k
                        ins = act.activation(hT[:, s, c, :], PT[u][:, k * P:(k + 1) * P], ACT.Copy,
                                             scale=nw0[:, c:c + 1])
                    ins.then_inc(S["hT_sb"], 1)

            def evacuate(t, s, q):
                act.wait_ge(S["pr_stored%d" % s], after(16 * q))
                for n, (a, b) in enumerate(A_CUTS):
                    act.wait_ge(S["m_ps"], after(NU * t + n + 1))
                    act.copy(pr[:, s, a:b], PA[n % 4][:, 0:b - a]).then_inc(S["m_evac"], 1)

            act.wait_ge(S["c0_loaded"], after(32))
            norm(0, 0, 0)
            turned(0, 0, 0)
            norm(1, 1, 0)
            with act.Fori(0, PAIRS) as q:
                for s in range(2):
                    turned(2 * q + s + 1, 1 - s, q + s)
                    norm(2 * q + s + 2, s, q + 1)
                    evacuate(2 * q + s, s, q)
            for t in range(2 * PAIRS, NT + 1):
                if t + 1 <= NT:
                    turned(t + 1, (t + 1) % 2, (t + 1) // 2)
                if t + 2 <= NT:
                    norm(t + 2, t % 2, t // 2 + 1)
                evacuate(t, t % 2, t // 2)

        @block.tensor
        def _(pe):
            def turn(t, s):
                pe.wait_ge(S["x0_scaled"], after(t + 1))
                pe.wait_ge(S["hT_sb"], after(2 * t))
                for u in range(2):
                    for k in range(4):
                        c = 4 * u + k
                        ins = pe.transpose(PT[u][:, k * P:(k + 1) * P], x[:, s, c * P:(c + 1) * P], ident[:, :])
                    ins.then_inc(S["xT_ps"], 1)

            def project(t, s, first=False):
                pe.wait_ge(S["hT_sb"], after(2 * t + 2))
                for n, (a, b) in enumerate(A_CUTS):
                    if first:
                        pe.wait_ge(S["w0_loaded%d" % n], after(16 * KD))
                    pe.wait_ge(S["m_evac"], after(NU * t + max(0, n - 3)))
                    for c in range(KD):
                        ins = pe.matmul(PA[n % 4][:, 0:b - a], hT[:, s, c, :], w_a[:, c, a:b], start=(c == 0),
                                        stop=(c == KD - 1))
                    ins.then_inc(S["m_ps"], 1)

            pe.wait_ge(S["c0_loaded"], after(32))
            turn(0, 0)
            turn(1, 1)
            project(0, 0, True)
            with pe.Fori(0, PAIRS) as q:
                for s in range(2):
                    turn(2 * q + s + 2, s)
                    project(2 * q + s + 1, 1 - s)
            for t in range(2 * PAIRS, NT):
                if t + 2 <= NT:
                    turn(t + 2, t % 2)
                project(t + 1, (t + 1) % 2)

        @block.gpsimd
        def _(pool):
            link, fresh = link_in(pool, S["pool_link"])
            pool.memset(nhalf[:, :], -0.5).then_inc(S["n0_ready"], 1)
            pool.wait_ge(S["n0_ready"], after(1))

            def tile(t, s):
                fresh()
                pool.wait_ge(S["ss0_ready"], after(t + 1))
                link()
                link(pool.tensor_scalar(rstd[:, s:s + 1], ssum[:, s:s + 1], 1.0 / D, EPS, ALU.mult, ALU.add))
                pool.tensor_tensor(rstd[:, s:s + 1], rstd[:, s:s + 1], nhalf[:, 0:1], ALU.pow)\
                    .then_inc(S["rstd0_ready"], 1)

            with pool.Fori(0, NT // 2) as q:
                for s in range(2):
                    tile(2 * q + s, s)
            tile(NT, 0)


def tiles(eng, front, hand_over, back, ahead=None):
    def step(t, U, NK, first):
        front(t, U, NK)
        if back and not first:
            back(t, U, NK)
        if ahead and first:
            ahead()
        if hand_over:
            hand_over(t)

    step(0, 0, 1, True)
    for g in range(GROUPS):
        with eng.Fori(0 if g else 1, GT) as j:
            step(j + GT * g, j * (g + 1) + units_before(g), g + 1, False)
    if back:
        back(NT, units_before(GROUPS), GROUPS, False)


def layer0_mixers(nc, io, S, w_b):
    ctx = ExitStack()
    with ctx:
        def sb(name, shape, dt=FP):
            return ctx.enter_context(nc.sbuf_tensor(name, shape, dt))

        pr = sb("pr", [P, ABW])
        kT = sb("kT", [P, SEQ])
        ikT = sb("ikT", [P, SEQ])
        vst = sb("vst", [P, NT, P])
        isc = sb("isc", [P, SEQ])
        sm = sb("sm", [P, 3, SEQ])
        mb = sb("mb", [P, SEQ], BF)
        ident = sb("ident", [P, P])
        caus = sb("caus_t", [P, CH])
        rmask = sb("rmask_t", [P, 2, 2 * P])
        qdec = sb("qdec_t", [P, 2, P])
        kdec = sb("kdec_t", [P, RH])
        cdec = sb("cdec_t", [P, RH])
        pow2 = sb("pow2_t", [P, STEPS + 1])
        ropea = sb("ropea_t", [P, 2, NHEADS17, 16])
        ropeb = sb("ropeb_t", [P, 2, HD])
        ptT = sb("ptT", [P, 2, CH])
        qT = sb("qT", [P, AH, P])
        iqT = sb("iqT", [P, 4, P])
        qkbT = sb("qkbT", [P, 4, P])
        qbd = sb("qbd", [P, 2, P])
        attm = sb("attm", [P, 2, 2 * P])
        qnext = sb("qnext", [P, 4, P])
        tg = sb("tg", [P, D])
        gates = sb("gates_cur", [P, AH * HD])
        ya = sb("ya", [P, AH * HD])
        yb = sb("yb", [P, AH * HD])
        band = sb("band", [P, SEQ], BF)
        above = sb("above", [P, SEQ], BF)
        junk = above
        hT = sb("hT_next", [P, KD, P])
        relu = sb("relu", [P, 2, CH])
        rst = sb("rst", [P, RH, RV])
        kd = sb("kd", [P, RH, P])
        gng = sb("gng", [P, RH * RV])
        small = sb("small", [P, 64])
        nhalf = sb("nhalf", [P, RH])
        lo_b, hi_b, rng_, mid, cnt, ph, hi_c, lo_c, cgt, need = [small[:, 2 + i:3 + i] for i in range(10)]
        mxc, negm, rsum = small[:, 12:16], small[:, 16:24], small[:, 24:32]
        gsum, gsq, grs = small[:, 32:36], small[:, 36:40], small[:, 40:44]
        iwc = small[:, 44:48]
        rinv = small[:, 48:56]
        vtmp = small[:, 56:57]
        halves = sb("halves", [P, STEPS + 1])
        rt_a, rt_b = sb("rt_a", [P, 512])[:, :], sb("rt_b", [P, 512])[:, :]
        gn_c, gn_q = rt_a, rt_b

        def ps(name):
            return ctx.enter_context(nc.psum_tensor(name, [P, 512], FP))

        PX = [ps("PX0"), ps("PX1")]
        PS = [ps("PS0"), ps("PS1")]
        PT = [ps("PT0"), ps("PT1")]
        PO, PR = ps("PO"), ps("PR")

        block = ctx.enter_context(nc.Block())

        @block.scalar
        def _(act):
            def front(t, U, NK):
                act.wait_ge(S["cur_ready"], after(t))
                act.wait_ge(S["tr_ps"], after(3 * t + 1))
                act.copy(qnext[:, :, :].rearrange("p r t -> p (r t)"), PX[0][:, :]).then_inc(S["tr_sb"], 1)
                act.wait_ge(S["tr_ps"], after(3 * t + 2))
                act.copy(kT[:, ds(t * P, P)], PX[1][:, 0:P])
                for a in range(2):
                    act.copy(iqT[:, :, :].rearrange("p (c a) t -> p c a t", a=2)[a * HD:(a + 1) * HD, :, a],
                             PX[1][a * HD:(a + 1) * HD, P:3 * P].rearrange("p (c t) -> p c t", c=2))
                act.copy(ikT[:, ds(t * P, P)], PX[1][:, 3 * P:4 * P]).then_inc(S["tr_sb"], 1)
                act.wait_ge(S["tr_ps"], after(3 * t + 3))
                act.copy(qkbT[:, :, :].rearrange("p r t -> p (r t)"), PX[0][:, :]).then_inc(S["tr_sb"], 1)
                act.wait_ge(S["pb_sb"], after(NB * (t + 1)))
                for u in range(4 * NK):
                    act.wait_ge(S["idx_ps"], after(4 * U + u + 1))
                    act.wait_ge(S["idx_acc"], after(4 * U + u - 1) if u >= 2 else after(4 * U))
                    act.activation(relu[:, u % 2, :], PX[u % 2][:, :], ACT.Relu, scale=1.0 / 16)\
                       .then_inc(S["idx_rd"], 1)
                act.wait_ge(S["gn_done"], after(t))
                act.activation(tg[:, 0:512], pr[:, C_ZA:C_ZA + 512], ACT.Tanh, scale=0.5)
                act.activation(tg[:, 512:1024], pr[:, C_ZB:C_ZB + 512], ACT.Tanh, scale=0.5).then_inc(S["g_tanh"], 1)

            def hand_over(t):
                act.wait_ge(S["gates_done"], after(t + 1))
                act.wait_ge(S["ya_ready"], after(t))
                act.wait_ge(S["tr_sb"], after(3 * t + 3))
                for a in range(2):
                    act.copy(qT[a * HD:(a + 1) * HD, 4 * a:4 * a + 4, :].rearrange("p r t -> p (r t)"),
                             qnext[a * HD:(a + 1) * HD, :, :].rearrange("p r t -> p (r t)"))
                act.copy(gates[:, :], tg[:, 0:512]).then_inc(S["cur_ready"], 1)

            def projected(t, n):
                if n == 0 and (not isinstance(t, int) or t):
                    act.wait_ge(S["ro_ps"], after(t))
                    act.wait_ge(S["rs_ps"], after(t))
                    act.wait_ge(S["gates_done"], after(t))
                a, b = B_CUTS[n]
                act.wait_ge(S["pb_ps"], after(NB * t + n + 1))
                act.copy(pr[:, a:b], PX[n % 2][:, 0:b - a]).then_inc(S["pb_sb"], 1)

            def back(t, U, NK, beside=True):
                W = NK * CH
                for h in range(1, AH + 2):
                    if beside and h % 2 == 0 and h // 2 - 1 < NB:
                        projected(t + 1, h // 2 - 1)
                    if h <= AH:
                        act.wait_ge(S["nm_ready"], after(8 * (t - 1) + h))
                        row = sm[:, (h - 1) % 3, 0:W]
                        act.activation(row, row, ACT.Exp, bias=negm[:, h - 1:h], scale=HD ** -0.5,
                                       accum_out=rsum[:, h - 1:h]).then_inc(S["exp_done"], 1)
                    if h >= 2:
                        for c in range(NK):
                            v = (h - 2) * NK + c
                            act.wait_ge(S["pt_ps"], after(8 * (U - 1) + v + 1))
                            act.wait_ge(S["pv_done"], after(8 * (U - 1) + max(v - 1, 0)))
                            act.copy(ptT[:, v % 2, :], PT[v % 2][:, :]).then_inc(S["pt_sb"], 1)

            act.wait_ge(S["const_ready"], after(2))
            act.wait_ge(S["c_loaded"], after(16 * 7))
            act.wait_ge(S["zeroed"], after(8))
            act.wait_ge(S["pr_loaded"], after(16))
            for n in range(NB):
                projected(0, n)
            tiles(act, front, hand_over, back, lambda: [projected(1, n) for n in range(NB)])

        @block.tensor
        def _(pe):
            def front(t, U, NK):
                pe.wait_ge(S["rope_done"], after(t + 1))
                pe.wait_ge(S["pb_sb"], after(NB * (t + 1)))
                pe.transpose(PX[1][:, 0:P], pr[:, C_KA:C_KA + P], ident[:, :])
                for h in range(AH):
                    lo, r = HD * (h // 4), h % 4
                    ins = turn_half(pe, PX[0][lo:lo + HD, r * P:(r + 1) * P], pr[:, h * HD:(h + 1) * HD],
                                    ident[:, :], h // 4)
                ins.then_inc(S["tr_ps"], 1)
                pe.transpose(PX[1][:, P:2 * P], pr[:, C_IQ:C_IQ + P], ident[:, :])
                pe.transpose(PX[1][:, 2 * P:3 * P], pr[:, C_IQ + P:C_IQ + 2 * P], ident[:, :])
                for a in range(2):
                    ins = turn_half(pe, PX[1][a * HD:(a + 1) * HD, 3 * P:4 * P], pr[:, C_IK:C_IK + HD],
                                    ident[:, :], a)
                ins.then_inc(S["tr_ps"], 1)
                pe.wait_ge(S["tr_sb"], after(3 * t + 1))
                for r in range(4):
                    ins = pe.transpose(PX[0][:, r * P:(r + 1) * P], pr[:, C_QB + r * P:C_QB + (r + 1) * P],
                                       ident[:, :])
                ins.then_inc(S["tr_ps"], 1)
                pe.wait_ge(S["tr_sb"], after(3 * t + 3))
                for u in range(4 * NK):
                    c, h = divmod(u, 4)
                    if u >= 2:
                        pe.wait_ge(S["idx_rd"], after(4 * U + u - 1))
                    pe.matmul(PX[u % 2][:, :], iqT[:, h, :], ikT[:, c * CH:(c + 1) * CH],
                              start=True, stop=True).then_inc(S["idx_ps"], 1)
                pe.wait_ge(S["tr_sb"], after(3 * t + 3))
                pe.wait_ge(S["idx_rd"], after(4 * U + 4 * NK))
                for h in range(RH):
                    lo = HD * (h % 2)
                    ins = pe.matmul(PX[h % 2][:, (h // 2) * P:(h // 2 + 1) * P], qkbT[lo:lo + HD, 2 + h // 2, :],
                                    qkbT[lo:lo + HD, h // 2, :], start=True, stop=True)
                ins.then_inc(S["ra_ps"], 1)
                pe.wait_ge(S["kd_ready"], after(t + 1))
                pe.wait_ge(S["ra_sb"], after(t + 1))
                for h in range(RH):
                    ins = pe.matmul(PX[h // 2][:, 2 * P + (h % 2) * RV:2 * P + (h % 2 + 1) * RV], kd[:, h, :],
                                    pr[:, C_VB + h * RV:C_VB + (h + 1) * RV], start=True, stop=True)
                ins.then_inc(S["rs_ps"], 1)
                pe.wait_ge(S["ra_sb"], after(t + 1))
                pe.wait_ge(S["qd_ready"], after(t + 1))
                pe.wait_ge(S["r_upd"], after(t))
                pe.wait_ge(S["gn_sum"], after(t))
                for h in range(RH):
                    o = PR[:, h * RV:(h + 1) * RV]
                    pe.matmul(o, attm[:, h % 2, (h // 2) * P:(h // 2 + 1) * P], pr[:, C_VB + h * RV:C_VB + (h + 1) * RV], start=True, stop=False)
                    ins = pe.matmul(o, qbd[:, h // 2, :], rst[:, h, :], start=False,
                                    stop=True)
                ins.then_inc(S["ro_ps"], 1)

            def project(t, n, chunks):
                if n == 0 and chunks[0] == 0:
                    pe.wait_ge(S["hT_loaded"], after(16 * (t + 1)))
                    pe.wait_ge(S["ra_sb"], after(t))
                    pe.wait_ge(S["r_upd"], after(t))
                if n >= 2 and chunks[0] == 0:
                    pe.wait_ge(S["pb_sb"], after(NB * t + n - 1))
                a, b = B_CUTS[n]
                for c in chunks:
                    ins = pe.matmul(PX[n % 2][:, 0:b - a], hT[:, c, :], w_b[:, c, a - AW:b - AW], start=(c == 0),
                                    stop=(c == KD - 1))
                if chunks[-1] == KD - 1:
                    ins.then_inc(S["pb_ps"], 1)

            def back(t, U, NK, beside=True):
                pe.wait_ge(S["cur_ready"], after(t))
                pe.wait_ge(S["v_stored"], after(t + 1) if not isinstance(t, int) else after(NT))
                for h in range(AH + 2):
                    for c in range(NK + 1):
                        u = h * NK + c
                        if h < AH and c < NK:
                            if u >= 2:
                                pe.wait_ge(S["sm_done"], after(8 * (U - 1) + u - 1))
                            pe.matmul(PS[u % 2][:, :], qT[:, h, :], kT[:, c * CH:(c + 1) * CH],
                                      start=True, stop=True).then_inc(S["s_ps"], 1)
                            chunks = range(4 * (h % 2) + 4 * c // NK, 4 * (h % 2) + 4 * (c + 1) // NK)
                            if beside and len(chunks):
                                project(t + 1, h // 2, chunks)
                        if h < 2:
                            continue
                        v = (h - 2) * NK + c
                        if c < NK:
                            if c == 0:
                                pe.wait_ge(S["exp_done"], after(8 * (t - 1) + h - 1))
                            if v >= 2:
                                pe.wait_ge(S["pt_sb"], after(8 * (U - 1) + v - 1))
                            for k in range(4):
                                ins = pe.transpose(PT[v % 2][:, k * P:(k + 1) * P],
                                                   sm[:, (h - 2) % 3, c * CH + k * P:c * CH + (k + 1) * P],
                                                   ident[:, :])
                            ins.then_inc(S["pt_ps"], 1)
                        if c:
                            if v == 1:
                                pe.wait_ge(S["ya_ready"], after(t - 1))
                            pe.wait_ge(S["pt_sb"], after(8 * (U - 1) + v))
                            gv = (h - 2) // 4
                            for k in range(4):
                                ins = pe.matmul(PO[:, (h - 2) * HD:(h - 1) * HD],
                                                ptT[:, (v - 1) % 2, k * P:(k + 1) * P],
                                                vst[:, 4 * (c - 1) + k, gv * HD:(gv + 1) * HD],
                                                start=(c == 1 and k == 0), stop=(c == NK and k == 3))
                            ins.then_inc(S["pv_done"], 1)

            pe.wait_ge(S["c_loaded"], after(16 * 7))
            pe.wait_ge(S["zeroed"], after(8))
            for n in range(NB):
                project(0, n, range(KD))
            tiles(pe, front, None, back, lambda: [project(1, n, range(KD)) for n in range(NB)])

        @block.vector
        def _(dve):
            link, fresh = link_in(dve, S["dve_link"])

            def front(t, U, NK, last=None):
                W = NK * CH
                fresh()
                dve.wait_ge(S["gn_done"], after(t))
                dve.wait_ge(S["pr_loaded"], after(16 * (t + 1)))
                dve.wait_ge(S["pb_sb"], after(NB * (t + 1)))
                dve.wait_ge(S["tab_loaded"], after(32 * (t + 1)))
                x17 = pr[:, 0:17 * HD].rearrange("p (h d) -> p h d", d=HD)
                ta = rt_a[:, 0:272].rearrange("p (h d) -> p h d", d=16)
                tb = rt_b[:, 0:272].rearrange("p (h d) -> p h d", d=16)
                dve.tensor_tensor(ta, x17[:, :, 0:16], ropea[:, 0], ALU.mult)
                dve.tensor_tensor(tb[:, :, 0:8], x17[:, :, 8:16], ropea[:, 1, :, 0:8], ALU.mult)
                link(dve.tensor_tensor(tb[:, :, 8:16], x17[:, :, 0:8], ropea[:, 1, :, 8:16], ALU.mult))
                link(dve.tensor_tensor(x17[:, :, 0:16], ta, tb, ALU.add))
                x8 = pr[:, C_QB:C_QB + 512].rearrange("p (h d) -> p h d", d=HD)
                ta = rt_a.rearrange("p (h d) -> p h d", d=HD)
                tb = rt_b.rearrange("p (h d) -> p h d", d=HD)

                def row(k, a, b):
                    return ropeb[:, k:k + 1, a:b].to_broadcast([P, 8, b - a])

                dve.tensor_tensor(ta, x8, row(0, 0, HD), ALU.mult)
                dve.tensor_tensor(tb[:, :, 0:32], x8[:, :, 32:64], row(1, 0, 32), ALU.mult)
                link(dve.tensor_tensor(tb[:, :, 32:64], x8[:, :, 0:32], row(1, 32, 64), ALU.mult))
                dve.tensor_copy(iwc, pr[:, C_IW:C_IW + 4]).then_inc(S["iw_ready"], 1)
                dve.tensor_tensor(x8, ta, tb, ALU.add).then_inc(S["rope_done"], 1)
                dve.wait_ge(S["rope_done"], after(t + 1))
                dve.wait_ge(S["rs_ps"], after(t))
                for a in range(2):
                    kv = kd[:, :, :].rearrange("p (c a) d -> p a c d", a=2)[:, a, :, a * HD:(a + 1) * HD]
                    src = pr[:, C_KB:C_KB + 256].rearrange("p (c a d) -> p a c d", a=2, d=HD)[:, a]
                    dec = kdec[:, :].rearrange("p (c a) -> p a c", a=2)[:, a].unsqueeze(2).to_broadcast([P, 2, HD])
                    ins = dve.tensor_tensor(kv, src, dec, ALU.mult)
                ins.then_inc(S["kd_ready"], 1)
                dve.wait_ge(S["tr_sb"], after(3 * t + 3))
                dve.wait_ge(S["ro_ps"], after(t))
                dve.tensor_tensor(qbd[:, :, :], qkbT[:, 0:2, :], qdec[:, :, :], ALU.mult)\
                   .then_inc(S["qd_ready"], 1)
                dve.wait_ge(S["iw_ready"], after(t + 1))
                for u in range(4 * NK):
                    c, h = divmod(u, 4)
                    dve.wait_ge(S["idx_rd"], after(4 * U + u + 1))
                    dst = isc[:, c * CH:(c + 1) * CH]
                    if h == 0:
                        dve.tensor_scalar(dst, relu[:, u % 2, :], iwc[:, 0:1], None, ALU.mult)\
                           .then_inc(S["idx_acc"], 1)
                    else:
                        dve.wait_ge(S["idx_acc"], after(4 * U + u))
                        dve.scalar_tensor_tensor(dst, relu[:, u % 2, :], iwc[:, h:h + 1], dst, ALU.mult, ALU.add)\
                           .then_inc(S["idx_acc"], 1)
                dve.wait_ge(S["ra_ps"], after(t + 1))
                for a in range(2):
                    ins = dve.tensor_tensor(attm[:, a, :], PX[a][:, 0:2 * P], rmask[:, a, :], ALU.mult)
                ins.then_inc(S["ra_sb"], 1)
                dve.wait_ge(S["g_tanh"], after(t + 1))
                dve.scalar_tensor_tensor(tg[:, 0:512], tg[:, 0:512], 1.0, pr[:, C_ZA:C_ZA + 512], ALU.add, ALU.mult)
                dve.scalar_tensor_tensor(tg[:, 512:1024], tg[:, 512:1024], 1.0, pr[:, C_ZB:C_ZB + 512], ALU.add,
                                         ALU.mult).then_inc(S["gates_done"], 1)
                dve.wait_ge(S["idx_acc"], after(4 * U + 4 * NK))
                link(dve.tensor_reduce(lo_b, isc[:, 0:W], AX, ALU.min))
                link(dve.tensor_reduce(hi_b, isc[:, 0:W], AX, ALU.max))
                dve.wait_ge(S["ro_ps"], after(t + 1))
                for h in range(RH):
                    ins = dve.scalar_tensor_tensor(rst[:, h, :], rst[:, h, :], cdec[:, h:h + 1],
                                                   PX[h // 2][:, 2 * P + (h % 2) * RV:2 * P + (h % 2 + 1) * RV],
                                                   ALU.mult, ALU.add)
                ins.then_inc(S["r_upd"], 1)
                pv = PR[:, :].rearrange("p (h d) -> p h d", d=RV)
                cv = gn_c.rearrange("p (h d) -> p h d", d=RV)
                qv = gn_q.rearrange("p (h d) -> p h d", d=RV)
                dve.wait_ge(S["gn_rs"], after(t))
                dve.wait_ge(S["idx_acc"], after(4 * U + 4 * NK))
                link(dve.tensor_reduce(gsum, pv, AX, ALU.add))
                link(dve.tensor_scalar(gsum, gsum, -1.0 / RV, None, ALU.mult))
                link(dve.tensor_tensor(cv, pv, gsum.unsqueeze(2).to_broadcast([P, RH, RV]), ALU.add))
                link(dve.tensor_tensor(qv, cv, cv, ALU.mult))
                dve.tensor_reduce(gsq, qv, AX, ALU.add).then_inc(S["gn_sum"], 1)
                dve.wait_ge(S["caus_loaded"], after(16 * (t + 1)))
                tail = isc[:, W - CH:W]
                link(dve.tensor_tensor(tail, tail, caus[:, :], ALU.add))
                link(dve.tensor_scalar(lo_b, lo_b, 0.0, None, ALU.min))
                link(dve.tensor_scalar(hi_b, hi_b, 0.0, 1e-20, ALU.max, ALU.add))
                link(dve.tensor_tensor(rng_, hi_b, lo_b, ALU.subtract))
                link(dve.tensor_scalar(halves[:, :], pow2[:, :], rng_, None, ALU.mult))
                link(dve.tensor_tensor(mid, lo_b, halves[:, 0:1], ALU.add))
                for n in range(STEPS):
                    if last is not None:
                        last(AH * NK * n // STEPS, AH * NK * (n + 1) // STEPS)
                    link(dve.tensor_scalar(junk[:, 0:W], isc[:, 0:W], mid, 0.0, ALU.is_gt, ALU.add, accum_out=cnt))
                    link(dve.tensor_scalar(ph, cnt, TOPK - 0.5, halves[:, n:n + 1], ALU.is_ge, ALU.mult))
                    link(dve.scalar_tensor_tensor(mid, ph, halves[:, n + 1:n + 2], mid, ALU.subtract, ALU.add))
                w = halves[:, STEPS - 3:STEPS - 2]
                link(dve.tensor_tensor(hi_c, mid, w, ALU.add))
                link(dve.tensor_tensor(lo_c, mid, w, ALU.subtract))
                over, tie, order = above[:, 0:W], band[:, 0:W], isc[:, 0:W]
                link(dve.tensor_scalar(over, isc[:, 0:W], hi_c, 0.0, ALU.is_gt, ALU.add, accum_out=cgt))
                link(dve.tensor_scalar(need, cgt, -1.0, float(TOPK), ALU.mult, ALU.add))
                link(dve.scalar_tensor_tensor(tie, isc[:, 0:W], lo_c, over, ALU.is_gt, ALU.subtract))
                link(dve.tensor_tensor_scan(order, tie, tie, 0.0, ALU.add, ALU.bypass))
                link(dve.scalar_tensor_tensor(tie, order, need, tie, ALU.is_le, ALU.mult))
                link(dve.tensor_tensor(tie, tie, over, ALU.add))
                dve.tensor_scalar(mb[:, 0:W], tie, BIG, -BIG, ALU.mult, ALU.add).then_inc(S["mask_ready"], 1)
                dve.wait_ge(S["gn_rs"], after(t + 1))
                link(dve.tensor_tensor(cv, cv, grs.unsqueeze(2).to_broadcast([P, RH, RV]), ALU.mult))
                link(dve.tensor_tensor(gn_c, gn_c, gng[:, :], ALU.mult))
                dve.wait_ge(S["yb_stored"], after(16 * t))
                dve.tensor_tensor(yb[:, :], gn_c, tg[:, 512:1024], ALU.mult).then_inc(S["gn_done"], 1)

            def attend(t, U, NK):
                def part(first, end):
                    for u in range(first, end):
                        h, c = divmod(u, NK)
                        if c == 0 and h >= 3:
                            dve.wait_ge(S["pt_ps"], after(8 * (U - 1) + (h - 2) * NK))
                        dve.wait_ge(S["s_ps"], after(8 * (U - 1) + u + 1))
                        link()
                        dve.tensor_tensor_reduce(sm[:, h % 3, c * CH:(c + 1) * CH], PS[u % 2][:, :],
                                                 mb[:, c * CH:(c + 1) * CH], 1.0, -3e38, ALU.add, ALU.max,
                                                 mxc[:, c:c + 1]).then_inc(S["sm_done"], 1)
                        if c == NK - 1:
                            dve.wait_ge(S["sm_done"], after(8 * (U - 1) + u + 1))
                            link(dve.tensor_reduce(vtmp, mxc[:, 0:NK], AX, ALU.max))
                            dve.tensor_scalar(negm[:, h:h + 1], vtmp, -HD ** -0.5, None, ALU.mult)\
                                .then_inc(S["nm_ready"], 1)
                return part

            def attended(t, U, NK):
                dve.wait_ge(S["exp_done"], after(8 * t))
                link(dve.reciprocal(rinv, rsum))
                link(dve.tensor_scalar(rinv, rinv, 0.5, None, ALU.mult))
                dve.wait_ge(S["pv_done"], after(8 * (U - 1) + 8 * NK))
                dve.wait_ge(S["ya_stored"], after(16 * (t - 1)))
                for h in range(AH):
                    hs = slice(h * HD, (h + 1) * HD)
                    ins = dve.scalar_tensor_tensor(ya[:, hs], PO[:, hs], rinv[:, h:h + 1], gates[:, hs], ALU.mult,
                                                   ALU.mult)
                ins.then_inc(S["ya_ready"], 1)

            dve.wait_ge(S["c_loaded"], after(16 * 7))
            dve.tensor_scalar(gng[:, :], gng[:, :], 0.5, None, ALU.mult).then_inc(S["const_ready"], 1)
            dve.memset(nhalf[:, :], -0.5).then_inc(S["const_ready"], 1)
            dve.wait_ge(S["const_ready"], after(2))
            dve.wait_ge(S["zeroed"], after(8))
            front(0, 0, 1)
            for g in range(GROUPS):
                with dve.Fori(0 if g else 1, GT) as j:
                    t, U, NK = j + GT * g, j * (g + 1) + units_before(g), g + 1
                    front(t, U, NK, attend(t, U, NK))
                    attended(t, U, NK)
            fresh()
            attend(NT, units_before(GROUPS), GROUPS)(0, AH * GROUPS)
            attended(NT, units_before(GROUPS), GROUPS)

        @block.gpsimd
        def _(pool):
            link, fresh = link_in(pool, S["pool_link"])
            pool.memset(mb[:, :], -BIG).then_inc(S["zeroed"], 1)
            for z in (qT[:, :, :], iqT[:, :, :], kT[:, :], ikT[:, :], vst[:, :, :], rst[:, :, :], kd[:, :, :]):
                pool.memset(z, 0.0).then_inc(S["zeroed"], 1)
            pool.wait_ge(S["const_ready"], after(2))

            def front(t, U, NK):
                fresh()
                pool.wait_ge(S["rope_done"], after(t + 1))
                pool.wait_ge(S["zeroed"], after(8))
                if not isinstance(t, int) or t:
                    pool.wait_ge(S["pv_done"], after(8 * (U - 1)))
                pool.tensor_copy(vst[:, ds(t, 1), :], pr[:, C_VA:C_VA + P].unsqueeze(1)).then_inc(S["v_stored"], 1)
                pool.wait_ge(S["gn_sum"], after(t + 1))
                link()
                link(pool.tensor_scalar(grs, gsq, 1.0 / RV, EPS, ALU.mult, ALU.add))
                pool.tensor_tensor(grs, grs, nhalf[:, :], ALU.pow).then_inc(S["gn_rs"], 1)

            tiles(pool, front, None, None)

        @block.sync
        def _(sp):
            def load_pr(t):
                sp.dma_start(pr[:, 0:AW], io["pr_all"][ds(t * P, P), 0:AW]).then_inc(S["pr_loaded"], 16)

            def load_hT(t):
                sp.dma_start(hT[:, :, :].rearrange("p c t -> p (c t)"), io["hT_all"][ds(t * P, P), :])\
                  .then_inc(S["hT_loaded"], 16)

            def load_tables(t):
                sp.dma_start(ropea[:, :, :, :].rearrange("p a h d -> p (a h d)"), io["ropea"][ds(t * P, P), :])\
                  .then_inc(S["tab_loaded"], 16)
                sp.dma_start(ropeb[:, :, :].rearrange("p a d -> p (a d)"), io["ropeb"][ds(t * P, P), :])\
                  .then_inc(S["tab_loaded"], 16)

            load_hT(0)
            load_pr(0)
            load_tables(0)
            for dst, src in ((ident, io["ident"]), (rmask, io["rmask"].rearrange("p (h t) -> p h t", h=2)),
                             (qdec, io["qdec"].rearrange("p (h t) -> p h t", h=2)), (kdec, io["kdec"]),
                             (cdec, io["cdec"]), (pow2, io["pow2"]),
                             (gng, io["gn_ret"].partition_broadcast(P))):
                sp.dma_start(dst[tuple(slice(None) for _ in dst.shape)], src,
                             allow_slow_non_contiguous=True).then_inc(S["c_loaded"], 16)

            def front(t, U, NK, j):
                sp.wait_ge(S["pb_ps"], after(NB * (t + 1)))
                load_hT(t + 1)
                sp.wait_ge(S["mask_ready"], after(t))
                sp.dma_start(caus[:, :], io["caus"][:, ds(j * CH, CH)]).then_inc(S["caus_loaded"], 16)
                sp.wait_ge(S["rope_done"], after(t + 1))
                sp.dma_start(io["k_all"][ds(t * P, P), :], pr[:, C_KA:C_KA + P]).then_inc(S["kv_stored"], 16)
                sp.dma_start(io["v_all"][ds(t * P, P), :], pr[:, C_VA:C_VA + P]).then_inc(S["kv_stored"], 16)
                sp.dma_start(io["ik_all"][ds(t * P, P), :], pr[:, C_IK:C_IK + HD]).then_inc(S["kv_stored"], 16)
                load_tables(t + 1)
                sp.wait_ge(S["kv_stored"], after(48 * (t + 1)))
                sp.wait_ge(S["v_stored"], after(t + 1))
                sp.wait_ge(S["ro_ps"], after(t + 1))
                sp.wait_ge(S["gates_done"], after(t + 1))
                load_pr(t + 1)
                if not isinstance(t, int) or t:
                    sp.wait_ge(S["ya_ready"], after(t))
                    sp.dma_start(io["yab_all"][ds((t - 1) * P, P), 0:512], ya[:, :]).then_inc(S["ya_stored"], 16)
                sp.wait_ge(S["gn_done"], after(t + 1))
                sp.dma_start(io["yab_all"][ds(t * P, P), 512:1024], yb[:, :]).then_inc(S["yb_stored"], 16)

            front(0, 0, 1, 0)
            for g in range(GROUPS):
                with sp.Fori(0 if g else 1, GT) as j:
                    front(j + GT * g, None, None, j)
            sp.wait_ge(S["ya_ready"], after(NT))
            sp.dma_start(io["yab_all"][(NT - 1) * P:NT * P, 0:512], ya[:, :]).then_inc(S["ya_stored"], 16)
            sp.wait_ge(S["r_upd"], after(NT))
            for h in range(RH):
                lo = HD * (h % 2)
                sp.dma_start(io["ret_prompt"][h], rst[lo:lo + HD, h, :]).then_inc(S["ret_stored"], 16)
            sp.wait_ge(S["pr_loaded"], after(16 * (NT + 1)))
            sp.wait_ge(S["kv_stored"], after(48 * NT))
            sp.wait_ge(S["ya_stored"], after(16 * NT))
            sp.wait_ge(S["yb_stored"], after(16 * NT))
            sp.wait_ge(S["pb_sb"], after(NB * (NT + 1)))
            sp.dma_start(io["pr_all"][SEQ:ROWS, AW:ABW], pr[:, AW:ABW]).then_inc(S["ret_stored"], 16)
            sp.wait_ge(S["ret_stored"], after(80))


NBLK = CC // P
CONV = 4
PROJECT_SIGNALS = """
    c0_loaded hT_sb hT_stored0 hT_stored1 m_evac m_ps n0_ready pr_stored0 pr_stored1 rstd0_ready ss0_ready
    w0_loaded0 w0_loaded1 w0_loaded2 wb_loaded x0_loaded0 x0_loaded1 x0_scaled xT_ps"""
LAYER0_SIGNALS = """
    c_loaded caus_loaded const_ready cur_ready exp_done g_tanh gates_done gn_done gn_rs gn_sum hT_loaded idx_acc idx_ps
    idx_rd iw_ready kd_ready kv_stored mask_ready nm_ready pb_ps pb_sb pr_loaded pt_ps pt_sb pv_done qd_ready r_upd ra_ps
    ra_sb ret_stored ro_ps rope_done rs_ps s_ps sm_done tab_loaded tr_ps tr_sb v_stored ya_ready ya_stored
    yb_stored zeroed"""
SAMPLES_SIGNALS = """
    c4_loaded const4 exp4 gr4 gs4 iS_ps iS_sb isc4 iw_ps kd4 kt_ps kt_sb0 kt_sb1 mb4 new_out nm4 oall4 og4
    pt4_ps pt4_sb ptab4 pv4 q4_ps qbm4 qkb4 qm4 ra4_ps ra4_sb ret4_done ro4_ps rope4 rs4_upd rs_loaded rs_stored
    s4_mx s4_ps s4_sb stage0 stage1 su4_ps tails4 tanh4 v4_0 vm4 vt4 w4 wsel4 ya4 yab4 zeroed4 zeroed5"""
CONV_SIGNALS = """
    blk_ps c2_loaded c_stored0 c_stored1 const2_ready crow_ps crow_ready cs_ps cs_ready cv_ready cv_stored
    cvh_ready cvt_ready hT2_ps hT2_sb hn2_ready pre_kept pre_loaded pre_ps pre_ready raw_ready rstd2_ready
    ss2_ready tail_kept w2c_loaded w2o_loaded x2_loaded y1_ps y1_ready y1_stored yT_ps yT_sb yab2_loaded
    z_free z_ps zg_ready zg_stored zt_ready"""
DELTA_SIGNALS = """
    ML_ready MT_ready QKD_ready R_ready bb_ps bv_ready c3_loaded cin_loaded const3_ready cur_ready dec_ready
    dif_ready egl_ps egl_read eglm_ready fr_ready fs_ready g_ready gc_ps gcb_ps kk_ps ks_ps ks_read kt_ready
    oT_ps oT_ready o_ps o_ready o_sq og_ready or_ready os_ready p1_ps p1_ready pre_a pre_d qkT_ps qkT_ready
    qk_ps qk_rs qk_sq qk_ss qkm_ready qkm_zero qkn_ready qs_ps qs_read sg_loaded sg_upd sgu_ps st_stored
    st_upd su_ps vn_ps vn_ready vnm_ready w3_loaded x_ps x_ready y13_loaded y2_ps y2_ready yo_ready
    yo_stored zg3_loaded"""
LINKS = "act_link dve_link pool_link late_values"
OUTS = {"y_all": (ROWS, D), "k_all": (ROWS, 128), "v_all": (ROWS, 128), "ik_all": (ROWS, 64),
        "ret_prompt": (RH, HD, RV), "ret_sample": (DB, RH, HD, RV),
        "gdn_prompt": (8, P, P), "gdn_sample": (DB, 8, P, P), "conv_prompt": (3, CC), "conv_sample": (DB * 3, CC),
        "yab_all": (ROWS, D), "y1_all": (ROWS, D), "zg_all": (ROWS, D), "c_all": (ROWS, CC), "pr_all": (ROWS, ABW),
        "hT_all": (ROWS, D)}


SKEYS = PAST + DT
N_CONST4 = 16
STAGE_FREE = (12, 16, 24, 32)
HB = DB // 2


def layer0_samples(nc, io, S):
    ctx = ExitStack()
    with ctx:
        def sb(name, shape, dt=FP):
            return ctx.enter_context(nc.sbuf_tensor(name, shape, dt))

        def ps(name):
            return ctx.enter_context(nc.psum_tensor(name, [P, 512], FP))

        pr = sb("prs", [P, ABW])
        K_T = [sb("kT0", [P, HB, SKEYS]), sb("kT1", [P, HB, SKEYS])]
        rows_a = sb("rows_a", [P, HB * SKEYS])
        rows_b = sb("rows_b", [P, 8 * DB * P])
        ikT = rows_a[:, :].rearrange("p (b s) -> p b s", b=HB)
        V_A = rows_a[:, 0:8 * DB * P].rearrange("p (g b d) -> p g b d", g=8, b=DB)
        V_B = rows_b[:, :].rearrange("p (g b d) -> p g b d", g=8, b=DB)
        stage = rows_b[:, :].rearrange("p (s g d) -> p s g d", s=2, g=NPG)
        sc = [sb("sc0", [P, SKEYS]), sb("sc1", [P, SKEYS])]
        isc = sb("isc_s", [SR, SKEYS])
        mb128 = sb("mb_s", [P, SKEYS])
        mb = mb128[0:SR, :]
        ptT = sb("ptT_s", [P, 2, 512])
        ptz = sb("ptt_s", [P, 2, P])
        vtz = sb("vtail", [P, DB, P])
        ptd = sb("ptd", [P, 512])
        qm = sb("qm", [P, 3, HB, P])
        hm = sb("hm_t", [P, HB, SR])
        rep = sb("rep_t", [P, SR])
        rep4 = sb("rep4_t", [P, P])
        tmask = sb("tmask_t", [SR, DT])
        dsel = sb("dsel_t", [P, DB])
        wcol = sb("wcol", [P, 1])
        wsel = sb("wsel", [P, SR])
        ident = sb("ident4", [P, P])
        pow2 = sb("pow2_s", [P, STEPS + 1])
        ptab = sb("ptab", [1, DB * NPG], I32)
        tg = sb("tg_s", [P, D])
        oall = sb("oall", [SR, 512])
        og = sb("og_s", [P, 2, HD])
        small = sb("small_s", [P, 64])
        halves = sb("halves_s", [P, STEPS + 1])
        nhalf = sb("nhalf_s", [P, RH])
        r0 = K_T[0][:, :, :].rearrange("p b s -> p (b s)")
        rs = r0[:, 0:DB * RH * P].rearrange("p (b h d) -> p b h d", b=DB, h=RH)
        vm = r0[:, 4096:4096 + 2048].rearrange("p (a b d) -> p a b d", a=2, b=DB)
        qbm = r0[:, 6144:6144 + 512].rearrange("p (c b t) -> p c b t", c=2, b=DB)
        kd = r0[:, 6656:7168].rearrange("p (h d) -> p h d", h=RH)
        qkbT = r0[:, 7168:7680].rearrange("p (h d) -> p h d", h=4)
        attm = r0[:, 7680:8192].rearrange("p (a d) -> p a d", a=2)
        r1 = K_T[1][:, :, :].rearrange("p b s -> p (b s)")
        rmask = r1[:, 0:512].rearrange("p (a d) -> p a d", a=2)
        qdec = r1[:, 512:1024].rearrange("p (c b t) -> p c b t", c=2, b=DB)
        gng = r1[:, 1024:1536]
        kdec = r1[:, 1536:1540]
        cdec = r1[:, 1540:1544]
        bsel = r1[:, 1544:1552]
        gn_c, gn_q = r1[:, 2048:2560], r1[:, 2560:3072]
        rt_a, rt_b = r1[:, 3072:3584], r1[:, 3584:4096]
        ropea = r1[:, 4096:4096 + 544].rearrange("p (a h d) -> p a h d", a=2, h=NHEADS17)
        ropeb = r1[:, 4640:4640 + 128].rearrange("p (a d) -> p a d", a=2)
        lo_b, hi_b, rng_, mid, cnt, ph, hi_c, lo_c, cgt, need = [small[0:SR, i:i + 1] for i in range(10)]
        gsum, gsq, grs = small[:, 12:16], small[:, 16:20], small[:, 20:24]
        mx8, mx1, negm, rsum, rinv = small[:, 24:34], small[:, 34:36], small[:, 36:38], small[:, 38:40], small[:, 40:42]
        PA = [ps("SA0"), ps("SA1")]
        PS = [ps("SS0"), ps("SS1")]
        PT = [ps("ST0"), ps("ST1")]
        PO = [ps("SO0"), ps("SO1")]
        block = ctx.enter_context(nc.Block())
        CHUNKS = [(c * CH, CH) for c in range(PAST // CH)] + [(PAST, DT)]
        NCH = len(CHUNKS)
        npool = io["cache_k"].shape[0]

        def fetch(eng, cache, b, first, count, dst_of, signal):
            with eng.Fori(0, count // 4) as g4:
                for k in range(4):
                    g = 4 * g4 + k
                    page = eng.value_load(ptab[0:1, ds(g + (b * NPG + first), 1)], min_val=0, max_val=npool - 1)
                    eng.dma_start(dst_of(g), cache(page)).then_inc(S[signal], 16)

        def index_pages(eng, i, a):
            fetch(eng, lambda page: io["cache_kidx"][ds(page, 1)].rearrange("a k d -> k (a d)"), i + HB * a, 0, NPG,
                  lambda g: stage[:, i % 2, ds(g, 1), a * HD:(a + 1) * HD].rearrange("p a d -> p (a d)"),
                  "stage%d" % (i % 2))

        def key_pages(eng, i, a):
            fetch(eng, lambda page: io["cache_k"][ds(page, 1)].rearrange("a k (g d) -> k (a g) d", g=2), i + HB * a,
                  0, NPG, lambda g: stage[:, i % 2, ds(g, 1), :]
                  .rearrange("p x (g a d) -> p (x g) a d", g=2, a=2)[:, :, a], "stage%d" % (i % 2))

        def value_pages(eng, part, b):
            dst = (V_A, V_B)[part]
            fetch(eng, lambda page: io["cache_v"][ds(page, 1)].rearrange("a k d -> k (a d)"), b, 8 * part, NPG // 2,
                  lambda g: dst[:, ds(g, 1), b, :].rearrange("p x d -> p (x d)"), ("v4_0", "late_values")[part])

        @block.sync
        def _(sp):
            consts = ((ident[:, :], io["ident"]), (hm[:, :, :].rearrange("p b t -> p (b t)"), io["hm"]),
                      (rep[:, :], io["rep"]), (rep4[:, :], io["rep4"]), (tmask[:, :], io["tmask"]),
                      (dsel[:, :], io["dsel"]), (pow2[:, :], io["pow2"]),
                      (rmask.rearrange("p a d -> p (a d)"), io["rmask_s"]),
                      (qdec.rearrange("p c b t -> p (c b t)"), io["qdec_s"]), (kdec, io["kdec_s"]),
                      (cdec, io["cdec_s"]), (bsel, io["bsel"][:, 0:DB]), (gng, io["gn_ret"].partition_broadcast(P)),
                      (ropea.rearrange("p a h d -> p (a h d)"), io["ropea"][SEQ:ROWS, :]),
                      (ropeb.rearrange("p a d -> p (a d)"), io["ropeb"][SEQ:ROWS, :]),
                      (pr[:, :], io["pr_all"][SEQ:ROWS, :]))
            sp.dma_start(ptab[:, :], io["page_table"]).then_inc(S["ptab4"], 16)
            for dst, src in consts:
                sp.dma_start(dst, src, allow_slow_non_contiguous=True).then_inc(S["c4_loaded"], 16)
            assert len(consts) == N_CONST4
            sp.wait_ge(S["zeroed4"], after(2))
            for h in range(RH):
                lo = HD * (h % 2)
                sp.dma_start(rs[lo:lo + HD, :, h, :], io["state_ret"][:, h].rearrange("b d e -> d b e"))\
                  .then_inc(S["rs_loaded"], 16)

            sp.wait_ge(S["ptab4"], after(16))
            for i in range(2):
                index_pages(sp, i, 0)
            sp.wait_ge(S["rope4"], after(1))
            sp.dma_start(io["k_all"][SEQ:ROWS, :], pr[:, C_KA:C_KA + P]).then_inc(S["new_out"], 16)
            sp.dma_start(io["v_all"][SEQ:ROWS, :], pr[:, C_VA:C_VA + P]).then_inc(S["new_out"], 16)
            sp.dma_start(io["ik_all"][SEQ:ROWS, :], pr[:, C_IK:C_IK + HD]).then_inc(S["new_out"], 16)
            for h in range(4):
                sp.dma_start(wcol[h * SR:(h + 1) * SR, :], pr[0:SR, C_IW + h:C_IW + h + 1]).then_inc(S["w4"], 16)
            sp.wait_ge(S["zeroed5"], after(3))
            for b in range(DB):
                sp.dma_start(vtz[0:DT, b, :], pr[b * DT:(b + 1) * DT, C_VA:C_VA + P]).then_inc(S["vt4"], 16)
            for i in range(2, HB):
                sp.wait_ge(S["kt_ps"], after(4 * (i - 1)))
                index_pages(sp, i, 0)
            sp.wait_ge(S["rs4_upd"], after(2 * RH))
            for h in range(RH):
                lo = HD * (h % 2)
                sp.dma_start(io["ret_sample"][:, h].rearrange("b d e -> d b e"), rs[lo:lo + HD, :, h, :])\
                  .then_inc(S["rs_stored"], 16)
            for i in range(HB):
                sp.wait_ge(S["kt_ps"], after(STAGE_FREE[i]))
                key_pages(sp, i, 0)
            sp.wait_ge(S["iS_ps"], after(NCH))
            for b in range(DB):
                value_pages(sp, 0, b)
            sp.wait_ge(S["og4"], after(2))
            for g in range(2):
                for r in range(4):
                    h = 4 * g + r
                    sp.dma_start(oall[:, h * HD:(h + 1) * HD], og[r * SR:(r + 1) * SR, g, :]).then_inc(S["oall4"], 16)
            sp.dma_start(io["yab_all"][SEQ + SR:ROWS, :], io["x_all"][SEQ + SR:ROWS, :]).then_inc(S["yab4"], 16)
            sp.wait_ge(S["ya4"], after(2))
            sp.dma_start(io["yab_all"][SEQ:SEQ + SR, :], tg[0:SR, :]).then_inc(S["yab4"], 16)
            sp.wait_ge(S["yab4"], after(32))
            sp.wait_ge(S["rs_stored"], after(64))
            sp.wait_ge(S["new_out"], after(48))

        @block.tensor
        def _(pe):
            pe.wait_ge(S["c4_loaded"], after(16 * N_CONST4))
            pe.wait_ge(S["rope4"], after(1))
            for n, base in enumerate((C_QA, C_QA + 256, C_IQ)):
                for r in range(4):
                    for a in range(2):
                        c0 = n * P + r * SR
                        ins = turn_half(pe, PO[0][a * HD:(a + 1) * HD, c0:c0 + SR],
                                        pr[0:SR, base + r * HD:base + (r + 1) * HD], ident[0:SR, 0:SR], a)
            ins.then_inc(S["q4_ps"], 1)
            for n, base in enumerate((C_KA, C_KA + HD, C_IK)):
                for a in range(2):
                    ins = turn_half(pe, PO[1][a * HD:(a + 1) * HD, n * SR:(n + 1) * SR],
                                    pr[0:SR, base:base + HD], ident[0:SR, 0:SR], a)
            ins.then_inc(S["q4_ps"], 1)
            for r in range(4):
                ins = pe.transpose(PA[0][:, r * P:(r + 1) * P], pr[:, C_QB + r * P:C_QB + (r + 1) * P], ident[:, :])
            ins.then_inc(S["q4_ps"], 1)
            pe.wait_ge(S["qkb4"], after(1))
            for h in range(RH):
                lo = HD * (h % 2)
                ins = pe.matmul(PS[h % 2][:, (h // 2) * P:(h // 2 + 1) * P], qkbT[lo:lo + HD, 2 + h // 2, :],
                                qkbT[lo:lo + HD, h // 2, :], start=True, stop=True)
            ins.then_inc(S["ra4_ps"], 1)
            pe.wait_ge(S["ra4_sb"], after(1))
            pe.wait_ge(S["qbm4"], after(1))
            pe.wait_ge(S["rs_loaded"], after(64))
            for h in range(RH):
                o = PA[1][0:SR, h * RV:(h + 1) * RV]
                pe.matmul(o, attm[:, h % 2, (h // 2) * P:(h // 2) * P + SR], pr[:, C_VB + h * RV:C_VB + (h + 1) * RV],
                          start=True, stop=False)
                for b in range(DB):
                    ins = pe.matmul(o, qbm[:, h // 2, b, :], rs[:, b, h, :], start=False, stop=(b == DB - 1))
            ins.then_inc(S["ro4_ps"], 1)
            pe.wait_ge(S["kd4"], after(1))
            for h in range(RH):
                pe.wait_ge(S["vm4"], after(h + 1))
                pe.wait_ge(S["rs4_upd"], after(2 * h))
                for g in range(2):
                    pe.matmul(PT[g][:, :], kd[:, h, :],
                              vm[:, h % 2, 4 * g:4 * g + 4, :].rearrange("p b d -> p (b d)"), start=True, stop=True)\
                      .then_inc(S["su4_ps"], 1)
            pe.wait_ge(S["rs4_upd"], after(2 * RH))

            def turn(units):
                for n, (slot, page, off) in enumerate(units):
                    u = turned[0] + n
                    if u >= 2:
                        pe.wait_ge(S["kt_sb%d" % (u % 2)], after(u // 2))
                    for k in range(4):
                        ins = pe.transpose(PT[u % 2][:, k * P:(k + 1) * P],
                                           stage[:, slot, page + k, off:off + P], ident[:, :])
                    ins.then_inc(S["kt_ps"], 1)
                turned[0] += len(units)

            turned = [0]
            for i in range(HB):
                pe.wait_ge(S["stage%d" % (i % 2)], after(512 * (i // 2 + 1)))
                turn([(i % 2, 4 * q, 0) for q in range(4)])
            pe.wait_ge(S["kt_sb0"], after(8))
            pe.wait_ge(S["kt_sb1"], after(8))
            pe.wait_ge(S["tails4"], after(1))
            pe.wait_ge(S["qm4"], after(3))
            for n, (c0, w) in enumerate(CHUNKS):
                if n >= 2:
                    pe.wait_ge(S["iS_sb"], after(n - 1))
                for i in range(HB):
                    ins = pe.matmul(PS[n % 2][:, 0:w], qm[:, 2, i, :], ikT[:, i, c0:c0 + w], start=(i == 0),
                                    stop=(i == HB - 1))
                ins.then_inc(S["iS_ps"], 1)
            pe.wait_ge(S["wsel4"], after(1))
            for n, (c0, w) in enumerate(CHUNKS):
                pe.wait_ge(S["iS_sb"], after(n + 1))
                if n >= 2:
                    pe.wait_ge(S["isc4"], after(n - 1))
                pe.matmul(PA[n % 2][0:SR, 0:w], wsel[:, :], sc[0][:, c0:c0 + w], start=True, stop=True)\
                  .then_inc(S["iw_ps"], 1)
            for i in range(HB):
                pe.wait_ge(S["stage%d" % (i % 2)], after(1024 + 512 * (i // 2 + 1)))
                turn([(i % 2, 4 * q, P * g) for g in range(2) for q in range(4)])
            pe.wait_ge(S["kt_sb0"], after(24))
            pe.wait_ge(S["kt_sb1"], after(24))
            pe.wait_ge(S["tails4"], after(3))
            pe.wait_ge(S["mb4"], after(1))
            pe.wait_ge(S["zeroed5"], after(3))
            for g in range(2):
                for n, (c0, w) in enumerate(CHUNKS):
                    u = g * NCH + n
                    if u >= 2:
                        pe.wait_ge(S["s4_sb"], after(u - 1))
                        pe.wait_ge(S["s4_mx"], after(u - 1))
                    for i in range(HB):
                        pe.matmul(PS[u % 2][:, 0:w], qm[:, g, i, :], K_T[g][:, i, c0:c0 + w], start=(i == 0),
                                  stop=False)
                    pe.matmul(PS[u % 2][:, 0:w], rep4[:, :], mb128[:, c0:c0 + w], start=False, stop=True)\
                      .then_inc(S["s4_ps"], 1)
            for g in range(2):
                pe.wait_ge(S["exp4"], after(g + 1))
                pe.wait_ge(S["vt4"], after(16 * DB))
                for q in range(5):
                    u = 5 * g + q
                    if u >= 2:
                        pe.wait_ge(S["pt4_sb"], after(u - 1))
                    if q < 4:
                        for k in range(4):
                            c0 = (4 * q + k) * P
                            ins = pe.transpose(PT[u % 2][:, k * P:(k + 1) * P], sc[g][:, c0:c0 + P], ident[:, :])
                    else:
                        ins = pe.transpose(PT[u % 2][0:DT, 0:P], sc[g][:, PAST:SKEYS], ident[:, :])
                    ins.then_inc(S["pt4_ps"], 1)
                    if q == 0:
                        pe.wait_ge(S["v4_0"], after(16 * 8 * DB))
                    if q == 2:
                        pe.wait_ge(S["late_values"], 16 * 8 * DB)
                    pe.wait_ge(S["pt4_sb"], after(u + 1))
                    if q < 4:
                        for k in range(4):
                            pg = 4 * q + k
                            V = (V_A, V_B)[pg // 8]
                            ins = pe.matmul(PO[g][:, :], ptT[:, u % 2, k * P:(k + 1) * P],
                                            V[:, pg % 8, :, g * HD:(g + 1) * HD], start=(pg == 0), stop=False)
                    else:
                        ins = pe.matmul(PO[g][:, :], ptz[:, g, :], vtz[:, :, g * HD:(g + 1) * HD], start=False,
                                        stop=True)
                    ins.then_inc(S["pv4"], 1)

        @block.scalar
        def _(act):
            act.wait_ge(S["ptab4"], after(16))
            for i in range(2):
                index_pages(act, i, 1)
            act.wait_ge(S["c4_loaded"], after(16 * N_CONST4))
            act.activation(tg[:, 0:512], pr[:, C_ZA:C_ZA + 512], ACT.Tanh, scale=0.5)
            act.activation(tg[:, 512:1024], pr[:, C_ZB:C_ZB + 512], ACT.Tanh, scale=0.5).then_inc(S["tanh4"], 1)
            act.wait_ge(S["q4_ps"], after(3))
            act.wait_ge(S["zeroed4"], after(2))
            act.copy(qkbT.rearrange("p h d -> p (h d)"), PA[0][:, :]).then_inc(S["qkb4"], 1)

            def evac(u, dst):
                act.wait_ge(S["kt_ps"], after(u + 1))
                act.copy(dst, PT[u % 2][:, :]).then_inc(S["kt_sb%d" % (u % 2)], 1)

            for i in range(HB):
                for q in (0, 2):
                    evac(4 * i + q, ikT[:, i, q * 512:(q + 1) * 512])
                act.wait_ge(S["kt_ps"], after(4 * (i + 1)))
                if i + 2 < HB:
                    index_pages(act, i + 2, 1)
                else:
                    key_pages(act, i + 2 - HB, 1)
            for n, (c0, w) in enumerate(CHUNKS):
                act.wait_ge(S["iS_ps"], after(n + 1))
                act.activation(sc[0][:, c0:c0 + w], PS[n % 2][:, 0:w], ACT.Relu, scale=1.0 / 16)\
                   .then_inc(S["iS_sb"], 1)
            act.wait_ge(S["ret4_done"], after(1))
            act.wait_ge(S["rs_stored"], after(64))
            for i in range(HB):
                for g in range(2):
                    for q in range(4):
                        evac(16 + 8 * i + 4 * g + q, K_T[g][:, i, q * 512:(q + 1) * 512])
                if i + 2 < HB:
                    act.wait_ge(S["kt_ps"], after(STAGE_FREE[i + 2]))
                    key_pages(act, i + 2, 1)
            act.wait_ge(S["mb4"], after(1))
            for g in range(2):
                for n, (c0, w) in enumerate(CHUNKS):
                    u = g * NCH + n
                    act.wait_ge(S["s4_mx"], after(u + 1))
                    act.copy(sc[g][:, c0:c0 + w], PS[u % 2][:, 0:w]).then_inc(S["s4_sb"], 1)
            for g in range(2):
                act.wait_ge(S["nm4"], after(g + 1))
                act.wait_ge(S["s4_sb"], after(NCH * (g + 1)))
                act.activation(sc[g][:, :], sc[g][:, :], ACT.Exp, bias=negm[:, g:g + 1], scale=HD ** -0.5,
                               accum_out=rsum[:, g:g + 1]).then_inc(S["exp4"], 1)
            for u in range(10):
                g, q = divmod(u, 5)
                act.wait_ge(S["pt4_ps"], after(u + 1))
                act.wait_ge(S["zeroed5"], after(3))
                if u >= 2:
                    act.wait_ge(S["pv4"], after(u - 1))
                if q < 4:
                    act.copy(ptT[:, u % 2, :], PT[u % 2][:, :]).then_inc(S["pt4_sb"], 1)
                else:
                    act.copy(ptz[0:DT, g, :], PT[u % 2][0:DT, 0:P]).then_inc(S["pt4_sb"], 1)

        @block.vector
        def _(dve):
            link, fresh = link_in(dve, S["dve_link"])
            dve.memset(nhalf[:, :], -0.5).then_inc(S["const4"], 1)
            dve.wait_ge(S["c4_loaded"], after(16 * N_CONST4))
            link(dve.tensor_scalar(gng, gng, 0.5, None, ALU.mult))
            x17 = pr[:, 0:17 * HD].rearrange("p (h d) -> p h d", d=HD)
            ta = rt_a[:, 0:272].rearrange("p (h d) -> p h d", d=16)
            tb = rt_b[:, 0:272].rearrange("p (h d) -> p h d", d=16)
            dve.tensor_tensor(ta, x17[:, :, 0:16], ropea[:, 0], ALU.mult)
            dve.tensor_tensor(tb[:, :, 0:8], x17[:, :, 8:16], ropea[:, 1, :, 0:8], ALU.mult)
            link(dve.tensor_tensor(tb[:, :, 8:16], x17[:, :, 0:8], ropea[:, 1, :, 8:16], ALU.mult))
            link(dve.tensor_tensor(x17[:, :, 0:16], ta, tb, ALU.add))
            x8 = pr[:, C_QB:C_QB + 512].rearrange("p (h d) -> p h d", d=HD)
            ta = rt_a.rearrange("p (h d) -> p h d", d=HD)
            tb = rt_b.rearrange("p (h d) -> p h d", d=HD)

            def row(k, a, b):
                return ropeb[:, k:k + 1, a:b].to_broadcast([P, 8, b - a])

            dve.tensor_tensor(ta, x8, row(0, 0, HD), ALU.mult)
            dve.tensor_tensor(tb[:, :, 0:32], x8[:, :, 32:64], row(1, 0, 32), ALU.mult)
            link(dve.tensor_tensor(tb[:, :, 32:64], x8[:, :, 0:32], row(1, 32, 64), ALU.mult))
            link(dve.tensor_tensor(x8, ta, tb, ALU.add))
            dve.sem_inc(S["rope4"], 1)
            dve.wait_ge(S["zeroed4"], after(2))
            for a in range(2):
                kv = kd.rearrange("p (c a) d -> p a c d", a=2)[:, a, :, a * HD:(a + 1) * HD]
                src = pr[:, C_KB:C_KB + 256].rearrange("p (c a d) -> p a c d", a=2, d=HD)[:, a]
                dec = kdec.rearrange("p (c a) -> p a c", a=2)[:, a].unsqueeze(2).to_broadcast([P, 2, HD])
                ins = dve.tensor_tensor(kv, src, dec, ALU.mult)
            ins.then_inc(S["kd4"], 1)
            dve.wait_ge(S["tanh4"], after(1))
            dve.scalar_tensor_tensor(tg[:, 0:512], tg[:, 0:512], 1.0, pr[:, C_ZA:C_ZA + 512], ALU.add, ALU.mult)
            link(dve.scalar_tensor_tensor(tg[:, 512:1024], tg[:, 512:1024], 1.0, pr[:, C_ZB:C_ZB + 512], ALU.add,
                                          ALU.mult))
            dve.wait_ge(S["q4_ps"], after(2))
            for n in range(3):
                src = PO[0][:, n * P:(n + 1) * P].rearrange("p (r t) -> p r t", t=SR).unsqueeze(1)\
                    .to_broadcast([P, HB, 4, SR])
                dve.tensor_tensor(qm[:, n].rearrange("p b (r t) -> p b r t", t=SR), src,
                                  hm[:, :, :].unsqueeze(2).to_broadcast([P, HB, 4, SR]), ALU.mult)\
                   .then_inc(S["qm4"], 1)
            dve.wait_ge(S["w4"], after(64))
            dve.tensor_scalar(wsel[:, :], rep[:, :], wcol[:, 0:1], None, ALU.mult).then_inc(S["wsel4"], 1)
            dve.wait_ge(S["qkb4"], after(1))
            dve.tensor_tensor(qbm, qkbT[:, 0:2, 0:SR].unsqueeze(2).to_broadcast([P, 2, DB, SR]), qdec, ALU.mult)\
               .then_inc(S["qbm4"], 1)
            dve.wait_ge(S["ra4_ps"], after(1))
            for a in range(2):
                ins = dve.tensor_tensor(attm[:, a, :], PS[a][:, 0:2 * P], rmask[:, a, :], ALU.mult)
            ins.then_inc(S["ra4_sb"], 1)
            for h in range(RH):
                if h >= 2:
                    dve.wait_ge(S["su4_ps"], after(2 * (h - 1)))
                vb = pr[:, C_VB + h * RV:C_VB + (h + 1) * RV].unsqueeze(1).to_broadcast([P, DB, RV])
                dve.tensor_tensor(vm[:, h % 2], vb, bsel.unsqueeze(2).to_broadcast([P, DB, RV]), ALU.mult)\
                   .then_inc(S["vm4"], 1)
                if h == 0:
                    dve.wait_ge(S["ro4_ps"], after(1))
                for g in range(2):
                    dve.wait_ge(S["su4_ps"], after(2 * h + g + 1))
                    dve.scalar_tensor_tensor(rs[:, 4 * g:4 * g + 4, h, :], rs[:, 4 * g:4 * g + 4, h, :], cdec[:, h:h + 1],
                                             PT[g][:, :].rearrange("p (b d) -> p b d", b=4), ALU.mult, ALU.add)\
                       .then_inc(S["rs4_upd"], 1)
            R32 = slice(0, SR)
            pv = PA[1][R32, :].rearrange("p (h d) -> p h d", d=RV)
            cv = gn_c[R32].rearrange("p (h d) -> p h d", d=RV)
            qv = gn_q[R32].rearrange("p (h d) -> p h d", d=RV)
            link(dve.tensor_reduce(gsum[R32], pv, AX, ALU.add))
            link(dve.tensor_scalar(gsum[R32], gsum[R32], -1.0 / RV, None, ALU.mult))
            link(dve.tensor_tensor(cv, pv, gsum[R32].unsqueeze(2).to_broadcast([SR, RH, RV]), ALU.add))
            link(dve.tensor_tensor(qv, cv, cv, ALU.mult))
            dve.tensor_reduce(gsq[R32], qv, AX, ALU.add).then_inc(S["gs4"], 1)
            dve.wait_ge(S["gr4"], after(1))
            link(dve.tensor_tensor(cv, cv, grs[R32].unsqueeze(2).to_broadcast([SR, RH, RV]), ALU.mult))
            link(dve.tensor_tensor(gn_c[R32], gn_c[R32], gng[R32], ALU.mult))
            link(dve.tensor_tensor(tg[R32, 512:1024], gn_c[R32], tg[R32, 512:1024], ALU.mult))
            dve.sem_inc(S["ret4_done"], 1)
            dve.sem_inc(S["ya4"], 1)

            def evac(u, dst):
                dve.wait_ge(S["kt_ps"], after(u + 1))
                dve.tensor_copy(dst, PT[1][:, :]).then_inc(S["kt_sb1"], 1)

            def tails(n, dst):
                for a in range(2):
                    lo = a * HD
                    src = PO[1][lo:lo + HD, n * SR + a * (SR // 2):n * SR + (a + 1) * (SR // 2)]
                    ins = dve.tensor_copy(dst[lo:lo + HD, :, PAST:SKEYS], src.rearrange("p (b t) -> p b t", t=DT))
                ins.then_inc(S["tails4"], 1)

            tails(2, ikT)
            for i in range(HB):
                for q in (1, 3):
                    evac(4 * i + q, ikT[:, i, q * 512:(q + 1) * 512])
            for n, (c0, w) in enumerate(CHUNKS):
                dve.wait_ge(S["iw_ps"], after(n + 1))
                dve.tensor_copy(isc[:, c0:c0 + w], PA[n % 2][0:SR, 0:w]).then_inc(S["isc4"], 1)
            dve.wait_ge(S["rs_stored"], after(64))
            tails(0, K_T[0])
            tails(1, K_T[1])
            dve.wait_ge(S["isc4"], after(NCH))
            pw = pow2[R32]
            hv = halves[R32]
            link(dve.tensor_reduce(lo_b, isc[:, :], AX, ALU.min))
            link(dve.tensor_reduce(hi_b, isc[:, :], AX, ALU.max))
            tail = isc[:, PAST:SKEYS]
            link(dve.tensor_tensor(tail, tail, tmask[:, :], ALU.add))
            link(dve.tensor_scalar(lo_b, lo_b, 0.0, None, ALU.min))
            link(dve.tensor_scalar(hi_b, hi_b, 0.0, 1e-20, ALU.max, ALU.add))
            link(dve.tensor_tensor(rng_, hi_b, lo_b, ALU.subtract))
            link(dve.tensor_scalar(hv, pw, rng_, None, ALU.mult))
            link(dve.tensor_tensor(mid, lo_b, hv[:, 0:1], ALU.add))
            dve.wait_ge(S["zeroed5"], after(3))
            for n in range(STEPS):
                link(dve.tensor_scalar(mb[:, :], isc[:, :], mid, 0.0, ALU.is_gt, ALU.add, accum_out=cnt))
                link(dve.tensor_scalar(ph, cnt, TOPK - 0.5, hv[:, n:n + 1], ALU.is_ge, ALU.mult))
                link(dve.scalar_tensor_tensor(mid, ph, hv[:, n + 1:n + 2], mid, ALU.subtract, ALU.add))
            w = hv[:, STEPS - 3:STEPS - 2]
            link(dve.tensor_tensor(hi_c, mid, w, ALU.add))
            link(dve.tensor_tensor(lo_c, mid, w, ALU.subtract))
            above, band, order = sc[0][R32, :], sc[1][R32, :], isc[:, :]
            dve.wait_ge(S["iw_ps"], after(NCH))
            link(dve.tensor_scalar(above, isc[:, :], hi_c, 0.0, ALU.is_gt, ALU.add, accum_out=cgt))
            link(dve.tensor_scalar(need, cgt, -1.0, float(TOPK), ALU.mult, ALU.add))
            link(dve.scalar_tensor_tensor(band, isc[:, :], lo_c, above, ALU.is_gt, ALU.subtract))
            link(dve.tensor_tensor_scan(order, band, band, 0.0, ALU.add, ALU.bypass))
            link(dve.scalar_tensor_tensor(band, order, need, band, ALU.is_le, ALU.mult))
            link(dve.tensor_tensor(band, band, above, ALU.add))
            dve.tensor_scalar(mb[:, :], band, BIG, -BIG, ALU.mult, ALU.add).then_inc(S["mb4"], 1)
            for g in range(2):
                for n, (c0, w) in enumerate(CHUNKS):
                    u = g * NCH + n
                    dve.wait_ge(S["s4_ps"], after(u + 1))
                    dve.tensor_reduce(mx8[:, u:u + 1], PS[u % 2][:, 0:w], AX, ALU.max).then_inc(S["s4_mx"], 1)
                dve.wait_ge(S["s4_mx"], after(NCH * (g + 1)))
                link(dve.tensor_reduce(mx1[:, g:g + 1], mx8[:, g * NCH:(g + 1) * NCH], AX, ALU.max))
                dve.tensor_scalar(negm[:, g:g + 1], mx1[:, g:g + 1], -HD ** -0.5, None, ALU.mult).then_inc(S["nm4"], 1)
            dve.wait_ge(S["exp4"], after(2))
            link(dve.reciprocal(rinv, rsum))
            od = ptd[:, :].rearrange("p (b d) -> p b d", b=DB)
            for g in range(2):
                dve.wait_ge(S["pv4"], after(5 * (g + 1)))
                link(dve.tensor_tensor(od, PO[g][:, :].rearrange("p (b d) -> p b d", b=DB),
                                       dsel[:, :].unsqueeze(2).to_broadcast([P, DB, HD]), ALU.mult))
                link(dve.tensor_reduce(og[:, g, :], ptd[:, :].rearrange("p (b d) -> p d b", b=DB), AX, ALU.add))
                dve.tensor_scalar(og[:, g, :], og[:, g, :], rinv[:, g:g + 1], None, ALU.mult).then_inc(S["og4"], 1)
            dve.wait_ge(S["oall4"], after(16 * AH))
            dve.scalar_tensor_tensor(tg[R32, 0:512], oall[:, :], 0.5, tg[R32, 0:512], ALU.mult, ALU.mult)\
               .then_inc(S["ya4"], 1)

        @block.gpsimd
        def _(pool):
            link, fresh = link_in(pool, S["pool_link"])
            pool.memset(rs, 0.0).then_inc(S["zeroed4"], 1)
            for z in (mb128[:, :], ptz[:, :, :], vtz[:, :, :]):
                pool.memset(z, 0.0).then_inc(S["zeroed5"], 1)
            pool.memset(kd, 0.0).then_inc(S["zeroed4"], 1)
            pool.wait_ge(S["gs4"], after(1))
            pool.wait_ge(S["const4"], after(1))
            link(pool.tensor_scalar(grs[0:SR], gsq[0:SR], 1.0 / RV, EPS, ALU.mult, ALU.add))
            pool.tensor_tensor(grs[0:SR], grs[0:SR], nhalf[0:SR, :], ALU.pow).then_inc(S["gr4"], 1)
            pool.wait_ge(S["ptab4"], after(16))
            pool.wait_ge(S["kt_ps"], after(48))
            for b in range(DB):
                value_pages(pool, 1, b)


def layer0_out_and_conv(nc, io, S, ab_all):
    ctx = ExitStack()
    with ctx:
        def sb(name, shape, dt=FP):
            return ctx.enter_context(nc.sbuf_tensor(name, shape, dt))

        def ps(name):
            return ctx.enter_context(nc.psum_tensor(name, [P, 512], FP))

        w_c = sb("w_c", [P, KD, CIN])
        w_o = sb("w_o", [P, KD, D])
        hT = sb("hT2", [P, KD, GT * P])
        yab = sb("yab2", [P, D])
        hn = sb("hn", [P, D])
        xin = sb("xin", [P, D])
        y1 = sb("y1", [P, D])
        sx = sb("sx", [P, DB * (DT + 3)])
        yT = sb("yT", [P, KD, P])
        raw = sb("raw", [P, 2, 3 + GT * P])
        cva = sb("cva", [P, 2, GT * P])
        cvt = sb("cvt", [P, GT * P])
        crow = sb("crow", [P, 2, GT * P])
        tails = sb("tails", [P, NBLK, 3])
        cw = sb("cw", [P, CONV, NBLK])
        ident = sb("ident2", [P, P])
        nw1 = sb("nw1", [P, KD])
        gn = sb("gn_t", [P, P])
        zg = sb("zg", [P, 512])
        pre = sb("pre", [P, NBLK, DB * 3])
        nhalf = sb("nhalf2", [P, 1])
        stat = sb("stat2", [P, 2])
        ssum, rstd = stat[:, 0:1], stat[:, 1:2]
        crw = sb("crw", [DB * 3, CC])
        PA = [ps("QA0"), ps("QA1")]
        PS = [ps("QS0"), ps("QS1")]
        PT = [ps("QT0"), ps("QT1")]
        PB = [ps("QB0"), ps("QB1")]
        block = ctx.enter_context(nc.Block())
        NSUB = NT + 1
        NB_ALL = NBLK * (GROUPS + 1)

        Z_CUTS = [(CC, CC + 512), (CC + 512, CC + 1024), (CC + 1024, CIN)]

        @block.sync
        def _(sp):
            for c in range(KD):
                sp.dma_start(w_o[:, c, :], io["w_out_ab"][c * P:(c + 1) * P, :]).then_inc(S["w2o_loaded"], 16)
            for dst, src in ((ident, io["ident"]),
                             (nw1, io["norm_w"][1:2, :].rearrange("a (c p) -> p (a c)", p=P)),
                             (gn, io["gdn_norm"].partition_broadcast(P))):
                sp.dma_start(dst[:, :], src, allow_slow_non_contiguous=True).then_inc(S["c2_loaded"], 16)
            for k in range(CONV):
                sp.dma_start(cw[:, k, :], io["conv_w"][k:k + 1, :].rearrange("a (c p) -> p (a c)", p=P),
                             allow_slow_non_contiguous=True).then_inc(S["c2_loaded"], 16)

            def sub_in(T):
                sp.wait_ge(S["yT_ps"], after(2 * T))
                sp.dma_start(yab[:, :], io["yab_all"][ds(T * P, P), :]).then_inc(S["yab2_loaded"], 16)
                sp.wait_ge(S["y1_ready"], after(2 * T))
                sp.dma_start(xin[:, :], io["x_all"][ds(T * P, P), :]).then_inc(S["x2_loaded"], 16)

            def sub_out(T):
                sp.wait_ge(S["y1_ready"], after(2 * T + 2))
                sp.dma_start(io["y1_all"][ds(T * P, P), :], y1[:, :]).then_inc(S["y1_stored"], 16)

            def z_out(T):
                for k in range(2):
                    sp.wait_ge(S["zg_ready"], after(2 * T + k + 1))
                    sp.dma_start(io["zg_all"][ds(T * P, P), k * 512:(k + 1) * 512], zg[:, :])\
                      .then_inc(S["zg_stored"], 16)

            def blocks(G, n):
                for b in range(NBLK):
                    u = NBLK * G + b
                    sp.wait_ge(S["crow_ready"], after(u + 1))
                    for s in range(n):
                        sp.dma_start(io["c_all"][ds((G * GT + s) * P, P), b * P:(b + 1) * P],
                                     crow[:, b % 2, s * P:(s + 1) * P]).then_inc(S["c_stored%d" % (b % 2)], 16)

            def group(G, n):
                for s in range(n + 1):
                    if s < n:
                        sub_in(G * GT + s)
                        sub_out(G * GT + s)
                    if s:
                        z_out(G * GT + s - 1)
                blocks(G, n)

            with sp.Fori(0, GROUPS) as G:
                group(G, GT)
            sp.wait_ge(S["cs_ready"], after(4))
            sp.dma_start(io["conv_prompt"], crw[0:3, :]).then_inc(S["cv_stored"], 16)
            sp.wait_ge(S["cv_stored"], after(16))
            sp.dma_start(crw[:, :], io["state_conv"]).then_inc(S["pre_loaded"], 16)
            group(GROUPS, 1)
            sp.wait_ge(S["cs_ready"], after(8))
            sp.dma_start(io["conv_sample"], crw[:, :]).then_inc(S["cv_stored"], 16)
            sp.wait_ge(S["cv_stored"], after(32))
            sp.wait_ge(S["y1_stored"], after(16 * NSUB))
            sp.wait_ge(S["zg_stored"], after(32 * NSUB))
            for k in range(2):
                sp.wait_ge(S["c_stored%d" % k], after(16 * NBLK // 2 * (NT + 1)))

        @block.tensor
        def _(pe):
            def out_proj(T):
                pe.wait_ge(S["yab2_loaded"], after(16 * (T + 1)))
                pe.wait_ge(S["hT2_sb"], after(2 * T))
                for u in range(2):
                    for k in range(4):
                        c = 4 * u + k
                        ins = pe.transpose(PT[u][:, k * P:(k + 1) * P], yab[:, c * P:(c + 1) * P], ident[:, :])
                    ins.then_inc(S["yT_ps"], 1)
                pe.wait_ge(S["yT_sb"], after(2 * T + 2))
                pe.wait_ge(S["y1_ready"], after(2 * T))
                for n in range(2):
                    for c in range(KD):
                        ins = pe.matmul(PS[n][:, :], yT[:, c, :], w_o[:, c, n * 512:(n + 1) * 512],
                                        start=(c == 0), stop=(c == KD - 1))
                    ins.then_inc(S["y1_ps"], 1)

            def turn_h(T, s):
                pe.wait_ge(S["hn2_ready"], after(T + 1))
                pe.wait_ge(S["yT_sb"], after(2 * T + 2))
                for u in range(2):
                    for k in range(4):
                        c = 4 * u + k
                        ins = pe.transpose(PT[u][:, k * P:(k + 1) * P], hn[:, c * P:(c + 1) * P], ident[:, :])
                    ins.then_inc(S["hT2_ps"], 1)

            def z_proj(T, s):
                pe.wait_ge(S["hT2_sb"], after(2 * T + 2))
                pe.wait_ge(S["w2c_loaded"], after(16 * KD))
                for n, (a, b) in enumerate(Z_CUTS):
                    if n < 2:
                        pe.wait_ge(S["z_free"], after(3 * T))
                    else:
                        pe.wait_ge(S["z_free"], after(3 * T + 1))
                    for c in range(KD):
                        ins = pe.matmul(PA[n % 2][:, 0:b - a], hT[:, c, s * P:(s + 1) * P], w_c[:, c, a:b],
                                        start=(c == 0), stop=(c == KD - 1))
                    ins.then_inc(S["z_ps"], 1)

            def blocks(G, n):
                N = n * P
                for b in range(NBLK + 2):
                    u = G * NBLK + b
                    if b < NBLK:
                        pe.wait_ge(S["raw_ready"], after(u - 1) if b >= 2 else after(G * NBLK))
                        for c in range(KD):
                            ins = pe.matmul(PB[b % 2][:, 0:N], w_c[:, c, b * P:(b + 1) * P], hT[:, c, 0:N],
                                            start=(c == 0), stop=(c == KD - 1))
                        ins.then_inc(S["blk_ps"], 1)
                    if b >= 2:
                        v = u - 2
                        pe.wait_ge(S["cv_ready"], after(v + 1))
                        if b >= 4:
                            pe.wait_ge(S["crow_ready"], after(v - 1))
                        elif b == 2:
                            pe.wait_ge(S["z_free"], after(3 * (G * GT + n)))
                        for s in range(n):
                            ins = pe.transpose(PA[b % 2][:, s * P:(s + 1) * P], cva[:, b % 2, s * P:(s + 1) * P],
                                               ident[:, :])
                        ins.then_inc(S["crow_ps"], 1)

            def group(G, n):
                for s in range(n + 1):
                    T = G * GT + s
                    if s < n:
                        out_proj(T)
                    if s:
                        z_proj(T - 1, s - 1)
                    if s < n:
                        if s == 0:
                            pe.wait_ge(S["crow_ready"], after(G * NBLK))
                        turn_h(T, s)
                blocks(G, n)

            def conv_state(src, width, k):
                for q in range(4):
                    pe.wait_ge(S["cs_ready"], after(4 * k + q))
                    for i in range(4):
                        ins = pe.transpose(PT[0][0:width, i * P:(i + 1) * P], src(4 * q + i), ident[:, :])
                    ins.then_inc(S["cs_ps"], 1)

            pe.wait_ge(S["w2o_loaded"], after(16 * KD))
            pe.wait_ge(S["c2_loaded"], after(16 * 7))
            with pe.Fori(0, GROUPS) as G:
                group(G, GT)
            pe.wait_ge(S["tail_kept"], after(NBLK * GROUPS))
            pe.wait_ge(S["hT2_sb"], after(2 * NT))
            conv_state(lambda b: tails[:, b, :], 3, 0)
            pe.wait_ge(S["pre_loaded"], after(16))
            pe.wait_ge(S["cs_ready"], after(4))
            for b in range(NBLK):
                ins = pe.transpose(PT[1][:, b * 24:(b + 1) * 24], crw[:, b * P:(b + 1) * P], ident[0:24, 0:24])
            ins.then_inc(S["pre_ps"], 1)
            pe.wait_ge(S["pre_ready"], after(1))
            group(GROUPS, 1)
            pe.wait_ge(S["pre_kept"], after(NBLK))
            pe.wait_ge(S["hT2_sb"], after(2 * NT + 2))
            conv_state(lambda b: pre[:, b, :], DB * 3, 1)

        @block.scalar
        def _(act):
            def z_gate(T, G):
                for n in range(2):
                    act.wait_ge(S["z_ps"], after(3 * T + n + 1))
                    act.wait_ge(S["cv_ready"], after(G * NBLK))
                    act.wait_ge(S["z_free"], after(3 * T + n))
                    act.activation(cvt[:, 0:512], PA[n][:, :], ACT.Tanh, scale=0.5).then_inc(S["zt_ready"], 1)

            def blocks(G, n):
                N = n * P
                act.wait_ge(S["z_free"], after(3 * (G * GT + n)))
                for b in range(NBLK):
                    u = G * NBLK + b
                    act.wait_ge(S["blk_ps"], after(u + 1))
                    act.wait_ge(S["tail_kept"], after(u - 1) if b >= 2 else after(G * NBLK))
                    act.wait_ge(S["cvh_ready"], after(u - 1) if b >= 2 else after(G * NBLK))
                    act.copy(raw[:, b % 2, 3:3 + N], PB[b % 2][:, 0:N]).then_inc(S["raw_ready"], 1)
                    if b:
                        tanh_and_rows(u - 1, b - 1, N)
                tanh_and_rows(G * NBLK + NBLK - 1, NBLK - 1, N)

            def tanh_and_rows(u, b, N):
                act.wait_ge(S["cvh_ready"], after(u + 1))
                act.wait_ge(S["cv_ready"], after(u))
                act.activation(cvt[:, 0:N], cva[:, b % 2, 0:N], ACT.Tanh).then_inc(S["cvt_ready"], 1)

            def group(G, n):
                for s in range(n + 1):
                    T = G * GT + s
                    if s < n:
                        sub_front(T)
                    if s:
                        z_gate(T - 1, G)
                    if s < n:
                        sub_back(T, s)
                blocks(G, n)

            def sub_front(T):
                for u in range(2):
                    act.wait_ge(S["yT_ps"], after(2 * T + u + 1))
                    act.copy(yT[:, 4 * u:4 * u + 4, :].rearrange("p c t -> p (c t)"), PT[u][:, :])\
                       .then_inc(S["yT_sb"], 1)
                act.wait_ge(S["y1_ready"], after(2 * T + 2))
                act.wait_ge(S["hT2_ps"], after(2 * T))
                act.activation(hn[:, :], y1[:, :], ACT.Square, accum_out=ssum).then_inc(S["ss2_ready"], 1)
                act.wait_ge(S["ss2_ready"], after(T + 1))
                act.wait_ge(S["rstd2_ready"], after(T + 1))
                act.activation(hn[:, :], y1[:, :], ACT.Copy, scale=rstd).then_inc(S["hn2_ready"], 1)

            def sub_back(T, s):
                for u in range(2):
                    act.wait_ge(S["hT2_ps"], after(2 * T + u + 1))
                    for k in range(4):
                        c = 4 * u + k
                        ins = act.activation(hT[:, c, s * P:(s + 1) * P], PT[u][:, k * P:(k + 1) * P], ACT.Copy,
                                             scale=nw1[:, c:c + 1])
                    ins.then_inc(S["hT2_sb"], 1)

            act.wait_ge(S["w2o_loaded"], after(16 * KD))
            for c in range(KD):
                act.dma_start(w_c[:, c, :], io["w_in_c"][c * P:(c + 1) * P, :]).then_inc(S["w2c_loaded"], 16)
            act.wait_ge(S["c2_loaded"], after(16 * 7))
            with act.Fori(0, GROUPS) as G:
                group(G, GT)
            for q in range(4):
                act.wait_ge(S["cs_ps"], after(q + 1))
                act.copy(crw[0:3, q * 512:(q + 1) * 512], PT[0][0:3, :]).then_inc(S["cs_ready"], 1)
            group(GROUPS, 1)
            for q in range(4):
                act.wait_ge(S["cs_ps"], after(4 + q + 1))
                act.copy(crw[:, q * 512:(q + 1) * 512], PT[0][0:DB * 3, :]).then_inc(S["cs_ready"], 1)

        @block.vector
        def _(dve):
            link, fresh = link_in(dve, S["dve_link"])

            def residual(T):
                dve.wait_ge(S["x2_loaded"], after(16 * (T + 1)))
                for n in range(2):
                    dve.wait_ge(S["y1_ps"], after(2 * T + n + 1))
                    dve.wait_ge(S["y1_stored"], after(16 * T))
                    dve.wait_ge(S["hn2_ready"], after(T))
                    dve.tensor_tensor(y1[:, n * 512:(n + 1) * 512], xin[:, n * 512:(n + 1) * 512], PS[n][:, :],
                                      ALU.add).then_inc(S["y1_ready"], 1)

            def z_gate(T):
                for n in range(2):
                    dve.wait_ge(S["zt_ready"], after(2 * T + n + 1))
                    dve.wait_ge(S["zg_stored"], after(16 * (2 * T + n)))
                    dve.scalar_tensor_tensor(zg[:, :], cvt[:, 0:512], 1.0, PA[n][:, :], ALU.add, ALU.mult)\
                       .then_inc(S["z_free"], 1)
                    dve.wait_ge(S["z_free"], after(3 * T + n + 1))
                    dve.tensor_tensor(zg[:, :].rearrange("p (h d) -> p h d", d=P),
                                      zg[:, :].rearrange("p (h d) -> p h d", d=P),
                                      gn[:, :].unsqueeze(1).to_broadcast([P, 4, P]), ALU.mult)\
                       .then_inc(S["zg_ready"], 1)
                dve.wait_ge(S["z_ps"], after(3 * T + 3))
                dve.tensor_copy(ab_all[:, ds(T, 1), :], PA[0][:, 0:16].unsqueeze(1)).then_inc(S["z_free"], 1)

            def blocks(G, n, sample=False):
                N = n * P
                fresh()
                for b in range(NBLK):
                    u = G * NBLK + b
                    dve.wait_ge(S["raw_ready"], after(u + 1))
                    if b >= 2:
                        dve.wait_ge(S["crow_ps"], after(u - 1))
                    r = raw[:, b % 2, :]
                    a = cva[:, b % 2, 0:N]
                    if sample:
                        rv = r[:, 3:3 + SR].rearrange("p (b t) -> p b t", t=DT)
                        xv = sx[:, :].rearrange("p (b t) -> p b t", t=DT + 3)
                        dve.tensor_copy(xv[:, :, 0:3], pre[:, b, :].rearrange("p (b t) -> p b t", t=3))
                        link(dve.tensor_copy(xv[:, :, 3:7], rv))
                        av = cva[:, b % 2, 0:SR].rearrange("p (b t) -> p b t", t=DT)
                        link(dve.tensor_scalar(av, xv[:, :, 0:DT], cw[:, 0, b:b + 1], None, ALU.mult))
                        for k in range(1, CONV):
                            ins = dve.scalar_tensor_tensor(av, xv[:, :, k:k + DT], cw[:, k, b:b + 1], av, ALU.mult,
                                                           ALU.add)
                            if k < CONV - 1:
                                link(ins)
                        ins.then_inc(S["cvh_ready"], 1)
                        dve.tensor_copy(pre[:, b, :].rearrange("p (b t) -> p b t", t=3), xv[:, :, 4:7])\
                           .then_inc(S["pre_kept"], 1)
                        dve.wait_ge(S["pre_kept"], after(b + 1))
                        dve.sem_inc(S["tail_kept"], 1)
                    else:
                        link(dve.tensor_copy(r[:, 0:3], tails[:, b, :]))
                        link(dve.tensor_scalar(a, r[:, 0:N], cw[:, 0, b:b + 1], None, ALU.mult))
                        for k in range(1, CONV):
                            ins = dve.scalar_tensor_tensor(a, r[:, k:k + N], cw[:, k, b:b + 1], a, ALU.mult, ALU.add)
                            if k < CONV - 1:
                                link(ins)
                        ins.then_inc(S["cvh_ready"], 1)
                        dve.tensor_copy(tails[:, b, :], r[:, N:N + 3]).then_inc(S["tail_kept"], 1)
                    if b:
                        silu(u - 1, b - 1, N)
                    if b >= 3:
                        rows(G, u - 3, b - 3, N)
                silu(G * NBLK + NBLK - 1, NBLK - 1, N)
                for b in range(NBLK - 3, NBLK):
                    rows(G, G * NBLK + b, b, N)

            def silu(u, b, N):
                dve.wait_ge(S["cvt_ready"], after(u + 1))
                dve.scalar_tensor_tensor(cva[:, b % 2, 0:N], cvt[:, 0:N], 1.0, cva[:, b % 2, 0:N], ALU.add, ALU.mult)\
                   .then_inc(S["cv_ready"], 1)

            def rows(G, u, b, N):
                dve.wait_ge(S["crow_ps"], after(u + 1))
                before = (16 * GT * (GROUPS * NBLK // 2) + 16 * (b // 2)) if N == P else 16 * GT * (G * (NBLK // 2) + b // 2)
                dve.wait_ge(S["c_stored%d" % (b % 2)], after(before))
                dve.tensor_copy(crow[:, b % 2, 0:N], PA[b % 2][:, 0:N]).then_inc(S["crow_ready"], 1)

            def group(G, n, sample=False):
                for s in range(n + 1):
                    if s < n:
                        residual(G * GT + s)
                    if s:
                        z_gate(G * GT + s - 1)
                blocks(G, n, sample)

            dve.memset(nhalf[:, :], -0.5).then_inc(S["const2_ready"], 1)
            dve.memset(tails[:, :, :], 0.0).then_inc(S["const2_ready"], 1)
            dve.wait_ge(S["c2_loaded"], after(16 * 7))
            dve.tensor_scalar(cw[:, :, :], cw[:, :, :], 0.5, None, ALU.mult).then_inc(S["const2_ready"], 1)
            dve.tensor_scalar(gn[:, :], gn[:, :], 0.5, None, ALU.mult).then_inc(S["const2_ready"], 1)
            dve.memset(cva[:, :, :], 0.0).then_inc(S["const2_ready"], 1)
            dve.wait_ge(S["const2_ready"], after(5))
            with dve.Fori(0, GROUPS) as G:
                group(G, GT)
            dve.wait_ge(S["pre_ps"], after(1))
            dve.tensor_copy(pre[:, :, :].rearrange("p b t -> p (b t)"), PT[1][:, 0:NBLK * 24])\
               .then_inc(S["pre_ready"], 1)
            dve.wait_ge(S["pre_ready"], after(1))
            group(GROUPS, 1, True)

        @block.gpsimd
        def _(pool):
            link, fresh = link_in(pool, S["pool_link"])
            pool.wait_ge(S["const2_ready"], after(5))
            with pool.Fori(0, NSUB) as T:
                fresh()
                pool.wait_ge(S["ss2_ready"], after(T + 1))
                link()
                link(pool.tensor_scalar(rstd, ssum, 1.0 / D, EPS, ALU.mult, ALU.add))
                pool.tensor_tensor(rstd, rstd, nhalf[:, 0:1], ALU.pow).then_inc(S["rstd2_ready"], 1)


GH = 8
LEVELS = 7
SAMPLE_LEVELS = 2
QT_G, QT_BETA, QT_GC, QT_EGC, QT_EKT, QT_EGL = range(6)


def tri_constants(size):
    f = np.float32
    j, i = np.arange(P)[:, None], np.arange(P)[None]
    same = j // size == i // size
    tri = (same & (j <= i)).astype(f)
    strict = (same & (j < i)).astype(f)
    levels = [((i >> n) % 2 == 1) & ((j >> n) == (i >> n) - 1) & same for n in range(LEVELS)]
    return np.concatenate([tri, strict, same.astype(f)] + [m.astype(f) for m in levels], 1)


def layer1_delta(nc, io, S, ab_all):
    ctx = ExitStack()
    with ctx:
        def sb(name, shape, dt=FP):
            return ctx.enter_context(nc.sbuf_tensor(name, shape, dt))

        def ps(name):
            return ctx.enter_context(nc.psum_tensor(name, [P, 512], FP))

        def heads(name):
            return sb(name, [P, GH, P])

        w_co = sb("w_co", [P, KD, D])
        state = heads("state")
        tc = sb("tri_t", [P, 3 + LEVELS, P])
        tcs = sb("tris_t", [P, 3 + LEVELS, P])
        ident = sb("ident3", [P, P])
        fng = sb("fng", [P, D])
        alog = sb("alog", [P, GH])
        dtb = sb("dtb", [P, GH])
        q_all = sb("q_all", [P, NT + 1, 6, GH])
        cur = sb("cur", [P, 6, GH])
        begc = sb("begc", [P, GH])
        spa = sb("spa", [P, NT + 1, GH])
        spb = sb("spb", [P, NT + 1, GH])
        spc = sb("spc", [P, NT + 1, GH])
        nhalf = sb("nhalf3", [P, GH])
        qks = sb("qks", [P, GH])
        st = sb("stat3", [P, 4 * GH])
        ss8, rs8, os8, or8 = [st[:, k * GH:(k + 1) * GH] for k in range(4)]
        fst = sb("fst", [P, 2])
        cin = sb("cin", [P, CC])
        zgt = sb("zgt", [P, D])
        y1t = sb("y1t", [P, D])
        y2 = sb("y2", [P, D])
        yo = sb("yo", [P, D])
        sq = sb("sq3", [P, D])
        qkn, qkT, dec, dst, MT, QKD = [heads(n) for n in ("qkn", "qkT", "dec", "dst", "MT", "QKD")]
        ML = sb("ML", [P, 2, GH, P])
        X, XT, P1, bv, kt, R, vn, qs, o, oT = [heads(n) for n in
                                               ("X", "XT", "P1", "bv", "kt", "R", "vn", "qsd", "o", "oT")]
        PA = [ps("RA0"), ps("RA1")]
        PS = [ps("RS0"), ps("RS1")]
        PT = [ps("RT0"), ps("RT1")]
        PB = [ps("RB0"), ps("RB1")]
        sq2 = sb("sq2", [P, D], BF)
        sg = sb("sg", [P, DB, GH, P])
        qkm = sb("qkm", [P, DB, GH, SR])
        vnm = sb("vnm", [SR, 2, DB, P])
        bsel = sb("bsel_t", [P, 2 * DB])
        eglm = sb("eglm", [P, DB, GH])
        eglb = sb("eglb", [P, DB, GH])
        block = ctx.enter_context(nc.Block())

        def flat(x):
            return x[:, :, :].rearrange("p h d -> p (h d)")

        def half(x, g):
            return x[:, 4 * g:4 * g + 4, :].rearrange("p h d -> p (h d)")

        def quad(x, g):
            return x[:, 4 * g:4 * g + 4, :]

        def bank(x):
            return x[:, :].rearrange("p (h d) -> p h d", d=P)

        def col(v, n=P):
            return v.unsqueeze(2).to_broadcast([P, v.shape[1], n])

        def over(m, n):
            return m.unsqueeze(1).to_broadcast([P, n, P])

        @block.sync
        def _(sp):
            for dst_, src in ((ident[:, :], io["ident"]), (tc[:, :, :].rearrange("p a b -> p (a b)"), io["tri"]),
                              (tcs[:, :, :].rearrange("p a b -> p (a b)"), io["tri_s"]),
                              (fng[:, :], io["final_norm"].partition_broadcast(P)),
                              (alog[:, :], io["a_log"].partition_broadcast(P)),
                              (dtb[:, :], io["dt_bias"].partition_broadcast(P)),
                              (qks[:, :], io["qk_scale"]), (bsel[:, :], io["bsel"])):
                sp.dma_start(dst_, src, allow_slow_non_contiguous=True).then_inc(S["c3_loaded"], 16)

            def tile(t):
                sp.wait_ge(S["bv_ready"], after(t))
                sp.wait_ge(S["qkn_ready"], after(t))
                sp.wait_ge(S["qk_sq"], after(t))
                sp.dma_start(cin[:, :], io["c_all"][ds(t * P, P), :]).then_inc(S["cin_loaded"], 16)

            def tile_late(t):
                sp.wait_ge(S["y2_ready"], after(2 * t))
                sp.dma_start(y1t[:, :], io["y1_all"][ds(t * P, P), :]).then_inc(S["y13_loaded"], 16)

            def gate_rows(t):
                sp.wait_ge(S["og_ready"], after(t))
                sp.dma_start(zgt[:, :], io["zg_all"][ds(t * P, P), :]).then_inc(S["zg3_loaded"], 16)

            def store(t):
                sp.wait_ge(S["yo_ready"], after(t + 1))
                sp.dma_start(io["y_all"][ds(t * P, P), :], yo[:, :]).then_inc(S["yo_stored"], 16)

            tile(0)
            gate_rows(0)
            for c in range(KD):
                sp.dma_start(w_co[:, c, :], io["w_out_c"][c * P:(c + 1) * P, :]).then_inc(S["w3_loaded"], 16)
            for b in range(DB):
                sp.dma_start(sg[:, b], io["state_gdn"][b].rearrange("h d e -> d h e")).then_inc(S["sg_loaded"], 16)

            def step(t, first=False):
                tile(t + 1)
                tile_late(t)
                gate_rows(t + 1)
                if not first:
                    store(t - 1)

            step(0, True)
            with sp.Fori(1, NT) as t:
                step(t)
            tile_late(NT)
            store(NT - 1)
            sp.wait_ge(S["st_upd"], after(NT))
            sp.dma_start(io["gdn_prompt"].rearrange("h d e -> d h e"), state[:, :, :]).then_inc(S["st_stored"], 16)
            store(NT)
            for b in range(DB):
                sp.wait_ge(S["sg_upd"], after(16))
                sp.dma_start(io["gdn_sample"][b].rearrange("h d e -> d h e"), sg[:, b])\
                  .then_inc(S["st_stored"], 16)
            sp.wait_ge(S["yo_stored"], after(16 * (NT + 1)))
            sp.wait_ge(S["st_stored"], after(16 * (DB + 1)))

        def tile_masks(sample):
            return tcs if sample else tc

        @block.tensor
        def _(pe):
            def front(t, sample):
                m = tile_masks(sample)
                pe.wait_ge(S["cur_ready"], after(t + 1))
                pe.wait_ge(S["o_ready"], after(2 * t))
                for g in range(2):
                    for k in range(4):
                        ins = pe.matmul(PS[g][:, k * P:(k + 1) * P],
                                        cur[:, QT_G, 4 * g + k:4 * g + k + 1].to_broadcast([P, P]), m[:, 0, :],
                                        start=True, stop=True)
                    ins.then_inc(S["gcb_ps"], 1)
                pe.wait_ge(S["st_upd"], after(t))
                for g in range(2):
                    for k in range(4):
                        ins = pe.matmul(PT[g][:, k * P:(k + 1) * P],
                                        cur[:, QT_BETA, 4 * g + k:4 * g + k + 1].to_broadcast([P, P]), ident[:, :],
                                        start=True, stop=True)
                    ins.then_inc(S["bb_ps"], 1)
                pe.wait_ge(S["qkn_ready"], after(t + 1))
                for g in range(2):
                    for k in range(4):
                        h = 4 * g + k
                        ins = pe.transpose(PA[g][:, k * P:(k + 1) * P], qkn[:, h, :], ident[:, :])
                    ins.then_inc(S["qkT_ps"], 1)
                pe.wait_ge(S["qkT_ready"], after(2 * t + 2))
                pe.wait_ge(S["oT_ready"], after(2 * t))
                for k in range(4):
                    ins = pe.matmul(PB[0][:, k * P:(k + 1) * P], qkT[:, 4 + k, :], qkT[:, 4 + k, :], start=True,
                                    stop=True)
                ins.then_inc(S["kk_ps"], 1)
                for k in range(4):
                    ins = pe.matmul(PB[1][:, k * P:(k + 1) * P], qkT[:, 4 + k, :], qkT[:, k, :], start=True,
                                    stop=True)
                ins.then_inc(S["qk_ps"], 1)

            def state_reads(t):
                pe.wait_ge(S["st_upd"], after(t))
                pe.wait_ge(S["MT_ready"], after(t + 1))
                pe.wait_ge(S["QKD_ready"], after(t + 1))
                for k in range(4):
                    ins = pe.matmul(PB[k // 2][:, (k % 2) * 256:(k % 2 + 1) * 256], qkT[:, 4 + k, :],
                                    state[:, 2 * k:2 * k + 2, :].rearrange("p h d -> p (h d)"), start=True,
                                    stop=True)
                ins.then_inc(S["ks_ps"], 1)

            def query_reads(t):
                pe.wait_ge(S["ks_read"], after(t + 1))
                for k in range(4):
                    ins = pe.matmul(PB[k // 2][:, (k % 2) * 256:(k % 2 + 1) * 256], qkT[:, k, :],
                                    state[:, 2 * k:2 * k + 2, :].rearrange("p h d -> p (h d)"), start=True,
                                    stop=True)
                ins.then_inc(S["qs_ps"], 1)

            def inverse(t, levels, after_level):
                pe.wait_ge(S["ML_ready"], after(LEVELS * t + 1))
                pe.wait_ge(S["qkT_ready"], after(2 * t + 2))
                if not isinstance(t, int) or t:
                    pe.wait_ge(S["y2_ready"], after(2 * t - 1))
                for g in range(2):
                    for k in range(4):
                        ins = pe.transpose(PA[g][:, k * P:(k + 1) * P], ML[:, 0, 4 * g + k, :], ident[:, :])
                    ins.then_inc(S["x_ps"], 1)
                for n in range(1, levels):
                    pe.wait_ge(S["ML_ready"], after(LEVELS * t + n + 1))
                    for g in range(2):
                        pe.wait_ge(S["x_ready"], after(14 * t + 2 * n - 1 + g))
                        pe.wait_ge(S["p1_ready"], after(12 * t + max(2 * (n - 1) - 1 + g, 0)))
                        for k in range(4):
                            ins = pe.matmul(PA[g][:, k * P:(k + 1) * P], ML[:, n % 2, 4 * g + k, :],
                                            X[:, 4 * g + k, :], start=True, stop=True)
                        ins.then_inc(S["p1_ps"], 1)
                    after_level(n)
                    for g in range(2):
                        pe.wait_ge(S["p1_ready"], after(12 * t + 2 * (n - 1) + 1 + g))
                        for k in range(4):
                            h = 4 * g + k
                            ins = pe.matmul(PT[g][:, k * P:(k + 1) * P], P1[:, h, :], XT[:, h, :], start=True,
                                            stop=True)
                            if n < levels - 1:
                                ins = pe.matmul(PS[g][:, k * P:(k + 1) * P], XT[:, h, :], P1[:, h, :], start=True,
                                                stop=True)
                        ins.then_inc(S["x_ps"], 1)

            def back(t, levels):
                pe.wait_ge(S["R_ready"], after(2 * t + 2))
                pe.wait_ge(S["x_ready"], after(14 * t + 2 * levels))
                for g in range(2):
                    for k in range(4):
                        h = 4 * g + k
                        ins = pe.matmul(PA[g][:, k * P:(k + 1) * P], XT[:, h, :], R[:, h, :], start=True, stop=True)
                    ins.then_inc(S["vn_ps"], 1)
                for g in range(2):
                    pe.wait_ge(S["vn_ready"], after(2 * t + g + 1))
                    for k in range(4):
                        h = 4 * g + k
                        ins = pe.matmul(PS[g][:, k * P:(k + 1) * P], QKD[:, h, :], vn[:, h, :], start=True,
                                        stop=True)
                    ins.then_inc(S["o_ps"], 1)

            def state_update(t):
                for g in range(2):
                    pe.wait_ge(S["kt_ready"], after(t + 1))
                    for k in range(4):
                        h = 4 * g + k
                        ins = pe.matmul(PT[g][:, k * P:(k + 1) * P], kt[:, h, :], vn[:, h, :], start=True, stop=True)
                    ins.then_inc(S["su_ps"], 1)

            def out(t):
                pe.wait_ge(S["og_ready"], after(t + 1))
                pe.wait_ge(S["qs_read"], after(t + 1))
                for g in range(2):
                    if g:
                        pe.wait_ge(S["y2_ready"], after(2 * t))
                    for k in range(4):
                        ins = pe.transpose(PB[g][:, k * P:(k + 1) * P], o[:, 4 * g + k, :], ident[:, :])
                    ins.then_inc(S["oT_ps"], 1)

            def project(t, n, chunks):
                pe.wait_ge(S["oT_ready"], after(2 * t + 2))
                for c in chunks:
                    ins = pe.matmul((PA[0], PB[1])[n][:, :], oT[:, c, :], w_co[:, c, n * 512:(n + 1) * 512],
                                    start=(c == 0), stop=(c == KD - 1))
                if chunks[-1] == KD - 1:
                    ins.then_inc(S["y2_ps"], 1)

            pe.wait_ge(S["c3_loaded"], after(16 * 8))
            pe.wait_ge(S["const3_ready"], after(2))
            pe.wait_ge(S["g_ready"], after(1))
            for r, which in enumerate((0, 2)):
                pe.matmul(PA[r][:, 0:NT * GH], tc[:, which, :], spa[:, 0:NT, :].rearrange("p t h -> p (t h)"),
                          start=True, stop=True)
                pe.matmul(PA[r][:, NT * GH:(NT + 1) * GH], tcs[:, which, :], spa[:, NT, :], start=True, stop=True)\
                  .then_inc(S["gc_ps"], 1)

            def step(t, first=False):
                front(t, False)
                if not first:
                    project(t - 1, 0, range(KD))

                def between(n):
                    if n == 1:
                        state_reads(t)
                    if n == 2:
                        query_reads(t)

                inverse(t, LEVELS, between)
                back(t, LEVELS)
                state_update(t)
                if not first:
                    pe.wait_ge(S["qs_read"], after(t + 1))
                    project(t - 1, 1, range(KD))
                out(t)

            step(0, True)
            pe.wait_ge(S["w3_loaded"], after(16 * KD))
            with pe.Fori(1, NT) as t:
                step(t)
            front(NT, True)
            project(NT - 1, 0, range(KD))
            t = NT
            pe.wait_ge(S["sg_loaded"], after(16 * DB))
            pe.wait_ge(S["qkm_ready"], after(1))
            pe.wait_ge(S["MT_ready"], after(t + 1))
            pe.wait_ge(S["QKD_ready"], after(t + 1))

            def sample_reads(first):
                for k in range(4):
                    for b in range(DB):
                        ins = pe.matmul(PB[k // 2][0:SR, (k % 2) * 256:(k % 2 + 1) * 256], qkm[:, b, first + k, :],
                                        sg[:, b, 2 * k:2 * k + 2, :].rearrange("p h d -> p (h d)"), start=(b == 0),
                                        stop=(b == DB - 1))
                return ins

            sample_reads(4).then_inc(S["ks_ps"], 1)
            pe.wait_ge(S["ks_read"], after(t + 1))
            sample_reads(0).then_inc(S["qs_ps"], 1)
            pe.wait_ge(S["qs_read"], after(t + 1))
            inverse(t, SAMPLE_LEVELS, lambda n: None)
            back(t, SAMPLE_LEVELS)
            pe.wait_ge(S["eglm_ready"], after(1))
            pe.matmul(PT[0][:, 0:DB * GH], tc[:, 2, :], eglm[:, :, :].rearrange("p b h -> p (b h)"), start=True,
                      stop=True).then_inc(S["egl_ps"], 1)
            pe.wait_ge(S["egl_read"], after(1))
            pe.wait_ge(S["kt_ready"], after(t + 1))
            for h in range(GH):
                pe.wait_ge(S["vnm_ready"], after(h + 1))
                if h:
                    pe.wait_ge(S["sg_upd"], after(2 * h))
                for g in range(2):
                    pe.matmul(PT[g][:, :], kt[0:SR, h, :], vnm[:, h % 2, 4 * g:4 * g + 4, :]
                              .rearrange("p b d -> p (b d)"), start=True, stop=True).then_inc(S["sgu_ps"], 1)
            project(t - 1, 1, range(KD))
            out(t)
            for n in range(2):
                project(t, n, range(KD))

        @block.scalar
        def _(act):
            def squares(t):
                act.wait_ge(S["y2_ready"], after(2 * t + 2))
                act.wait_ge(S["fr_ready"], after(t))
                act.wait_ge(S["fs_ready"], after(t))
                act.activation(sq2[:, :], y2[:, :], ACT.Square, accum_out=fst[:, 0:1]).then_inc(S["fs_ready"], 1)

            def front(t):
                act.wait_ge(S["cin_loaded"], after(16 * (t + 1)))
                act.wait_ge(S["os_ready"], after(t))
                act.activation(sq[:, :], cin[:, 0:D], ACT.Square).then_inc(S["qk_sq"], 1)
                if not isinstance(t, int) or t >= 2:
                    squares(t - 2)
                for g in range(2):
                    act.wait_ge(S["qkT_ps"], after(2 * t + g + 1))
                    act.copy(half(qkT, g), PA[g][:, :]).then_inc(S["qkT_ready"], 1)
                act.wait_ge(S["dif_ready"], after(t + 1))
                act.activation(flat(dec), flat(dec), ACT.Exp).then_inc(S["dec_ready"], 1)

            def inverse(t, levels):
                for n in range(1, levels):
                    for g in range(2):
                        act.wait_ge(S["p1_ps"], after(12 * t + 2 * (n - 1) + g + 1))
                        act.copy(half(P1, g), PA[g][:, :]).then_inc(S["p1_ready"], 1)

            def back(t):
                for g in range(2):
                    act.wait_ge(S["vn_ps"], after(2 * t + g + 1))
                    act.copy(half(vn, g), PA[g][:, :]).then_inc(S["vn_ready"], 1)
                act.wait_ge(S["o_ready"], after(2 * t + 2))
                act.activation(sq[:, :], flat(o), ACT.Square).then_inc(S["o_sq"], 1)
                for g in range(2):
                    act.wait_ge(S["oT_ps"], after(2 * t + g + 1))
                    act.copy(half(oT, g), PB[g][:, :]).then_inc(S["oT_ready"], 1)

            act.wait_ge(S["c3_loaded"], after(16 * 8))
            act.activation(alog[:, :], alog[:, :], ACT.Exp).then_inc(S["pre_a"], 1)
            act.wait_ge(S["pre_d"], after(2))
            act.activation(spb[:, :, :], spb[:, :, :], ACT.Exp, scale=-1.0).then_inc(S["pre_a"], 1)
            act.activation(q_all[:, :, QT_BETA, :], ab_all[:, :, GH:2 * GH], ACT.Tanh, scale=0.5)\
               .then_inc(S["pre_a"], 1)
            act.wait_ge(S["pre_a"], after(3))
            act.activation(spb[:, :, :], spb[:, :, :], ACT.Ln, bias=1.0).then_inc(S["pre_a"], 1)
            act.wait_ge(S["pre_d"], after(3))
            for r, k in enumerate((QT_EGC, QT_EKT, QT_EGL)):
                ins = act.activation(q_all[:, :, k, :], (spa, spb, spc)[r][:, :, :], ACT.Exp)
            ins.then_inc(S["pre_a"], 1)
            for t in range(2):
                front(t)
                inverse(t, LEVELS)
                back(t)
            with act.Fori(2, NT) as t:
                front(t)
                inverse(t, LEVELS)
                back(t)
            front(NT)
            inverse(NT, SAMPLE_LEVELS)
            back(NT)
            squares(NT - 1)
            squares(NT)

        @block.vector
        def _(dve):
            link, fresh = link_in(dve, S["dve_link"])

            def front(t, sample):
                m = tile_masks(sample)
                dve.wait_ge(S["R_ready"], after(2 * t))
                dve.tensor_copy(cur[:, :, :].unsqueeze(1), q_all[:, ds(t, 1), :, :]).then_inc(S["cur_ready"], 1)
                dve.wait_ge(S["cur_ready"], after(t + 1))
                link(dve.tensor_tensor(begc[:, :], cur[:, QT_BETA, :], cur[:, QT_EGC, :], ALU.mult))
                dve.wait_ge(S["qk_sq"], after(t + 1))
                dve.tensor_reduce(ss8, sq[:, :].rearrange("p (h d) -> p h d", d=P), AX, ALU.add)\
                   .then_inc(S["qk_ss"], 1)
                for g in range(2):
                    dve.wait_ge(S["gcb_ps"], after(2 * t + g + 1))
                    for k in range(4):
                        h = 4 * g + k
                        ins = dve.tensor_scalar(dec[:, h, :], PS[g][:, k * P:(k + 1) * P],
                                                cur[:, QT_GC, h:h + 1], 0.0, ALU.subtract, ALU.min)
                ins.then_inc(S["dif_ready"], 1)
                dve.wait_ge(S["qk_rs"], after(t + 1))
                dve.tensor_tensor(qkn[:, :, :], cin[:, 0:D].rearrange("p (h d) -> p h d", d=P), col(rs8),
                                  ALU.mult).then_inc(S["qkn_ready"], 1)
                if not isinstance(t, int) or t >= 2:
                    final(t - 2)
                dve.wait_ge(S["dec_ready"], after(t + 1))
                link(dve.tensor_tensor(dst[:, :, :], dec[:, :, :], over(m[:, 1, :], GH), ALU.mult))
                link(dve.tensor_tensor(dec[:, :, :], dec[:, :, :], over(m[:, 0, :], GH), ALU.mult))
                dve.wait_ge(S["kk_ps"], after(t + 1))
                kk = PB[0][:, :].rearrange("p (q d) -> p q d", d=P).unsqueeze(2).to_broadcast([P, 4, 2, P])
                link(dve.tensor_tensor(MT[:, :, :].rearrange("p (q r) d -> p q r d", r=2), kk,
                                       dst[:, :, :].rearrange("p (q r) d -> p q r d", r=2), ALU.mult))
                dve.wait_ge(S["bb_ps"], after(2 * t + 2))
                for g in range(2):
                    ins = dve.tensor_tensor(half(MT, g), half(MT, g), PT[g][:, :], ALU.mult)
                ins.then_inc(S["MT_ready"], 1)
                dve.wait_ge(S["qk_ps"], after(t + 1))
                qk = PB[1][:, :].rearrange("p (q d) -> p q d", d=P).unsqueeze(2).to_broadcast([P, 4, 2, P])
                dve.tensor_tensor(QKD[:, :, :].rearrange("p (q r) d -> p q r d", r=2), qk,
                                  dec[:, :, :].rearrange("p (q r) d -> p q r d", r=2), ALU.mult)\
                   .then_inc(S["QKD_ready"], 1)

            def add_half(t, n):
                if n == 0:
                    dve.wait_ge(S["y13_loaded"], after(16 * (t + 1)))
                    dve.wait_ge(S["yo_ready"], after(t))
                    dve.wait_ge(S["fs_ready"], after(t))
                dve.wait_ge(S["y2_ps"], after(2 * t + n + 1))
                dve.tensor_tensor(y2[:, n * 512:(n + 1) * 512], y1t[:, n * 512:(n + 1) * 512],
                                  (PA[0], PB[1])[n][:, :], ALU.add).then_inc(S["y2_ready"], 1)

            def level_0(t):
                dve.wait_ge(S["ML_ready"], after(LEVELS * t + 1))
                link(dve.tensor_tensor(XT[:, :, :], over(ident[:, :], GH), ML[:, 0], ALU.subtract))
                if not isinstance(t, int) or t:
                    add_half(t - 1, 0)
                for g in range(2):
                    dve.wait_ge(S["x_ps"], after(14 * t + g + 1))
                    dve.tensor_tensor(quad(X, g), over(ident[:, :], 4), bank(PA[g]), ALU.subtract)\
                       .then_inc(S["x_ready"], 1)

            def level(t, n, last=False):
                for g in range(2):
                    dve.wait_ge(S["x_ps"], after(14 * t + 2 * n + g + 1))
                    dve.wait_ge(S["x_ready"], after(14 * t + 2 * (n - 1) + g + 1))
                    ins = dve.tensor_tensor(half(XT, g), half(XT, g), PT[g][:, :], ALU.subtract)
                    if not last:
                        ins = dve.tensor_tensor(half(X, g), half(X, g), PS[g][:, :], ALU.subtract)
                    ins.then_inc(S["x_ready"], 1)

            def key_reads(t):
                dve.wait_ge(S["ks_ps"], after(t + 1))
                for g in range(2):
                    ins = dve.tensor_tensor(quad(R, g), bank(PB[g]), col(begc[:, 4 * g:4 * g + 4]), ALU.mult)
                ins.then_inc(S["ks_read"], 1)
                dve.wait_ge(S["ks_read"], after(t + 1))
                dve.wait_ge(S["bv_ready"], after(t + 1))
                for g in range(2):
                    dve.tensor_tensor(half(R, g), half(bv, g), half(R, g), ALU.subtract).then_inc(S["R_ready"], 1)

            def query_reads(t):
                dve.wait_ge(S["qs_ps"], after(t + 1))
                for g in range(2):
                    ins = dve.tensor_tensor(quad(qs, g), bank(PB[g]), col(cur[:, QT_EGC, 4 * g:4 * g + 4]), ALU.mult)
                ins.then_inc(S["qs_read"], 1)

            def back(t):
                dve.wait_ge(S["qs_read"], after(t + 1))
                for g in range(2):
                    dve.wait_ge(S["o_ps"], after(2 * t + g + 1))
                    dve.tensor_tensor(half(o, g), half(qs, g), PS[g][:, :], ALU.add).then_inc(S["o_ready"], 1)

            def state_update(t):
                for g in range(2):
                    dve.wait_ge(S["su_ps"], after(2 * t + g + 1))
                    for k in range(4):
                        h = 4 * g + k
                        ins = dve.scalar_tensor_tensor(state[:, h, :], state[:, h, :], cur[:, QT_EGL, h:h + 1],
                                                       PT[g][:, k * P:(k + 1) * P], ALU.mult, ALU.add)
                ins.then_inc(S["st_upd"], 1)

            def out(t):
                dve.wait_ge(S["o_sq"], after(t + 1))
                dve.tensor_reduce(os8, sq[:, :].rearrange("p (h d) -> p h d", d=P), AX, ALU.add)\
                   .then_inc(S["os_ready"], 1)
                dve.wait_ge(S["or_ready"], after(t + 1))
                link(dve.tensor_tensor(o[:, :, :], o[:, :, :], col(or8), ALU.mult))
                dve.wait_ge(S["zg3_loaded"], after(16 * (t + 1)))
                dve.tensor_tensor(flat(o), flat(o), zgt[:, :], ALU.mult).then_inc(S["og_ready"], 1)
                if not isinstance(t, int) or t:
                    add_half(t - 1, 1)

            def final(t):
                dve.wait_ge(S["fr_ready"], after(t + 1))
                dve.wait_ge(S["yo_stored"], after(16 * t))
                dve.scalar_tensor_tensor(yo[:, :], y2[:, :], fst[:, 1:2], fng[:, :], ALU.mult, ALU.mult)\
                   .then_inc(S["yo_ready"], 1)

            dve.memset(nhalf[:, :], -0.5).then_inc(S["const3_ready"], 1)
            dve.memset(state[:, :, :], 0.0).then_inc(S["const3_ready"], 1)
            dve.wait_ge(S["const3_ready"], after(2))
            dve.wait_ge(S["c3_loaded"], after(16 * 8))
            dt_b = dtb[:, :].unsqueeze(1).to_broadcast([P, NT + 1, GH])
            dve.tensor_tensor(spa[:, :, :], ab_all[:, :, 0:GH], dt_b, ALU.add).then_inc(S["pre_d"], 1)
            dve.wait_ge(S["pre_d"], after(1))
            dve.scalar_tensor_tensor(spb[:, :, :], spa[:, :, :], -1.0, spa[:, :, :], ALU.mult, ALU.max).then_inc(S["pre_d"], 1)
            dve.wait_ge(S["pre_a"], after(4))
            link(dve.scalar_tensor_tensor(spa[:, :, :], spa[:, :, :], 0.0, spb[:, :, :], ALU.max, ALU.add))
            link(dve.tensor_scalar(alog[:, :], alog[:, :], -1.0, None, ALU.mult))
            dve.tensor_tensor(spa[:, :, :], spa[:, :, :], alog[:, :].unsqueeze(1).to_broadcast([P, NT + 1, GH]),
                              ALU.mult).then_inc(S["g_ready"], 1)
            dve.wait_ge(S["g_ready"], after(1))
            dve.tensor_copy(q_all[:, :, QT_G, :], spa[:, :, :])
            link(dve.tensor_scalar(q_all[:, :, QT_BETA, :], q_all[:, :, QT_BETA, :], 0.5, 0.5, ALU.mult, ALU.add))
            dve.wait_ge(S["gc_ps"], after(2))
            gc = PA[0][:, 0:(NT + 1) * GH].rearrange("p (t h) -> p t h", h=GH)
            gl = PA[1][:, 0:(NT + 1) * GH].rearrange("p (t h) -> p t h", h=GH)
            dve.tensor_copy(q_all[:, :, QT_GC, :], gc)
            link(dve.tensor_copy(spa[:, :, :], gc))
            link(dve.tensor_tensor(spb[:, :, :], gl, spa[:, :, :], ALU.subtract))
            dve.tensor_copy(spc[:, :, :], gl).then_inc(S["pre_d"], 1)
            dve.wait_ge(S["pre_a"], after(5))

            def step(t):
                fresh()
                front(t, False)
                level_0(t)
                for n in range(1, LEVELS):
                    if n == 2:
                        key_reads(t)
                    if n == 3:
                        query_reads(t)
                    level(t, n, n == LEVELS - 1)
                back(t)
                state_update(t)
                out(t)

            for t in range(2):
                step(t)
            with dve.Fori(2, NT) as t:
                step(t)
            t = NT
            fresh()
            front(t, True)
            dve.wait_ge(S["qkT_ready"], after(2 * t + 2))
            dve.wait_ge(S["qkm_zero"], after(1))
            for b in range(DB):
                ins = dve.tensor_copy(qkm[:, b, :, b * DT:(b + 1) * DT], qkT[:, :, b * DT:(b + 1) * DT])
            ins.then_inc(S["qkm_ready"], 1)
            dve.tensor_tensor(eglm[:, :, :], cur[:, QT_EGL:QT_EGL + 1, :].to_broadcast([P, DB, GH]),
                              bsel[:, DB:2 * DB].unsqueeze(2).to_broadcast([P, DB, GH]), ALU.mult)\
               .then_inc(S["eglm_ready"], 1)
            key_reads(t)
            query_reads(t)
            level_0(t)
            level(t, 1, True)
            back(t)
            dve.wait_ge(S["egl_ps"], after(1))
            dve.tensor_copy(eglb[:, :, :].rearrange("p b h -> p (b h)"), PT[0][:, 0:DB * GH])\
               .then_inc(S["egl_read"], 1)
            dve.wait_ge(S["egl_read"], after(1))
            dve.wait_ge(S["qs_ps"], after(t + 1))
            sgf = sg[:, :, :, :].rearrange("p b h d -> p (b h) d")
            link(dve.tensor_tensor(sgf, sgf, eglb[:, :, :].rearrange("p b h -> p (b h)").unsqueeze(2)
                                   .to_broadcast([P, DB * GH, P]), ALU.mult))
            for h in range(GH):
                if h >= 2:
                    dve.wait_ge(S["sgu_ps"], after(2 * (h - 1)))
                dve.tensor_tensor(vnm[:, h % 2], vn[0:SR, h:h + 1, :].to_broadcast([SR, DB, P]),
                                  bsel[0:SR, 0:DB].unsqueeze(2).to_broadcast([SR, DB, P]), ALU.mult)\
                   .then_inc(S["vnm_ready"], 1)
                for g in range(2):
                    dve.wait_ge(S["sgu_ps"], after(2 * h + g + 1))
                    dve.tensor_tensor(sg[:, 4 * g:4 * g + 4, h, :], sg[:, 4 * g:4 * g + 4, h, :], bank(PT[g]), ALU.add)\
                       .then_inc(S["sg_upd"], 1)
            out(t)
            final(t - 1)
            for n in range(2):
                add_half(t, n)
            final(t)

        @block.gpsimd
        def _(pool):
            link, fresh = link_in(pool, S["pool_link"])

            def tile(t, sample):
                m = tile_masks(sample)
                fresh()
                if sample:
                    pool.memset(qkm[:, :, :, :], 0.0).then_inc(S["qkm_zero"], 1)
                pool.wait_ge(S["qk_ss"], after(t + 1))
                link()
                link(pool.tensor_scalar(rs8, ss8, EPS, None, ALU.add))
                link(pool.tensor_tensor(rs8, rs8, nhalf[:, :], ALU.pow))
                pool.tensor_tensor(rs8, rs8, qks[:, :], ALU.mult).then_inc(S["qk_rs"], 1)
                pool.wait_ge(S["cur_ready"], after(t + 1))
                pool.tensor_tensor(bv[:, :, :], cin[:, D:2 * D].rearrange("p (h d) -> p h d", d=P),
                                   col(cur[:, QT_BETA, :]), ALU.mult).then_inc(S["bv_ready"], 1)
                if not isinstance(t, int) or t >= 2:
                    final(t - 2)
                for n in range(SAMPLE_LEVELS if sample else LEVELS):
                    if n == 0:
                        pool.wait_ge(S["MT_ready"], after(t + 1))
                        pool.wait_ge(S["x_ready"], after(14 * t))
                    elif n >= 2:
                        pool.wait_ge(S["x_ready"], after(14 * t + 2 * (n - 1)))
                    pool.tensor_tensor(ML[:, n % 2], MT[:, :, :], over(m[:, 3 + n, :], GH), ALU.mult)\
                        .then_inc(S["ML_ready"], 1)
                    if n == 0:
                        pool.wait_ge(S["qkn_ready"], after(t + 1))
                        pool.wait_ge(S["su_ps"], after(2 * t))
                        for g in range(2):
                            ins = pool.tensor_tensor(
                                quad(kt, g).rearrange("p (q r) d -> p q r d", r=2),
                                qkn[:, 4 + 2 * g:6 + 2 * g, :].unsqueeze(2).to_broadcast([P, 2, 2, P]),
                                cur[:, QT_EKT, 4 * g:4 * g + 4].rearrange("p (q r) -> p q r", r=2).unsqueeze(3)
                                .to_broadcast([P, 2, 2, P]), ALU.mult)
                        ins.then_inc(S["kt_ready"], 1)
                pool.wait_ge(S["os_ready"], after(t + 1))
                link()
                link(pool.tensor_scalar(or8, os8, 1.0 / P, EPS, ALU.mult, ALU.add))
                pool.tensor_tensor(or8, or8, nhalf[:, :], ALU.pow).then_inc(S["or_ready"], 1)

            def final(t):
                pool.wait_ge(S["fs_ready"], after(t + 1))
                link()
                link(pool.tensor_scalar(fst[:, 1:2], fst[:, 0:1], 1.0 / D, EPS, ALU.mult, ALU.add))
                pool.tensor_tensor(fst[:, 1:2], fst[:, 1:2], nhalf[:, 0:1], ALU.pow).then_inc(S["fr_ready"], 1)

            pool.wait_ge(S["const3_ready"], after(1))
            pool.wait_ge(S["c3_loaded"], after(16 * 8))
            for t in range(2):
                tile(t, False)
            with pool.Fori(2, NT) as t:
                tile(t, False)
            tile(NT, True)
            final(NT - 1)
            final(NT)


def hybrid_step(nc, io):
    ctx = ExitStack()
    with ctx:
        most = max(len(n.split()) for n in (PROJECT_SIGNALS, LAYER0_SIGNALS, SAMPLES_SIGNALS, CONV_SIGNALS, DELTA_SIGNALS))
        pool = [ctx.enter_context(nc.semaphore(f"signal{k}")) for k in range(most)]
        links = {n: ctx.enter_context(nc.semaphore(n)) for n in LINKS.split()}
        ab_all = ctx.enter_context(nc.sbuf_tensor("ab_all", [P, NT + 1, 16], FP))

        def signals(names):
            given = dict(zip(names.split(), pool))
            with nc.Block() as block:
                @block.sync
                def _(sp):
                    for s in given.values():
                        sp.sem_clear(s)
                        sp.sem_inc(s, START)
            return given | links

        with nc.sbuf_tensor("w_b", [P, KD, ABW - AW], FP) as w_b:
            layer0_project(nc, io, signals(PROJECT_SIGNALS), w_b)
            layer0_mixers(nc, io, signals(LAYER0_SIGNALS), w_b)
        layer0_samples(nc, io, signals(SAMPLES_SIGNALS))
        layer0_out_and_conv(nc, io, signals(CONV_SIGNALS), ab_all)
        layer1_delta(nc, io, signals(DELTA_SIGNALS), ab_all)


def kernel(**inputs):
    import concourse.bacc as _bacc
    from concourse.bass_utils import run_bass_kernel_spmd as _run

    nc = _bacc.Bacc("TRN2", target_bir_lowering=False, num_devices=1)
    inp = {k: np.ascontiguousarray(v) for k, v in inputs.items()}
    f = np.float32
    pad = np.zeros((ROWS - SEQ - SR, D), f)
    arrays = {
        "x_all": np.concatenate([inp["x_prompt"][0], inp["x_sample"].reshape(SR, D), pad]),
        "w_in_ab": inp["w_in_ab"][0], "norm_w": inp["norm_w"], "gn_ret": inp["gn_ret"],
        "w_out_ab": inp["w_out_ab"][0], "w_in_c": inp["w_in_c"][0], "w_out_c": inp["w_out_c"][0],
        "conv_w": inp["conv_w"][0], "gdn_norm": inp["gdn_norm"], "final_norm": inp["final_norm"][None],
        "state_conv": inp["state_conv"][0].reshape(DB * 3, CC),
        "a_log": inp["a_log"], "dt_bias": inp["dt_bias"],
        "state_ret": inp["state_ret"][0], "state_gdn": inp["state_gdn"][0],
        "cache_k": inp["cache_k"][0].reshape(-1, PAGE, 128), "cache_v": inp["cache_v"][0].reshape(-1, PAGE, 128),
        "cache_kidx": inp["cache_kidx"][0], "page_table": inp["page_table"].reshape(1, -1).astype(np.int32),
    }
    arrays.update(constants())
    p = np.arange(P)
    arrays["tri"], arrays["tri_s"] = tri_constants(P), tri_constants(DT)
    arrays["qk_scale"] = np.tile(np.where(np.arange(GH) < 4, P ** -0.5, 1.0), (P, 1)).astype(f)
    batch = p[:, None] // DT == np.arange(DB)[None]
    arrays["bsel"] = np.concatenate([batch, batch & (p[:, None] % DT == 0)], 1).astype(f)
    lg = np.log(1.0 - 2.0 ** (-5.0 - np.arange(RH)))
    same = p[:, None] // DT == p[None] // DT
    dif = p[None, :] - p[:, None]
    rm = np.where((same & (dif >= 0))[:, None, :], np.exp(dif[:, None, :] * lg[None, :, None]), 0.0) * HD ** -0.5
    arrays["rmask_s"] = rm[:, [0, 2, 1, 3]].reshape(P, RH * P).astype(f)
    head = 2 * np.arange(2)[None] + (p[:, None] >= HD)
    tok = np.arange(SR)
    own = tok[None] // DT == np.arange(DB)[:, None]
    qd = np.exp((tok % DT + 1.0)[None, None] * lg[head][:, :, None])
    arrays["qdec_s"] = (qd[:, :, None] * own[None, None]).reshape(P, -1).astype(f)
    arrays["kdec_s"] = (np.exp((DT - 1.0 - p % DT)[:, None] * lg[None]) * HD ** -0.5).astype(f)
    arrays["cdec_s"] = np.tile(np.exp(DT * lg), (P, 1)).astype(f)
    pair = np.arange(HB)[None, :, None] + HB * (p[:, None, None] >= HD)
    arrays["hm"] = (tok[None, None] // DT == pair).reshape(P, -1).astype(f)
    arrays["rep"] = (p[:, None] % SR == tok[None]).astype(f)
    arrays["rep4"] = ((p[:, None] == p[None] % SR)).astype(f)
    arrays["tmask"] = np.where(np.arange(DT)[None] <= tok[:, None] % DT, 0.0, -BIG).astype(f)
    arrays["dsel"] = ((p[:, None] % SR) // DT == np.arange(DB)[None]).astype(f)
    io = {}
    for name, a in arrays.items():
        io[name] = nc.dram_tensor(f"in_{name}", a.shape, mybir.dt.from_np(a.dtype), kind="ExternalInput").ap()
    for name, shape in OUTS.items():
        io[name] = nc.dram_tensor(f"out_{name}", shape, FP, kind="ExternalOutput").ap()
    hybrid_step(nc, io)
    r = _run(nc, [{f"in_{k}": v for k, v in arrays.items()}], core_ids=[0])
    o = {n: r.results[0][f"out_{n}"] for n in OUTS}
    k, v, ik = o["k_all"], o["v_all"], o["ik_all"]
    return (o["y_all"][None, :SEQ], o["y_all"][SEQ:SEQ + SR].reshape(DB, DT, D),
            k[:SEQ].reshape(1, 1, SEQ, 2, HD), v[:SEQ].reshape(1, 1, SEQ, 2, HD), ik[:SEQ].reshape(1, 1, SEQ, HD),
            k[SEQ:SEQ + SR].reshape(1, DB, DT, 2, HD), v[SEQ:SEQ + SR].reshape(1, DB, DT, 2, HD),
            ik[SEQ:SEQ + SR].reshape(1, DB, DT, HD),
            o["ret_prompt"][None, None], o["ret_sample"][None], o["gdn_prompt"][None, None], o["gdn_sample"][None],
            o["conv_prompt"][None, None], o["conv_sample"].reshape(1, DB, 3, CC))
```
